# Optimizing a Trainium2 kernel written in Bass

```python
import jax
import jax.numpy as jnp
from jax import lax
import numpy as np
import math
import jax, jax.numpy as jnp

D_MODEL = 1024
BATCH = 1
SEQ = 1024
DEPTH = 1

GRID_W = 64
CTX_LEN = 256
D_MIX = D_MODEL
D_MLSTM = D_MIX // 2
D_CONV = D_MIX - D_MLSTM
M_HEADS = 4
V_DIM = D_MLSTM // M_HEADS
QK_DIM = V_DIM // 2
D_QK = M_HEADS * QK_DIM
N_GATES = 4 * M_HEADS
CHUNK = 128
CONV_WIDTH = 31
N_EXPERTS = 64
TOP_K = 8
D_EXPERT = D_MODEL // 4
D_SHARED = D_EXPERT
ROUTE_SCALE = 2.5
EXPERT_BLOCK = 128
EPS = 1e-6
IN_SPLITS = (D_QK, 2 * D_QK, 2 * D_QK + D_MLSTM, 2 * D_QK + 2 * D_MLSTM,
             2 * D_QK + 2 * D_MLSTM + N_GATES, 2 * D_QK + 2 * D_MLSTM + N_GATES + D_CONV)
D_IN = 2 * D_QK + 2 * D_MLSTM + N_GATES + 2 * D_CONV


def _rms_norm(x, g):
    xf = x.astype(jnp.float32)
    y = xf * lax.rsqrt(jnp.mean(xf * xf, axis=-1, keepdims=True) + EPS)
    return (y * g.astype(jnp.float32)).astype(x.dtype)

def _layer_norm(x, g, b):
    xf = x.astype(jnp.float32)
    mu = jnp.mean(xf, axis=-1, keepdims=True)
    xc = xf - mu
    y = xc * lax.rsqrt(jnp.mean(xc * xc, axis=-1, keepdims=True) + EPS)
    return (y * g.astype(jnp.float32) + b.astype(jnp.float32)).astype(x.dtype)

def _modulate(h, shift, scale):
    return h * (1.0 + scale) + shift

def _heads(t, n):
    B, T, _ = t.shape
    return t.reshape(B, T, n, -1).transpose(0, 2, 1, 3).astype(jnp.float32)

def _mlstm_chunk_states(k, v, log_i, log_f, state0):
    B, H, T, dk = k.shape
    dv = v.shape[-1]
    nc = T // CHUNK
    kc = k.reshape(B, H, nc, CHUNK, dk)
    vc = v.reshape(B, H, nc, CHUNK, dv)
    li = log_i.reshape(B, H, nc, CHUNK)
    b = jnp.cumsum(log_f.reshape(B, H, nc, CHUNK), axis=-1)
    b_tot = b[..., -1]
    g = b_tot[..., None] - b + li
    m_loc = jnp.max(g, axis=-1)
    w = jnp.exp(g - m_loc[..., None])
    C_loc = jnp.einsum('bhcs,bhcsv,bhcsk->bhcvk', w, vc, kc)
    n_loc = jnp.einsum('bhcs,bhcsk->bhck', w, kc)

    def step(state, xs):
        C, n, m = state
        bt, ml, Cl, nl = xs
        m_new = jnp.maximum(bt + m, ml)
        a = jnp.exp(bt + m - m_new)
        e = jnp.exp(ml - m_new)
        C_new = a[..., None, None] * C + e[..., None, None] * Cl
        n_new = a[..., None] * n + e[..., None] * nl
        return (C_new, n_new, m_new), (C, n, m)

    xs = (jnp.moveaxis(b_tot, 2, 0), jnp.moveaxis(m_loc, 2, 0),
          jnp.moveaxis(C_loc, 2, 0), jnp.moveaxis(n_loc, 2, 0))
    final, prev = lax.scan(step, state0, xs)
    prev = (jnp.moveaxis(prev[0], 0, 2), jnp.moveaxis(prev[1], 0, 2), jnp.moveaxis(prev[2], 0, 2))
    return prev, final

def _mlstm_chunk_outputs(q, k, v, log_i, log_f, prev):
    C_prev, n_prev, m_prev = prev
    B, H, T, dk = q.shape
    dv = v.shape[-1]
    nc = T // CHUNK
    qc = q.reshape(B, H, nc, CHUNK, dk)
    kc = k.reshape(B, H, nc, CHUNK, dk)
    vc = v.reshape(B, H, nc, CHUNK, dv)
    li = log_i.reshape(B, H, nc, CHUNK)
    b = jnp.cumsum(log_f.reshape(B, H, nc, CHUNK), axis=-1)
    lower = jnp.tril(jnp.ones((CHUNK, CHUNK), dtype=bool))
    log_d = jnp.where(lower, b[..., :, None] - b[..., None, :] + li[..., None, :], -jnp.inf)
    a = b + m_prev[..., None]
    m_t = jnp.maximum(a, jnp.max(log_d, axis=-1))
    s = jnp.einsum('bhctk,bhcsk->bhcts', qc, kc) * jnp.exp(log_d - m_t[..., None])
    e_int = jnp.exp(a - m_t)
    num = (jnp.einsum('bhcts,bhcsv->bhctv', s, vc)
           + e_int[..., None] * jnp.einsum('bhcvk,bhctk->bhctv', C_prev, qc))
    den = jnp.sum(s, axis=-1) + e_int * jnp.einsum('bhck,bhctk->bhct', n_prev, qc)
    h = num / jnp.maximum(jnp.abs(den), jnp.exp(-m_t))[..., None]
    return h.reshape(B, H, T, dv)

def _mlstm_direction(q, k, v, log_i, log_f, state0, reverse, want_out):
    if reverse:
        q, k, v = jnp.flip(q, 2), jnp.flip(k, 2), jnp.flip(v, 2)
        log_i, log_f = jnp.flip(log_i, 2), jnp.flip(log_f, 2)
    prev, final = _mlstm_chunk_states(k, v, log_i, log_f, state0)
    h = None
    if want_out:
        h = _mlstm_chunk_outputs(q, k, v, log_i, log_f, prev)
        if reverse:
            h = jnp.flip(h, 2)
    return h, final

def _mlstm_bidir(q, k, v, gates, states0, want_out):
    h_f, s_f = _mlstm_direction(q, k, v, gates[:, 0], jax.nn.log_sigmoid(gates[:, 1]),
                                states0[0], False, want_out)
    h_b, s_b = _mlstm_direction(q, k, v, gates[:, 2], jax.nn.log_sigmoid(gates[:, 3]),
                                states0[1], True, want_out)
    h = h_f + h_b if want_out else None
    return h, (s_f, s_b)

def _project(h, w_in, b_in, b_gate):
    B, T, _ = h.shape
    z = h @ w_in + b_in
    q, k, v, o, gt, ga, gb = jnp.split(z, IN_SPLITS, axis=-1)
    q = _heads(q, M_HEADS)
    k = _heads(k, M_HEADS) * (QK_DIM ** -0.5)
    v = _heads(v, M_HEADS)
    gates = (gt.reshape(B, T, 4, M_HEADS).transpose(0, 2, 3, 1).astype(jnp.float32)
             + b_gate.astype(jnp.float32)[None, :, :, None])
    u = ga * jax.nn.sigmoid(gb)
    return (q, k, v, gates), o, u

def _mlstm_group_out(h, o, norm_g):
    B, H, T, dv = h.shape
    hn = h * lax.rsqrt(jnp.mean(h * h, axis=-1, keepdims=True) + EPS) * norm_g.astype(jnp.float32)[:, None, :]
    return hn.transpose(0, 2, 1, 3).reshape(B, T, H * dv).astype(o.dtype) * jax.nn.sigmoid(o)

def _conv_group_out(u, conv_w, conv_b, ln_g, ln_b, rows):
    B, T, C = u.shape
    lhs = u.reshape(B * rows, T // rows, C)
    y = lax.conv_general_dilated(lhs, conv_w.astype(u.dtype)[:, None, :], (1,), 'SAME',
                                 dimension_numbers=('NWC', 'WIO', 'NWC'), feature_group_count=C)
    y = y.reshape(B, T, C) + conv_b
    return jax.nn.silu(_layer_norm(y, ln_g, ln_b))

def _token_mixer(hx, hc, w_in, b_in, b_gate, norm_g, conv_w, conv_b, ln_g, ln_b, w_out, b_out, ctx_out):
    B = hx.shape[0]
    rows = hx.shape[1] // GRID_W
    mx_in, ox, ux = _project(hx, w_in, b_in, b_gate)
    mc_in, oc, uc = _project(hc, w_in, b_in, b_gate)
    zero = (jnp.zeros((B, M_HEADS, V_DIM, QK_DIM), jnp.float32),
            jnp.zeros((B, M_HEADS, QK_DIM), jnp.float32),
            jnp.zeros((B, M_HEADS), jnp.float32))
    hc_m, ctx_states = _mlstm_bidir(*mc_in, (zero, zero), ctx_out)
    hx_m, _ = _mlstm_bidir(*mx_in, ctx_states, True)
    yx = jnp.concatenate([_mlstm_group_out(hx_m, ox, norm_g),
                          _conv_group_out(ux, conv_w, conv_b, ln_g, ln_b, rows)], axis=-1) @ w_out + b_out
    yc = None
    if ctx_out:
        yc = jnp.concatenate([_mlstm_group_out(hc_m, oc, norm_g),
                              _conv_group_out(uc, conv_w, conv_b, ln_g, ln_b, 1)], axis=-1) @ w_out + b_out
    return yx, yc

def _moe_ffn(h, w_router, b_router, we_gate, we_up, we_down, ws_gate, ws_up, ws_down):
    B, T, D = h.shape
    hf = h.reshape(-1, D)
    nt = hf.shape[0]
    s = jax.nn.sigmoid((hf @ w_router).astype(jnp.float32))
    _, idx = lax.top_k(s + b_router.astype(jnp.float32), TOP_K)
    s_sel = jnp.take_along_axis(s, idx, axis=-1)
    wts = s_sel / jnp.sum(s_sel, axis=-1, keepdims=True) * ROUTE_SCALE
    n_assign = nt * TOP_K
    e_flat = idx.reshape(-1)
    tok_flat = jnp.repeat(jnp.arange(nt, dtype=jnp.int32), TOP_K)
    order = jnp.argsort(e_flat)
    e_s, tok_s, w_s = e_flat[order], tok_flat[order], wts.reshape(-1)[order]
    counts = jnp.bincount(e_flat, length=N_EXPERTS)
    starts = jnp.cumsum(counts) - counts
    padded = (counts + EXPERT_BLOCK - 1) // EXPERT_BLOCK * EXPERT_BLOCK
    pend = jnp.cumsum(padded)
    pstarts = pend - padded
    dest = pstarts[e_s] + (jnp.arange(n_assign, dtype=jnp.int32) - starts[e_s])
    n_rows = -(-(n_assign + N_EXPERTS * (EXPERT_BLOCK - 1)) // EXPERT_BLOCK) * EXPERT_BLOCK
    n_blocks = n_rows // EXPERT_BLOCK
    row_tok = jnp.full((n_rows,), nt, jnp.int32).at[dest].set(tok_s)
    row_w = jnp.zeros((n_rows,), jnp.float32).at[dest].set(w_s)
    block_e = jnp.minimum(jnp.searchsorted(pend, jnp.arange(n_blocks) * EXPERT_BLOCK, side='right'),
                          N_EXPERTS - 1)
    hpad = jnp.concatenate([hf, jnp.zeros((1, D), hf.dtype)], axis=0)

    def body(acc, xs):
        rows, rw, e = xs
        xb = hpad[rows]
        y = (jax.nn.silu(xb @ we_gate[e]) * (xb @ we_up[e])) @ we_down[e]
        return acc.at[rows].add(y * rw[:, None].astype(y.dtype)), None

    acc, _ = lax.scan(body, jnp.zeros((nt + 1, D), hf.dtype),
                      (row_tok.reshape(n_blocks, EXPERT_BLOCK), row_w.reshape(n_blocks, EXPERT_BLOCK), block_e))
    shared = (jax.nn.silu(hf @ ws_gate) * (hf @ ws_up)) @ ws_down
    return (acc[:nt] + shared).reshape(B, T, D)

def first_inputs(seed: int = 0) -> dict:
    key = jax.random.key(seed)
    ks = jax.random.split(key, 32)

    def nrm(k, shape, scale):
        return jax.random.normal(k, shape, jnp.float32) * scale

    D = D_MODEL
    b_gate = jnp.stack([nrm(ks[12], (DEPTH, M_HEADS), 0.1),
                        3.0 + 3.0 * jax.random.uniform(ks[13], (DEPTH, M_HEADS), jnp.float32),
                        nrm(ks[14], (DEPTH, M_HEADS), 0.1),
                        3.0 + 3.0 * jax.random.uniform(ks[15], (DEPTH, M_HEADS), jnp.float32)], axis=1)
    return {
        "x": nrm(ks[0], (BATCH, SEQ, D), 1.0),
        "c": nrm(ks[1], (BATCH, D), 1.0),
        "ctx": nrm(ks[2], (BATCH, CTX_LEN, D), 1.0),
        "c_ctx": nrm(ks[3], (D,), 1.0),
        "w_ada": nrm(ks[4], (DEPTH, D, 6 * D), 0.5 * D ** -0.5),
        "b_ada": nrm(ks[5], (DEPTH, 6 * D), 0.02),
        "g_pre_mix": 1.0 + nrm(ks[6], (DEPTH, D), 0.1),
        "g_post_mix": 1.0 + nrm(ks[7], (DEPTH, D), 0.1),
        "g_pre_ffn": 1.0 + nrm(ks[8], (DEPTH, D), 0.1),
        "g_post_ffn": 1.0 + nrm(ks[9], (DEPTH, D), 0.1),
        "w_in": nrm(ks[10], (DEPTH, D, D_IN), D ** -0.5),
        "b_in": nrm(ks[11], (DEPTH, D_IN), 0.02),
        "b_gate": b_gate,
        "mlstm_norm_g": 1.0 + nrm(ks[16], (DEPTH, M_HEADS, V_DIM), 0.1),
        "conv_w": nrm(ks[17], (DEPTH, CONV_WIDTH, D_CONV), CONV_WIDTH ** -0.5),
        "conv_b": nrm(ks[18], (DEPTH, D_CONV), 0.02),
        "conv_ln_g": 1.0 + nrm(ks[19], (DEPTH, D_CONV), 0.1),
        "conv_ln_b": nrm(ks[20], (DEPTH, D_CONV), 0.02),
        "w_out": nrm(ks[21], (DEPTH, D_MIX, D), D_MIX ** -0.5),
        "b_out": nrm(ks[22], (DEPTH, D), 0.02),
        "w_router": nrm(ks[23], (DEPTH, D, N_EXPERTS), D ** -0.5),
        "b_router": nrm(ks[24], (DEPTH, N_EXPERTS), 0.01),
        "we_gate": nrm(ks[25], (DEPTH, N_EXPERTS, D, D_EXPERT), D ** -0.5),
        "we_up": nrm(ks[26], (DEPTH, N_EXPERTS, D, D_EXPERT), D ** -0.5),
        "we_down": nrm(ks[27], (DEPTH, N_EXPERTS, D_EXPERT, D), D_EXPERT ** -0.5),
        "ws_gate": nrm(ks[28], (DEPTH, D, D_SHARED), D ** -0.5),
        "ws_up": nrm(ks[29], (DEPTH, D, D_SHARED), D ** -0.5),
        "ws_down": nrm(ks[30], (DEPTH, D_SHARED, D), D_SHARED ** -0.5),
    }

def first_block(x, c, ctx, c_ctx, w_ada, b_ada, g_pre_mix, g_post_mix, g_pre_ffn, g_post_ffn,
              w_in, b_in, b_gate, mlstm_norm_g, conv_w, conv_b, conv_ln_g, conv_ln_b, w_out, b_out,
              w_router, b_router, we_gate, we_up, we_down, ws_gate, ws_up, ws_down):
    for l in range(DEPTH):
        ctx_out = l < DEPTH - 1
        mx = [t[:, None, :] for t in jnp.split(jax.nn.silu(c) @ w_ada[l] + b_ada[l], 6, axis=-1)]
        mc = jnp.split(jax.nn.silu(c_ctx) @ w_ada[l] + b_ada[l], 6, axis=-1)
        hx = _modulate(_rms_norm(x, g_pre_mix[l]), mx[0], mx[1])
        hc = _modulate(_rms_norm(ctx, g_pre_mix[l]), mc[0], mc[1])
        yx, yc = _token_mixer(hx, hc, w_in[l], b_in[l], b_gate[l], mlstm_norm_g[l], conv_w[l], conv_b[l],
                              conv_ln_g[l], conv_ln_b[l], w_out[l], b_out[l], ctx_out)
        x = x + mx[2] * _rms_norm(yx, g_post_mix[l])
        hx = _modulate(_rms_norm(x, g_pre_ffn[l]), mx[3], mx[4])
        x = x + mx[5] * _rms_norm(_moe_ffn(hx, w_router[l], b_router[l], we_gate[l], we_up[l], we_down[l],
                                           ws_gate[l], ws_up[l], ws_down[l]), g_post_ffn[l])
        if ctx_out:
            ctx = ctx + mc[2] * _rms_norm(yc, g_post_mix[l])
            hc = _modulate(_rms_norm(ctx, g_pre_ffn[l]), mc[3], mc[4])
            ctx = ctx + mc[5] * _rms_norm(_moe_ffn(hc, w_router[l], b_router[l], we_gate[l], we_up[l], we_down[l],
                                                 ws_gate[l], ws_up[l], ws_down[l]), g_post_ffn[l])
    return x


CHUNK_2 = 64
LEFT_CHUNKS = 8
BAND = LEFT_CHUNKS + 1
ATTN_HEADS = 8
HEAD_DIM = 64
D_ATTN = ATTN_HEADS * HEAD_DIM
MAX_REL = 256
REL_FUTURE = CHUNK_2 - 1
N_REL = REL_FUTURE + MAX_REL + 1
D_SSM = D_MODEL // 2
SSM_GROUP = 16
SSM_GROUPS = D_SSM // SSM_GROUP
SSM_STATE = 64
STEP_MIN = 0.001
STEP_MAX = 0.1
N_BRANCH = 2
D_IN_2 = 3 * D_ATTN + D_SSM + N_BRANCH * D_MODEL
N_GROUPS = 4
EXPERTS_PER_GROUP = 4
N_EXPERTS_2 = N_GROUPS * EXPERTS_PER_GROUP
TOP_K_2 = 2
D_EXPERT_2 = D_MODEL // 4
NEG_INF = -1e30


def rms_norm(x, gain):
    xf = x.astype(jnp.float32)
    y = xf * lax.rsqrt(jnp.mean(xf * xf, axis=-1, keepdims=True) + EPS)
    return (y * gain.astype(jnp.float32)).astype(x.dtype)

def chunked_relpos_attention(q, k, v, q_gain, k_gain, rel_bias):
    b, l = q.shape[0], q.shape[1]
    nc = l // CHUNK_2
    q = rms_norm(q, q_gain)
    k = rms_norm(k, k_gain)
    pad = ((0, 0), (LEFT_CHUNKS * CHUNK_2, 0), (0, 0), (0, 0))
    kp = jnp.pad(k, pad).reshape(b, nc + LEFT_CHUNKS, CHUNK_2, ATTN_HEADS, HEAD_DIM)
    vp = jnp.pad(v, pad).reshape(b, nc + LEFT_CHUNKS, CHUNK_2, ATTN_HEADS, HEAD_DIM)
    band = jnp.arange(nc)[:, None] + jnp.arange(BAND)[None, :]
    kb = kp[:, band].reshape(b, nc, BAND * CHUNK_2, ATTN_HEADS, HEAD_DIM)
    vb = vp[:, band].reshape(b, nc, BAND * CHUNK_2, ATTN_HEADS, HEAD_DIM)
    qc = q.reshape(b, nc, CHUNK_2, ATTN_HEADS, HEAD_DIM)
    s = jnp.einsum('bnqhd,bnkhd->bhnqk', qc, kb).astype(jnp.float32) * (HEAD_DIM ** -0.5)
    q_off = jnp.arange(CHUNK_2)[:, None] + LEFT_CHUNKS * CHUNK_2
    k_off = jnp.arange(BAND * CHUNK_2)[None, :]
    rel_idx = jnp.clip(q_off - k_off, -REL_FUTURE, MAX_REL) + REL_FUTURE
    bias = rel_bias.astype(jnp.float32)[:, rel_idx]
    key_pos = (jnp.arange(nc)[:, None] - LEFT_CHUNKS) * CHUNK_2 + k_off
    valid = key_pos >= 0
    s = jnp.where(valid[None, None, :, None, :], s + bias[None, :, None], NEG_INF)
    p = jax.nn.softmax(s, axis=-1).astype(v.dtype)
    o = jnp.einsum('bhnqk,bnkhd->bnqhd', p, vb)
    return o.reshape(b, l, D_ATTN)

def _complex_linear_combine(e1, e2):
    a1r, a1i, b1r, b1i = e1
    a2r, a2i, b2r, b2i = e2
    ar = a2r * a1r - a2i * a1i
    ai = a2r * a1i + a2i * a1r
    br = a2r * b1r - a2i * b1i + b2r
    bi = a2r * b1i + a2i * b1r + b2i
    return (ar, ai, br, bi)

def s5_ssm_glu(u, lambda_re, lambda_im, log_step, b_re, b_im, c_re, c_im, d_skip, w_glu, b_glu):
    bsz, l = u.shape[0], u.shape[1]
    uf = u.astype(jnp.float32).reshape(bsz, l, SSM_GROUPS, SSM_GROUP)
    lre = lambda_re.astype(jnp.float32)
    lim = lambda_im.astype(jnp.float32)
    step = jnp.exp(log_step.astype(jnp.float32))[:, None]
    mag = jnp.exp(lre * step)
    ang = lim * step
    a_re = mag * jnp.cos(ang)
    a_im = mag * jnp.sin(ang)
    num_re = a_re - 1.0
    num_im = a_im
    den = lre * lre + lim * lim
    f_re = (num_re * lre + num_im * lim) / den
    f_im = (num_im * lre - num_re * lim) / den
    br = b_re.astype(jnp.float32)
    bi = b_im.astype(jnp.float32)
    bb_re = f_re[..., None] * br - f_im[..., None] * bi
    bb_im = f_re[..., None] * bi + f_im[..., None] * br
    bu_re = jnp.einsum('blgc,gpc->blgp', uf, bb_re)
    bu_im = jnp.einsum('blgc,gpc->blgp', uf, bb_im)
    a_re_t = jnp.broadcast_to(a_re[None, None], (1, l, SSM_GROUPS, SSM_STATE))
    a_im_t = jnp.broadcast_to(a_im[None, None], (1, l, SSM_GROUPS, SSM_STATE))
    _, _, s_re, s_im = lax.associative_scan(
        _complex_linear_combine, (a_re_t, a_im_t, bu_re, bu_im), axis=1)
    y = (jnp.einsum('blgp,gcp->blgc', s_re, c_re.astype(jnp.float32))
         - jnp.einsum('blgp,gcp->blgc', s_im, c_im.astype(jnp.float32))
         + d_skip.astype(jnp.float32).reshape(SSM_GROUPS, SSM_GROUP) * uf)
    y = y.reshape(bsz, l, D_SSM).astype(u.dtype)
    z = jax.nn.gelu(y)
    return z * jax.nn.sigmoid(z @ w_glu + b_glu)

def hierarchical_moe(h, w_group_router, group_bias, w_expert_router, expert_bias, w_e_gate, w_e_up, w_e_down):
    bsz, l, d = h.shape
    t = bsz * l
    ht = h.reshape(t, d)
    group_logits = (ht @ w_group_router).astype(jnp.float32) + group_bias.astype(jnp.float32)
    group_prob = jax.nn.softmax(group_logits, axis=-1)
    g_prob, g_idx = lax.top_k(group_prob, 1)
    expert_logits = (ht @ w_expert_router).astype(jnp.float32) + expert_bias.astype(jnp.float32)
    expert_logits = expert_logits.reshape(t, N_GROUPS, EXPERTS_PER_GROUP)
    in_group = jnp.take_along_axis(expert_logits, g_idx[:, :, None], axis=1)[:, 0]
    e_prob = jax.nn.softmax(in_group, axis=-1)
    e_val, e_loc = lax.top_k(e_prob, TOP_K_2)
    e_val = e_val / jnp.sum(e_val, axis=-1, keepdims=True)
    weights = g_prob * e_val
    e_glob = g_idx * EXPERTS_PER_GROUP + e_loc
    gates = jnp.sum(jax.nn.one_hot(e_glob, N_EXPERTS_2, dtype=jnp.float32) * weights[..., None], axis=1)
    gates = gates.astype(h.dtype)
    a = jnp.einsum('td,edf->tef', ht, w_e_gate)
    u = jnp.einsum('td,edf->tef', ht, w_e_up)
    hid = jax.nn.silu(a) * u * gates[:, :, None]
    out = hid.reshape(t, N_EXPERTS_2 * D_EXPERT_2) @ w_e_down.reshape(N_EXPERTS_2 * D_EXPERT_2, d)
    return out.reshape(bsz, l, d)

def second_inputs(seed: int = 0) -> dict:
    key = jax.random.key(seed)
    ks = jax.random.split(key, 32)
    f32 = jnp.float32

    def nrm(k, shape, scale):
        return jax.random.normal(k, shape, f32) * scale

    n_idx = jnp.arange(SSM_STATE, dtype=f32)
    return {
        'x': nrm(ks[0], (BATCH, SEQ, D_MODEL), 1.0),
        'mix_norm_gain': 1.0 + nrm(ks[1], (DEPTH, D_MODEL), 0.02),
        'w_in': nrm(ks[2], (DEPTH, D_MODEL, D_IN_2), D_MODEL ** -0.5),
        'b_gate': nrm(ks[3], (DEPTH, N_BRANCH * D_MODEL), 0.02),
        'q_gain': 1.0 + nrm(ks[4], (DEPTH, HEAD_DIM), 0.02),
        'k_gain': 1.0 + nrm(ks[5], (DEPTH, HEAD_DIM), 0.02),
        'rel_bias': nrm(ks[6], (DEPTH, ATTN_HEADS, N_REL), 0.1),
        'ssm_lambda_re': -0.5 + nrm(ks[7], (DEPTH, SSM_GROUPS, SSM_STATE), 0.01),
        'ssm_lambda_im': math.pi * n_idx[None, None, :] + nrm(ks[8], (DEPTH, SSM_GROUPS, SSM_STATE), 0.01),
        'ssm_log_step': jax.random.uniform(ks[9], (DEPTH, SSM_GROUPS), f32, math.log(STEP_MIN), math.log(STEP_MAX)),
        'ssm_b_re': nrm(ks[10], (DEPTH, SSM_GROUPS, SSM_STATE, SSM_GROUP), (2 * SSM_GROUP) ** -0.5),
        'ssm_b_im': nrm(ks[11], (DEPTH, SSM_GROUPS, SSM_STATE, SSM_GROUP), (2 * SSM_GROUP) ** -0.5),
        'ssm_c_re': nrm(ks[12], (DEPTH, SSM_GROUPS, SSM_GROUP, SSM_STATE), (2 * SSM_STATE) ** -0.5),
        'ssm_c_im': nrm(ks[13], (DEPTH, SSM_GROUPS, SSM_GROUP, SSM_STATE), (2 * SSM_STATE) ** -0.5),
        'ssm_d': nrm(ks[14], (DEPTH, D_SSM), 1.0),
        'w_glu': nrm(ks[15], (DEPTH, D_SSM, D_SSM), D_SSM ** -0.5),
        'b_glu': nrm(ks[16], (DEPTH, D_SSM), 0.02),
        'w_branch': nrm(ks[17], (DEPTH, D_ATTN + D_SSM, D_MODEL), D_ATTN ** -0.5),
        'w_out': nrm(ks[18], (DEPTH, D_MODEL, D_MODEL), D_MODEL ** -0.5),
        'ffn_norm_gain': 1.0 + nrm(ks[19], (DEPTH, D_MODEL), 0.02),
        'w_group_router': nrm(ks[20], (DEPTH, D_MODEL, N_GROUPS), D_MODEL ** -0.5),
        'group_bias': nrm(ks[21], (DEPTH, N_GROUPS), 0.01),
        'w_expert_router': nrm(ks[22], (DEPTH, D_MODEL, N_EXPERTS_2), D_MODEL ** -0.5),
        'expert_bias': nrm(ks[23], (DEPTH, N_EXPERTS_2), 0.01),
        'w_e_gate': nrm(ks[24], (DEPTH, N_EXPERTS_2, D_MODEL, D_EXPERT_2), D_MODEL ** -0.5),
        'w_e_up': nrm(ks[25], (DEPTH, N_EXPERTS_2, D_MODEL, D_EXPERT_2), D_MODEL ** -0.5),
        'w_e_down': nrm(ks[26], (DEPTH, N_EXPERTS_2, D_EXPERT_2, D_MODEL), D_EXPERT_2 ** -0.5),
    }

def second_block(x, mix_norm_gain, w_in, b_gate, q_gain, k_gain, rel_bias,
              ssm_lambda_re, ssm_lambda_im, ssm_log_step, ssm_b_re, ssm_b_im,
              ssm_c_re, ssm_c_im, ssm_d, w_glu, b_glu, w_branch, w_out,
              ffn_norm_gain, w_group_router, group_bias, w_expert_router, expert_bias,
              w_e_gate, w_e_up, w_e_down):
    bsz, l, _ = x.shape
    for i in range(DEPTH):
        h = rms_norm(x, mix_norm_gain[i])
        proj = h @ w_in[i]
        q = proj[..., :D_ATTN].reshape(bsz, l, ATTN_HEADS, HEAD_DIM)
        k = proj[..., D_ATTN:2 * D_ATTN].reshape(bsz, l, ATTN_HEADS, HEAD_DIM)
        v = proj[..., 2 * D_ATTN:3 * D_ATTN].reshape(bsz, l, ATTN_HEADS, HEAD_DIM)
        u = proj[..., 3 * D_ATTN:3 * D_ATTN + D_SSM]
        gate = jax.nn.sigmoid(proj[..., 3 * D_ATTN + D_SSM:] + b_gate[i])
        gate = gate.reshape(bsz, l, N_BRANCH, D_MODEL)
        y_attn = chunked_relpos_attention(q, k, v, q_gain[i], k_gain[i], rel_bias[i])
        y_ssm = s5_ssm_glu(u, ssm_lambda_re[i], ssm_lambda_im[i], ssm_log_step[i],
                           ssm_b_re[i], ssm_b_im[i], ssm_c_re[i], ssm_c_im[i],
                           ssm_d[i], w_glu[i], b_glu[i])
        wb = w_branch[i]
        merged = (gate[:, :, 0] * (y_attn @ wb[:D_ATTN])
                  + gate[:, :, 1] * (y_ssm @ wb[D_ATTN:]))
        x = x + merged @ w_out[i]
        h = rms_norm(x, ffn_norm_gain[i])
        x = x + hierarchical_moe(h, w_group_router[i], group_bias[i], w_expert_router[i],
                                 expert_bias[i], w_e_gate[i], w_e_up[i], w_e_down[i])
    return x


def setup_inputs(seed=0):
    out = dict(first_inputs(seed))
    for name, value in second_inputs(seed + 1).items():
        if name != "x":
            out[name + "_2"] = value
    return out


def reference(
    x, c, ctx, c_ctx, w_ada, b_ada, g_pre_mix, g_post_mix, g_pre_ffn, g_post_ffn, w_in, b_in,
    b_gate, mlstm_norm_g, conv_w, conv_b, conv_ln_g, conv_ln_b, w_out, b_out, w_router,
    b_router, we_gate, we_up, we_down, ws_gate, ws_up, ws_down, mix_norm_gain_2, w_in_2,
    b_gate_2, q_gain_2, k_gain_2, rel_bias_2, ssm_lambda_re_2, ssm_lambda_im_2, ssm_log_step_2,
    ssm_b_re_2, ssm_b_im_2, ssm_c_re_2, ssm_c_im_2, ssm_d_2, w_glu_2, b_glu_2, w_branch_2,
    w_out_2, ffn_norm_gain_2, w_group_router_2, group_bias_2, w_expert_router_2, expert_bias_2,
    w_e_gate_2, w_e_up_2, w_e_down_2,
):
    x = first_block(
        x, c, ctx, c_ctx, w_ada, b_ada, g_pre_mix, g_post_mix, g_pre_ffn, g_post_ffn, w_in,
        b_in, b_gate, mlstm_norm_g, conv_w, conv_b, conv_ln_g, conv_ln_b, w_out, b_out,
        w_router, b_router, we_gate, we_up, we_down, ws_gate, ws_up, ws_down,
    )
    return second_block(
        x, mix_norm_gain_2, w_in_2, b_gate_2, q_gain_2, k_gain_2, rel_bias_2, ssm_lambda_re_2,
        ssm_lambda_im_2, ssm_log_step_2, ssm_b_re_2, ssm_b_im_2, ssm_c_re_2, ssm_c_im_2,
        ssm_d_2, w_glu_2, b_glu_2, w_branch_2, w_out_2, ffn_norm_gain_2, w_group_router_2,
        group_bias_2, w_expert_router_2, expert_bias_2, w_e_gate_2, w_e_up_2, w_e_down_2,
    )


_drawn_inputs = setup_inputs


def setup_inputs(seed=0):
    import zlib

    import numpy as np

    out = dict(_drawn_inputs(seed))
    spreads = {}
    factors = {'conv_ln_b': 2.819,
     'mix_norm_gain_2': 3.657,
     'b_gate_2': 8.0,
     'q_gain_2': 8.0,
     'k_gain_2': 5.985,
     'rel_bias_2': 5.44,
     'ssm_lambda_re_2': 64.0,
     'ssm_log_step_2': 18.887,
     'ssm_b_re_2': 31.728,
     'ssm_b_im_2': 24.624,
     'ssm_c_re_2': 28.848,
     'ssm_c_im_2': 24.952,
     'b_glu_2': 23.275,
     'group_bias_2': 46.705,
     'expert_bias_2': 33.413,
     'ssm_lambda_im_2': 6.289,
     'ffn_norm_gain_2': 4.721}
    for name, (base, spread) in spreads.items():
        noise = np.random.default_rng([zlib.crc32(name.encode()), seed]).standard_normal(out[name].shape)
        drawn = base * np.exp(spread * noise) if base else spread * noise
        out[name] = jnp.asarray(drawn.astype(out[name].dtype))
    for name, factor in factors.items():
        out[name] = (out[name] * factor).astype(out[name].dtype)
    return out
```

```python
import math
from contextlib import ExitStack

import concourse.bass as bass
from concourse import mybir

F32 = mybir.dt.float32
I32 = mybir.dt.int32
ACT = mybir.ActivationFunctionType
ALU = mybir.AluOpType
AX_X = mybir.AxisListType.X

P = 128
D = 1024
KD = D // P
T = 1024
NT = T // P
CTX = 256
NC = CTX // P
EPS = 1e-6
NEG = -1.0e30

H1, DK, DV = 4, 64, 128
D_QK, D_V = H1 * DK, H1 * DV
C_QK, C_V, C_O, C_GT = 0, 2 * D_QK, 2 * D_QK + D_V, 2 * D_QK + 2 * D_V
N_GT = 4 * H1
C_GA = C_GT + N_GT
D_CONV = 512
C_GB = C_GA + D_CONV
KC = D_CONV // P
TAPS = 31
GRID = 64
ROWS = T // GRID
PAD = TAPS // 2
STEPS = NC + NT
NCOL = STEPS * 2 * H1
E1, F1, TOP1 = 64, 256, 8
ROUTE_SCALE = 2.5


class Chain:

    def __init__(self, nc, name):
        self.sem, self.n = nc.alloc_semaphore(name), 0

    def then(self, ins):
        self.n += 1
        return ins.then_inc(self.sem, 1)

    def wait(self, eng):
        eng.wait_ge(self.sem, self.n)

    def link(self, eng, ins):
        self.then(ins)
        self.wait(eng)


class State:
    pass


def setup(nc, A, out):
    s = State()
    s.nc, s.A, s.out = nc, A, out
    sb = lambda name, shape, dt=F32: nc.alloc_sbuf_tensor(name, shape, dt)
    s.psum = nc.alloc_psum_tensor("psum", [P, 8 * 512], F32)
    s.bank = [s.psum[:, i * 512:(i + 1) * 512] for i in range(8)]
    s.ident = sb("ident", [P, P])
    s.ones = sb("ones", [P, P])
    s.tri_le = sb("tri_le", [P, P])
    s.tri_ge = sb("tri_ge", [P, P])
    s.vec = sb("vec", [P, P])
    s.vec2 = sb("vec2", [P, 18])
    s.convw = sb("convw", [P, TAPS * KC])
    s.mod = sb("mod", [P, 4, KD, 2])
    s.gpost = sb("gpost", [P, 2, D])
    s.x = sb("x", [P, NT, D])
    s.hT = sb("hT", [P, KD, T])
    s.stat = sb("stat", [P, 64])
    s.act_c = Chain(nc, "act_own")
    s.dve_c = Chain(nc, "dve_own")
    s.pool_c = Chain(nc, "pool_own")
    s.sems = []
    return s


COL_BANK = {0: 1, 1: 6, 3: 7, 4: 0}

VEC = {"b_ada": 0, "g_pre_mix": 48, "g_pre_ffn": 56, "mix_norm_gain_2": 64, "ffn_norm_gain_2": 72,
       "b_qk": 80, "b_gab": 84, "b_gate_2": 92, "b_glu_2": 108, "conv_b": 112, "conv_ln_g": 116,
       "conv_ln_b": 120, "spare": 124}


def sem(s, name):
    s.sems.append(s.nc.alloc_semaphore(name))
    return s.sems[-1]


def return_sems(s):
    s.nc.clear_and_free_semaphores(s.sems)
    s.sems = []
    s.nc.all_engine_barrier()


def rows_of(ap, n):
    return ap.rearrange("a (r p) -> (a r) p", p=P)


def stage_condition(s):
    nc, A = s.nc, s.A
    with nc.sbuf_tensor("v1", [P, P], F32) as v1, nc.sbuf_tensor("v2", [18, P], F32) as v2, \
            nc.sbuf_tensor("v3", [TAPS * KC, P], F32) as v3, \
            nc.sbuf_tensor("wada", [P, 2, KD, D], F32) as wada, \
            nc.sbuf_tensor("brow", [P, 4, D], F32) as brow, \
            nc.sbuf_tensor("cond", [P, KD, 2], F32) as cond, \
            nc.sbuf_tensor("condw", [P, KD, P], F32) as condw:
        vecs_in, x_in, rows_in = sem(s, "vecs_in"), sem(s, "x_in"), sem(s, "rows_in")
        s.x_in = x_in
        wada_in = [sem(s, "wada_in0"), sem(s, "wada_in1")]
        consts_set, vecs_turned, vecs_ready = sem(s, "consts_set"), sem(s, "vecs_turned"), sem(s, "vecs_ready")
        cond_ready, ada_done, ada_read = sem(s, "cond_ready"), sem(s, "ada_done"), sem(s, "ada_read")
        wide_ready = sem(s, "wide_ready")
        w_src = A["w_ada"][0].rearrange("(k p) (s n) -> s p k n", p=P, n=D)
        N_VEC = 20
        with nc.Block() as block:
            @block.sync
            def _(sp):
                def vec(dst, src):
                    sp.dma_start(dst, src).then_inc(vecs_in, 16)
                for k in range(0, KD, 2):
                    sp.dma_start(wada[:, 0, k:k + 2], w_src[0][:, k:k + 2]).then_inc(wada_in[0], 16)
                vec(v1[0:48, :], rows_of(A["b_ada"], 48))
                for n in ("g_pre_mix", "g_pre_ffn", "mix_norm_gain_2", "ffn_norm_gain_2"):
                    vec(v1[VEC[n]:VEC[n] + 8, :], rows_of(A[n], 8))
                vec(v1[80:84, :], rows_of(A["b_in"][:, 0:512], 4))
                vec(v1[84:92, :], rows_of(A["b_in"][:, C_GA:C_GA + 1024], 8))
                vec(v1[92:108, :], rows_of(A["b_gate_2"], 16))
                vec(v1[108:112, :], rows_of(A["b_glu_2"], 4))
                for n in ("conv_b", "conv_ln_g", "conv_ln_b"):
                    vec(v1[VEC[n]:VEC[n] + 4, :], rows_of(A[n], 4))
                vec(v1[124:128, :], rows_of(A["conv_b"], 4))
                vec(v2[0:8, :], rows_of(A["c"], 8))
                vec(v2[8:16, :], A["c_ctx"].rearrange("(r p) -> r p", p=P))
                for r, n in ((16, "q_gain_2"), (17, "k_gain_2")):
                    for h in range(2):
                        vec(v2[r:r + 1, h * 64:h * 64 + 64], A[n])
                vec(v3[:, :], A["conv_w"][0].rearrange("w (m p) -> (w m) p", p=P))
                for r, (n, c0) in enumerate((("b_ada", 2 * D), ("g_post_mix", 0), ("b_ada", 5 * D), ("g_post_ffn", 0))):
                    sp.dma_start(brow[:, r, :], A[n][0:1, c0:c0 + D].to_broadcast([P, D])).then_inc(rows_in, 16)
                for i in range(1, 6):
                    if i >= 2:
                        sp.wait_ge(ada_done, i - 1)
                    for k in range(0, KD, 2):
                        sp.dma_start(wada[:, i % 2, k:k + 2], w_src[i][:, k:k + 2]).then_inc(wada_in[i % 2], 16)
                    if i == 1:
                        for t in range(NT):
                            sp.dma_start(s.x[:, t, :], A["x"][0, t * P:(t + 1) * P, :]).then_inc(x_in, 16)

            @block.gpsimd
            def _(pool):
                c = s.pool_c
                c.then(pool.memset(s.ident[:, :], 0.0))
                c.then(pool.memset(s.ones[:, :], 1.0))
                c.then(pool.memset(s.tri_le[:, :], 1.0))
                c.then(pool.memset(s.tri_ge[:, :], 1.0))
                c.wait(pool)
                pool.affine_select(out=s.ident[:, :], in_=s.ident[:, :], compare_op=ALU.not_equal, fill=1.0,
                                   base=0, pattern=[[-1, P]], channel_multiplier=1).then_inc(consts_set, 1)
                pool.affine_select(out=s.tri_le[:, :], in_=s.tri_le[:, :], compare_op=ALU.is_ge, fill=0.0,
                                   base=0, pattern=[[1, P]], channel_multiplier=-1).then_inc(consts_set, 1)
                pool.affine_select(out=s.tri_ge[:, :], in_=s.tri_ge[:, :], compare_op=ALU.is_ge, fill=0.0,
                                   base=0, pattern=[[-1, P]], channel_multiplier=1).then_inc(consts_set, 1)

            @block.tensor
            def _(pe):
                pe.wait_ge(consts_set, 3)
                pe.wait_ge(vecs_in, 16 * N_VEC)
                pe.transpose(s.bank[0][:, 0:P], v1[:, :], s.ident[:, :])
                pe.transpose(s.bank[0][:, 128:146], v2[:, :], s.ident[0:18, 0:18])
                pe.transpose(s.bank[0][:, 256:256 + TAPS * KC], v3[:, :],
                             s.ident[0:TAPS * KC, 0:TAPS * KC]).then_inc(vecs_turned, 1)
                pe.wait_ge(cond_ready, 1)
                pe.wait_ge(wide_ready, 1)
                for i in range(6):
                    pe.wait_ge(wada_in[i % 2], 16 * (KD // 2) * (i // 2 + 1))
                    w = wada[:, i % 2]
                    if i % 3 == 2:
                        for n in range(2):
                            for k in range(KD):
                                last = pe.matmul(s.bank[2 + n + 2 * (i // 3)][:, :], condw[:, k, :],
                                                 w[:, k, n * 512:(n + 1) * 512], start=(k == 0), stop=(k == KD - 1))
                    else:
                        for m in range(KD):
                            for k in range(KD):
                                last = pe.matmul(s.bank[COL_BANK[i]][:, 16 * i + 2 * m:16 * i + 2 * m + 2],
                                                 w[:, k, m * P:(m + 1) * P], cond[:, k, :],
                                                 start=(k == 0), stop=(k == KD - 1))
                    last.then_inc(ada_done, 1)

            @block.scalar
            def _(act):
                act.wait_ge(vecs_ready, 1)
                act.activation(cond[:, :, :].rearrange("p k j -> p j k"),
                               s.vec2[:, 0:16].rearrange("p (j k) -> p j k", j=2), ACT.Silu).then_inc(cond_ready, 1)

            @block.vector
            def _(dve):
                c = s.dve_c
                dve.wait_ge(vecs_turned, 1)
                c.then(dve.tensor_copy(s.vec[:, :], s.bank[0][:, 0:P]))
                c.then(dve.tensor_copy(s.convw[:, :], s.bank[0][:, 256:256 + TAPS * KC]))
                dve.tensor_copy(s.vec2[:, :], s.bank[0][:, 128:146]).then_inc(vecs_ready, 1)
                dve.wait_ge(cond_ready, 1)
                dve.tensor_copy(condw[:, :, :], cond[:, :, 0:1].to_broadcast([P, KD, P])).then_inc(wide_ready, 1)
                c.wait(dve)
                dve.wait_ge(rows_in, 64)
                for i in range(6):
                    dve.wait_ge(ada_done, i + 1)
                    if i % 3 == 2:
                        h = i // 3
                        for n in range(2):
                            cols = slice(n * 512, (n + 1) * 512)
                            c.link(dve, dve.tensor_tensor(s.gpost[:, h, cols], s.bank[2 + n + 2 * h][:, :],
                                                          brow[:, 2 * h, cols], ALU.add))
                            c.then(dve.tensor_tensor(s.gpost[:, h, cols], s.gpost[:, h, cols],
                                                     brow[:, 2 * h + 1, cols], ALU.mult))
                    else:
                        j = i if i < 2 else i - 1
                        got = s.bank[COL_BANK[i]][:, 16 * i:16 * i + 16].rearrange("p (m j) -> p m j", j=2)
                        bias = s.vec[:, 8 * i:8 * i + 8].rearrange("p (m o) -> p m o", o=1).to_broadcast([P, KD, 2])
                        c.link(dve, dve.tensor_tensor(s.mod[:, j], got, bias, ALU.add))
                        if i % 3 == 1:
                            g = VEC["g_pre_mix"] if i == 1 else VEC["g_pre_ffn"]
                            gain = s.vec[:, g:g + 8].rearrange("p (m o) -> p m o", o=1).to_broadcast([P, KD, 2])
                            c.then(dve.scalar_tensor_tensor(s.mod[:, j], s.mod[:, j], 1.0, gain, ALU.add, ALU.mult))


def stage_norm(s, name, src, n_tiles, dst, gain, shift, loaded=None, rows_to=None):
    nc = s.nc
    G = min(4, n_tiles)
    with nc.sbuf_tensor(f"{name}_sq", [P, 2, D], F32) as sq, \
            nc.sbuf_tensor(f"{name}_xn", [P, n_tiles, D], F32) as xn, \
            nc.sbuf_tensor(f"{name}_ss", [P, n_tiles], F32) as ss, \
            nc.sbuf_tensor(f"{name}_rs", [P, n_tiles], F32) as rs:
        summed, inverted, rooted = sem(s, f"{name}_summed"), sem(s, f"{name}_inverted"), sem(s, f"{name}_rooted")
        normed, turned, moved_a, moved_v = (sem(s, f"{name}_{x}") for x in ("normed", "turned", "moved_a", "moved_v"))
        with nc.Block() as block:
            if rows_to is not None:
                kept = sem(s, f"{name}_kept")

                @block.sync
                def _(sp):
                    for t in range(n_tiles):
                        sp.wait_ge(normed, t + 1)
                        sp.dma_start(rows_to[t * P:(t + 1) * P, :], xn[:, t, :]).then_inc(kept, 16)
                    sp.wait_ge(kept, 16 * n_tiles)

            @block.scalar
            def _(act):
                if loaded is not None:
                    act.wait_ge(loaded, 16 * n_tiles)
                for t in range(n_tiles):
                    if t >= 2:
                        act.wait_ge(summed, t - 1)
                    act.activation(sq[:, t % 2, :], src[:, t, :], ACT.Square,
                                   accum_out=ss[:, t:t + 1]).then_inc(summed, 1)
                act.wait_ge(inverted, 1)
                act.activation(rs[:, :], ss[:, :], ACT.Sqrt).then_inc(rooted, 1)
                for i in range(1, KD * n_tiles // G, 2):
                    g, k = divmod(i, KD)
                    act.wait_ge(turned, i + 1)
                    act.activation(dst[:, k, g * G * P:(g + 1) * G * P], s.bank[i % 8][:, 0:G * P], ACT.Identity,
                                   scale=gain(k), bias=shift(k) if shift else 0.0).then_inc(moved_a, 1)

            @block.vector
            def _(dve):
                c = s.dve_c
                dve.wait_ge(summed, n_tiles)
                c.link(dve, dve.tensor_scalar(ss[:, :], ss[:, :], 1.0 / D, EPS, ALU.mult, ALU.add))
                dve.reciprocal(ss[:, :], ss[:, :]).then_inc(inverted, 1)
                dve.wait_ge(rooted, 1)
                for t in range(n_tiles):
                    dve.tensor_scalar(xn[:, t, :], src[:, t, :], rs[:, t:t + 1], None, ALU.mult).then_inc(normed, 1)
                for i in range(0, KD * n_tiles // G, 2):
                    g, k = divmod(i, KD)
                    dve.wait_ge(turned, i + 1)
                    to, of = dst[:, k, g * G * P:(g + 1) * G * P], s.bank[i % 8][:, 0:G * P]
                    if shift:
                        dve.tensor_scalar(to, of, gain(k), shift(k), ALU.mult, ALU.add).then_inc(moved_v, 1)
                    else:
                        dve.tensor_scalar(to, of, gain(k), None, ALU.mult).then_inc(moved_v, 1)

            @block.tensor
            def _(pe):
                for i in range(KD * n_tiles // G):
                    g, k = divmod(i, KD)
                    if k == 0:
                        pe.wait_ge(normed, G * (g + 1))
                    if i >= 8:
                        pe.wait_ge((moved_v, moved_a)[i % 2], (i - 8) // 2 + 1)
                    for j in range(G):
                        last = pe.transpose(s.bank[i % 8][:, j * P:(j + 1) * P],
                                            xn[:, g * G + j, k * P:(k + 1) * P], s.ident[:, :])
                    last.then_inc(turned, 1)


def project_plan():
    plan = [("qk", m, n) for n in range(3) for m in range(4) if n < 2 or m >= 2]
    plan += [("v", t, 0) for t in range(STEPS)] + [("kt", t, 0) for t in range(STEPS)]
    plan += [("gt", t, 0) for t in range(STEPS)]
    plan += [("o", t, 0) for t in range(NT)]
    plan += [(kind, m, n) for m in range(KC) for n in range(2) for kind in ("gb", "ga")]
    return plan


def stage_project(s):
    nc, A = s.nc, s.A
    plan = project_plan()
    by_act = ("kt", "gb")
    place = []
    count = {True: 0, False: 0}
    for kind, _, _ in plan:
        count[kind in by_act] += 1
        place.append(count[kind in by_act])
    first = {kind: min(i for i, p in enumerate(plan) if p[0] == kind) for kind in ("qk", "v", "kt", "gt", "o", "ga", "gb")}
    last_of = {kind: max(i for i, p in enumerate(plan) if p[0] == kind) for kind in ("qk", "v", "kt", "gt", "o", "ga", "gb")}
    with nc.sbuf_tensor("w_ring", [P, 2, KD, 512], F32) as ring:
        w_in = A["w_in"][0].rearrange("(k p) n -> p k n", p=P)
        biases_in, sig_free = sem(s, "biases_in"), sem(s, "sig_free")
        w_ready = {k: sem(s, f"w_{k}_in") for k in ("qk", "v", "gt", "o", "gab0", "gab1")}
        tile_done, moved_v, moved_a = sem(s, "proj_tile_done"), sem(s, "proj_moved_v"), sem(s, "proj_moved_a")
        o_added, sig_ready, pads_set = sem(s, "o_added"), sem(s, "sig_ready"), sem(s, "pads_set")
        b_v, b_o = s.x[:, 0, 0:512], s.x[:, 0, 512:1024]
        sig = s.x[:, 1, :].rearrange("p (b n) -> p b n", b=2)
        with nc.Block() as block, nc.sbuf_tensor("b_gt", [P, 2, N_GT], F32) as b_gt, \
                nc.sbuf_tensor("w_gt", [P, KD, N_GT], F32) as w_gt:
            @block.sync
            def _(sp):
                def load(slot, c0, signal, to=0, n=512):
                    for k in range(0, KD, 4):
                        sp.dma_start(ring[:, slot, k:k + 4, to:to + n], w_in[:, k:k + 4, c0:c0 + n]).then_inc(signal, 16)
                load(0, C_QK, w_ready["qk"])
                load(1, C_V, w_ready["v"])
                sp.dma_start(w_gt[:, :, :], w_in[:, :, C_GT:C_GT + N_GT]).then_inc(w_ready["gt"], 16)
                sp.dma_start(b_v, A["b_in"][0:1, C_V:C_V + 512].to_broadcast([P, 512])).then_inc(biases_in, 16)
                sp.dma_start(b_o, A["b_in"][0:1, C_O:C_O + 512].to_broadcast([P, 512])).then_inc(biases_in, 16)
                sp.dma_start(b_gt[:, 0, :], A["b_in"][0:1, C_GT:C_GT + N_GT].to_broadcast([P, N_GT])).then_inc(biases_in, 16)
                sp.dma_start(b_gt[:, 1, :], A["b_gate"].rearrange("a b h -> a (b h)").to_broadcast([P, N_GT])).then_inc(biases_in, 16)
                sp.wait_ge(tile_done, last_of["qk"] + 1)
                load(0, C_O, w_ready["o"])
                sp.wait_ge(tile_done, last_of["v"] + 1)
                load(1, C_GA, w_ready["gab0"], 0, 256)
                load(1, C_GB, w_ready["gab0"], 256, 256)
                sp.wait_ge(tile_done, last_of["o"] + 1)
                load(0, C_GA + 256, w_ready["gab1"], 0, 256)
                load(0, C_GB + 256, w_ready["gab1"], 256, 256)

            @block.tensor
            def _(pe):
                for i, (kind, a, n) in enumerate(plan):
                    bank = s.bank[i % 8]
                    if i >= 8:
                        pe.wait_ge(moved_a if plan[i - 8][0] in by_act else moved_v, place[i - 8])
                    if i == first[kind] and kind in ("qk", "v", "gt", "o"):
                        pe.wait_ge(w_ready[kind], 16 if kind == "gt" else 32)
                    if (kind, n) == ("gb", 0) and a in (0, 2):
                        pe.wait_ge(w_ready[f"gab{a // 2}"], 64)
                    if kind in ("v", "gt", "o"):
                        h = s.hcT[:, :, (a - NT) * P:(a - NT + 1) * P] if a >= NT else s.hT[:, :, a * P:(a + 1) * P]
                        w = w_gt[:, :, :] if kind == "gt" else ring[:, {"v": 1, "o": 0}[kind]]
                        for k in range(KD):
                            last = pe.matmul(bank[:, 0:N_GT if kind == "gt" else 512], h[:, k], w[:, k],
                                             start=(k == 0), stop=(k == KD - 1))
                    elif kind == "kt":
                        if i == first["kt"]:
                            pe.wait_ge(moved_v, place[last_of["qk"]])
                        for m in range(2):
                            last = pe.transpose(bank[:, m * P:(m + 1) * P], s.qkT[:, 2 + m, a * P:(a + 1) * P], s.ident[:, :])
                    else:
                        width = CTX if n == 2 else 512
                        h = s.hcT if n == 2 else s.hT[:, :, n * 512:(n + 1) * 512]
                        if kind == "qk":
                            w, c0 = ring[:, 0], a * P
                        else:
                            w, c0 = ring[:, 1 - a // 2], (a % 2) * P + (256 if kind == "gb" else 0)
                        for k in range(KD):
                            last = pe.matmul(bank[:, 0:width], w[:, k, c0:c0 + P], h[:, k, :],
                                             start=(k == 0), stop=(k == KD - 1))
                    last.then_inc(tile_done, 1)

            @block.vector
            def _(dve):
                dve.wait_ge(biases_in, 64)
                c = s.dve_c
                c.link(dve, dve.tensor_tensor(b_gt[:, 0, :], b_gt[:, 0, :], b_gt[:, 1, :], ALU.add))
                n_sig = 0
                for i, (kind, a, n) in enumerate(plan):
                    if kind in by_act:
                        continue
                    bank = s.bank[i % 8]
                    dve.wait_ge(tile_done, i + 1)
                    if kind == "qk":
                        width = CTX if n == 2 else 512
                        bias = s.vec[:, VEC["b_qk"] + a:VEC["b_qk"] + a + 1]
                        moved = dve.tensor_scalar(s.qkT[:, a, n * 512:n * 512 + width], bank[:, 0:width], bias,
                                                  DK ** -0.5 if a >= 2 else 1.0, ALU.add, ALU.mult)
                    elif kind == "v":
                        moved = dve.tensor_tensor(s.v_aug[:, a, :, 0:DV], bank[:, :].rearrange("p (h v) -> p h v", h=H1),
                                                  b_v.rearrange("p (h v) -> p h v", h=H1), ALU.add)
                    elif kind == "gt":
                        moved = dve.tensor_tensor(s.gates[:, a, :], bank[:, 0:N_GT], b_gt[:, 0, :], ALU.add)
                    elif kind == "o":
                        c.then(dve.tensor_tensor(s.sig_o[:, a, :], bank[:, :], b_o, ALU.add))
                        c.wait(dve)
                        moved = dve.sem_inc(moved_v, 1)
                        dve.sem_inc(o_added, 1)
                        continue
                    else:
                        if n_sig == 0:
                            dve.wait_ge(pads_set, 1)
                        dve.wait_ge(sig_ready, n_sig + 1)
                        bias = s.vec[:, VEC["b_gab"] + a:VEC["b_gab"] + a + 1]
                        to = s.upad[:, a, n * ROWS // 2:(n + 1) * ROWS // 2, PAD:PAD + GRID]
                        moved = dve.scalar_tensor_tensor(to, bank[:, :].rearrange("p (r w) -> p r w", w=GRID), bias,
                                                         sig[:, n_sig % 2, :].rearrange("p (r w) -> p r w", w=GRID),
                                                         ALU.add, ALU.mult)
                        n_sig += 1
                    moved.then_inc(moved_v, 1)

            @block.scalar
            def _(act):
                n_sig = 0
                for i, (kind, a, n) in enumerate(plan):
                    if kind == "o":
                        act.wait_ge(o_added, a + 1)
                        s.act_c.then(act.activation(s.sig_o[:, a, :], s.sig_o[:, a, :], ACT.Sigmoid))
                    if kind not in by_act:
                        continue
                    bank = s.bank[i % 8]
                    act.wait_ge(tile_done, i + 1)
                    if kind == "kt":
                        act.activation(s.k_tok[:, a, :], bank[:, 0:2 * P], ACT.Copy).then_inc(moved_a, 1)
                    else:
                        if n_sig >= 2:
                            act.wait_ge(moved_v, place[first["ga"]] + n_sig - 2)
                        bias = s.vec[:, VEC["b_gab"] + 4 + a:VEC["b_gab"] + 5 + a]
                        act.activation(sig[:, n_sig % 2, :], bank[:, :], ACT.Sigmoid, bias=bias).then_inc(moved_a, 1)
                        act.wait_ge(moved_a, place[i])
                        act.sem_inc(sig_ready, 1)
                        n_sig += 1

            @block.gpsimd
            def _(pool):
                c = s.pool_c
                c.then(pool.memset(s.v_aug[:, :, :, DV:DV + 1], 1.0))
                pool.memset(s.upad[:, :, :, :], 0.0).then_inc(pads_set, 1)


def fwd_tile(j):
    return (j + NT) % STEPS


def bwd_tile(j):
    return STEPS - 1 - j


def stage_gates(s):
    nc = s.nc
    V = {n: nc.sbuf_tensor(f"g_{n}", [P, STEPS, 2, H1], F32) for n in ("LI", "FG", "AB", "MN", "BT", "TOT", "CM", "MT", "tmp", "tmp2")}
    with ExitStack() as ctx:
        V = {n: ctx.enter_context(v) for n, v in V.items()}
        ET = ctx.enter_context(nc.sbuf_tensor("g_ET", [NCOL, 3, P], F32))
        abs_ready, logs_ready, lf_ready, sums_done = (sem(s, f"g_{x}") for x in ("abs_ready", "logs_ready", "lf_ready", "sums_done"))
        e_ready, e_turned, e_max, scans_ready, scans_turned = (sem(s, f"g_{x}") for x in ("e_ready", "e_turned", "e_max", "scans_ready", "scans_turned"))
        mt_ready, mt_turned, exps_ready = (sem(s, f"g_{x}") for x in ("mt_ready", "mt_turned", "exps_ready"))
        flat = lambda t: t[:, :, :, :].rearrange("p j d h -> p (j d h)")
        s_of = lambda b, w=NCOL: b[:, 0:w]
        with nc.Block() as block:
            @block.vector
            def _(dve):
                c = s.dve_c
                G = s.gates
                for to, g0 in ((V["LI"], 0), (V["FG"], H1)):
                    c.then(dve.tensor_copy(to[:, 0:NC, 0, :], G[:, NT:STEPS, g0:g0 + H1]))
                    c.then(dve.tensor_copy(to[:, NC:STEPS, 0, :], G[:, 0:NT, g0:g0 + H1]))
                    for j in range(STEPS):
                        c.then(dve.tensor_copy(to[:, j, 1, :], G[:, bwd_tile(j), 2 * H1 + g0:3 * H1 + g0]))
                c.wait(dve)
                c.then(dve.tensor_scalar(flat(V["MN"]), flat(V["FG"]), 0.0, None, ALU.min))
                c.link(dve, dve.tensor_scalar(flat(V["AB"]), flat(V["FG"]), -1.0, None, ALU.mult))
                dve.tensor_tensor(flat(V["AB"]), flat(V["AB"]), flat(V["FG"]), ALU.max).then_inc(abs_ready, 1)
                dve.wait_ge(logs_ready, 1)
                dve.tensor_tensor(flat(V["FG"]), flat(V["MN"]), flat(V["AB"]), ALU.subtract).then_inc(lf_ready, 1)
                dve.wait_ge(sums_done, 1)
                for d in range(2):
                    got = s.bank[d][:, 0:NCOL].rearrange("p (j d h) -> p j d h", j=STEPS, d=2)
                    c.then(dve.tensor_copy(V["BT"][:, :, d, :], got[:, :, d, :]))
                c.then(dve.tensor_copy(flat(V["TOT"]), s.bank[2][:, 0:NCOL]))
                c.wait(dve)
                dve.tensor_tensor(flat(s.E), flat(V["LI"]), flat(V["BT"]), ALU.subtract).then_inc(e_ready, 1)
                dve.wait_ge(e_turned, 1)
                c.link(dve, dve.tensor_copy(ET[:, 0, :], s.bank[3][0:NCOL, 0:P]))
                dve.tensor_tensor_scan(ET[:, 1, :], ET[:, 0, :], ET[:, 0, :], NEG, ALU.max, ALU.max).then_inc(scans_ready, 1)
                dve.tensor_tensor_scan(ET[:, 2, ::-1], ET[:, 0, ::-1], ET[:, 0, ::-1], NEG, ALU.max, ALU.max).then_inc(scans_ready, 1)
                dve.wait_ge(scans_turned, 1)
                for d in range(2):
                    got = s.bank[4][:, d * P:d * P + NCOL].rearrange("p (j d h) -> p j d h", j=STEPS, d=2)
                    c.then(dve.tensor_copy(V["CM"][:, :, d, :], got[:, :, d, :]))
                c.link(dve, dve.memset(s.M[:, 0], 0.0))
                dve.wait_ge(e_max, 1)
                for j in range(STEPS):
                    c.link(dve, dve.tensor_tensor(s.MX[:, j], s.M[:, j], s.EM[:, j], ALU.max))
                    c.link(dve, dve.tensor_tensor(s.M[:, j + 1], V["TOT"][:, j], s.MX[:, j], ALU.add))
                M = s.M[:, 0:STEPS].rearrange("p j d h -> p (j d h)")
                c.link(dve, dve.tensor_tensor(flat(V["MT"]), M, flat(V["CM"]), ALU.max))
                c.link(dve, dve.tensor_scalar(flat(V["tmp"]), flat(V["MT"]), -1.0, None, ALU.mult))
                c.then(dve.tensor_tensor(flat(s.EI), M, flat(V["MT"]), ALU.subtract))
                c.then(dve.tensor_tensor(flat(s.EN), flat(V["tmp"]), flat(V["BT"]), ALU.subtract))
                c.then(dve.tensor_tensor(flat(s.WS), flat(s.E), flat(s.MX), ALU.subtract))
                c.then(dve.tensor_tensor(flat(s.EA), M, flat(s.MX), ALU.subtract))
                c.wait(dve)
                dve.sem_inc(mt_ready, 1)
                dve.wait_ge(mt_turned, 1)
                c.link(dve, dve.tensor_copy(s.NMT[:, :], s.bank[5][0:NCOL, 0:P]))
                dve.wait_ge(exps_ready, 4)

            @block.scalar
            def _(act):
                c = s.act_c
                act.wait_ge(abs_ready, 1)
                c.link(act, act.activation(flat(V["AB"]), flat(V["AB"]), ACT.Exp, scale=-1.0))
                act.activation(flat(V["AB"]), flat(V["AB"]), ACT.Ln, bias=1.0).then_inc(logs_ready, 1)
                act.wait_ge(mt_ready, 1)
                for t in (s.EI, s.EN, s.WS, s.EA):
                    act.activation(flat(t), flat(t), ACT.Exp).then_inc(exps_ready, 1)

            @block.tensor
            def _(pe):
                pe.wait_ge(lf_ready, 1)
                lf = flat(V["FG"])
                pe.matmul(s.bank[0][:, 0:NCOL], s.tri_le[:, :], lf, start=True, stop=True)
                pe.matmul(s.bank[1][:, 0:NCOL], s.tri_ge[:, :], lf, start=True, stop=True)
                pe.matmul(s.bank[2][:, 0:NCOL], s.ones[:, :], lf, start=True, stop=True).then_inc(sums_done, 1)
                pe.wait_ge(e_ready, 1)
                pe.transpose(s.bank[3][0:NCOL, 0:P], flat(s.E), s.ident[:, :]).then_inc(e_turned, 1)
                pe.wait_ge(scans_ready, 2)
                pe.transpose(s.bank[4][:, 0:NCOL], ET[:, 1, :], s.ident[0:NCOL, 0:NCOL])
                pe.transpose(s.bank[4][:, P:P + NCOL], ET[:, 2, :], s.ident[0:NCOL, 0:NCOL]).then_inc(scans_turned, 1)
                pe.wait_ge(mt_ready, 1)
                pe.transpose(s.bank[5][0:NCOL, 0:P], flat(V["tmp"]), s.ident[:, :]).then_inc(mt_turned, 1)

            @block.gpsimd
            def _(pool):
                pool.wait_ge(e_ready, 1)
                pool.partition_all_reduce(flat(s.EM), flat(s.E), P, bass.bass_isa.ReduceOp.max).then_inc(e_max, 1)


def mixer_inputs(s):
    nc, A = s.nc, s.A
    s.mixer = ExitStack()
    sb = lambda name, shape: s.mixer.enter_context(nc.sbuf_tensor(name, shape, F32))
    s.hcT = sb("hcT", [P, KD, CTX])
    with nc.sbuf_tensor("ctx_tok", [P, NC, D], F32) as ctx_tok:
        ctx_in = sem(s, "ctx_in")
        with nc.Block() as block:
            @block.sync
            def _(sp):
                for t in range(NC):
                    sp.dma_start(ctx_tok[:, t, :], A["ctx"][0, t * P:(t + 1) * P, :]).then_inc(ctx_in, 16)
        stage_norm(s, "norm_c", ctx_tok, NC, s.hcT, lambda k: s.mod[:, 1, k, 1:2], lambda k: s.mod[:, 0, k, 1:2], ctx_in)
    stage_norm(s, "norm_x", s.x, NT, s.hT, lambda k: s.mod[:, 1, k, 0:1], lambda k: s.mod[:, 0, k, 0:1], s.x_in)
    s.gates = sb("gates", [P, STEPS, N_GT])
    s.qkT = sb("qkT", [P, 4, T + CTX])
    s.k_tok = sb("k_tok", [P, STEPS, D_QK])
    s.v_aug = sb("v_aug", [P, STEPS, H1, DV + 1])
    s.sig_o = s.x[:, NT // 2:NT, :].rearrange("p t (a n) -> p (t a) n", a=2)
    s.upad = sb("upad", [P, KC, ROWS, GRID + 2 * PAD])
    stage_project(s)
    s.E, s.EM, s.MX, s.EI, s.EN, s.WS, s.EA = (sb(n, [P, STEPS, 2, H1]) for n in ("E", "EM", "MX", "EI", "EN", "WS", "EA"))
    s.M = sb("M", [P, STEPS + 1, 2, H1])
    s.NMT = sb("NMT", [NCOL, P])


def stage_mlstm(s):
    nc = s.nc
    units = [(j, d, h) for j in range(STEPS) for d in range(2) for h in range(H1)]
    U0 = NC * 2 * H1
    US = (STEPS - 1) * 2 * H1
    NV = len(units) - U0
    CONV = 2 * TAPS
    W = DV + 1
    s.h = s.x[:, 0:NT // 2, :].rearrange("p t (a n) -> p (t a) n", a=2)
    s.y = s.hT[:, KD // 2:KD, :]
    out_unit = lambda v: units[U0 + v]
    tile_of = lambda j, d: bwd_tile(j) if d else fwd_tile(j)
    with nc.sbuf_tensor("neg_mask", [P, 2, P], F32) as neg_mask, \
            nc.sbuf_tensor("dec", [P, 2, P], F32) as dec, nc.sbuf_tensor("pt", [P, 2, P], F32) as pt, \
            nc.sbuf_tensor("wv", [P, 2, W], F32) as wv, nc.sbuf_tensor("c_state", [P, 2, 2, W], F32) as state, \
            nc.sbuf_tensor("inter", [P, 2, W], F32) as inter, nc.sbuf_tensor("hsum", [P, 2, W], F32) as hsum, \
            nc.sbuf_tensor("dn", [P, 2, 2], F32) as dn, nc.sbuf_tensor("diag", [P, 2, P], F32) as diag:
        masks_set, scores_done, dec_ready, exp_ready, pt_ready = (sem(s, f"m_{x}") for x in ("masks_set", "scores_done", "dec_ready", "exp_ready", "pt_ready"))
        wv_ready, local_done, state_moved = (sem(s, f"m_{x}") for x in ("wv_ready", "local_done", "state_moved"))
        num_done, inter_ready, combined = (sem(s, f"m_{x}") for x in ("num_done", "inter_ready", "combined"))
        diag_ready, conv_done, conv_moved = (sem(s, f"m_{x}") for x in ("diag_ready", "conv_done", "conv_moved"))

        def lanes(h):
            return slice((h % 2) * DK, (h % 2) * DK + DK)

        with nc.Block() as block:
            @block.gpsimd
            def _(pool):
                c = s.pool_c
                c.link(pool, pool.memset(neg_mask[:, :, :], 0.0))
                pool.affine_select(out=neg_mask[:, 0, :], in_=neg_mask[:, 0, :], compare_op=ALU.is_ge, fill=NEG,
                                   base=0, pattern=[[1, P]], channel_multiplier=-1).then_inc(masks_set, 1)
                pool.affine_select(out=neg_mask[:, 1, :], in_=neg_mask[:, 1, :], compare_op=ALU.is_ge, fill=NEG,
                                   base=0, pattern=[[-1, P]], channel_multiplier=1).then_inc(masks_set, 1)
                for u, (j, d, h) in enumerate(units):
                    if u < US:
                        if u >= 2:
                            pool.wait_ge(local_done, u - 1)
                        pool.tensor_scalar(wv[:, u % 2, :], s.v_aug[:, tile_of(j, d), h, :], s.WS[:, j, d, h:h + 1],
                                           None, ALU.mult).then_inc(wv_ready, 1)
                    if u < CONV:
                        if u >= 2:
                            pool.wait_ge(conv_done, u - 1)
                        col = (u % TAPS) * KC + 2 + u // TAPS
                        pool.tensor_scalar(diag[:, u % 2, :], s.ident[:, :], s.convw[:, col:col + 1], None,
                                           ALU.mult).then_inc(diag_ready, 1)

            @block.tensor
            def _(pe):
                def scores(v):
                    j, d, h = out_unit(v)
                    t0 = tile_of(j, d) * P
                    if v >= 2:
                        pe.wait_ge(pt_ready, v - 1)
                    bank = s.bank[v % 2]
                    pe.matmul(bank[:, 0:P], s.qkT[lanes(h), 2 + h // 2, t0:t0 + P], s.qkT[lanes(h), h // 2, t0:t0 + P],
                              start=True, stop=True)
                    r = (j * 2 + d) * H1 + h
                    pe.matmul(bank[:, P:2 * P], s.ident[0:NCOL, r:r + 1].to_broadcast([NCOL, P]), s.NMT[:, :],
                              start=True, stop=True).then_inc(scores_done, 1)

                for u, (j, d, h) in enumerate(units):
                    v = u - U0
                    if v == -2:
                        scores(0)
                    if v == -1:
                        scores(1)
                    if u < US:
                        pe.wait_ge(wv_ready, u + 1)
                        if u >= 2:
                            pe.wait_ge(state_moved, u - 1)
                        pe.matmul(s.bank[4 + u % 2][lanes(h), 0:W], s.k_tok[:, tile_of(j, d), h * DK:(h + 1) * DK],
                                  wv[:, u % 2, :], start=True, stop=True).then_inc(local_done, 1)
                    if v >= 0:
                        t0 = tile_of(j, d) * P
                        bank = s.bank[2 + v % 2]
                        if v >= 2:
                            pe.wait_ge(combined, v - 1)
                        pe.wait_ge(state_moved, u - 2 * H1 + 1)
                        pe.matmul(bank[:, 256:256 + W], s.qkT[lanes(h), h // 2, t0:t0 + P], state[lanes(h), d, h // 2, :],
                                  start=True, stop=True)
                        pe.wait_ge(pt_ready, v + 1)
                        pe.matmul(bank[:, 0:W], pt[:, v % 2, :], s.v_aug[:, tile_of(j, d), h, :],
                                  start=True, stop=True).then_inc(num_done, 1)
                        if v + 2 < NV:
                            scores(v + 2)
                    if u < CONV:
                        m, tap = 2 + u // TAPS, u % TAPS
                        pe.wait_ge(diag_ready, u + 1)
                        if u == TAPS:
                            pe.wait_ge(conv_moved, 2)
                        for n in range(2):
                            rows = s.upad[:, m, n * ROWS // 2:(n + 1) * ROWS // 2, tap:tap + GRID]
                            last = pe.matmul(s.bank[6 + n][:, :].rearrange("p (r w) -> p r w", w=GRID), diag[:, u % 2, :], rows,
                                             start=(tap == 0), stop=(tap == TAPS - 1))
                        last.then_inc(conv_done, 1)

            @block.scalar
            def _(act):
                def exp(v):
                    act.wait_ge(dec_ready, v + 1)
                    act.activation(dec[:, v % 2, :], dec[:, v % 2, :], ACT.Exp).then_inc(exp_ready, 1)

                def conv_out(m):
                    act.wait_ge(conv_done, TAPS * (m - 1))
                    bias = s.vec[:, VEC["conv_b"] + m:VEC["conv_b"] + m + 1]
                    for n in range(2):
                        act.activation(s.y[:, m, n * 512:(n + 1) * 512], s.bank[6 + n][:, :], ACT.Identity,
                                       bias=bias).then_inc(conv_moved, 1)

                for u, (j, d, h) in enumerate(units):
                    v = u - U0
                    if 0 <= v + 1 < NV:
                        exp(v + 1)
                    if v >= 0:
                        act.wait_ge(num_done, v + 1)
                        if v >= 2:
                            act.wait_ge(combined, v - 1)
                        act.activation(inter[:, v % 2, :], s.bank[2 + v % 2][:, 256:256 + W], ACT.Copy,
                                       scale=s.EI[:, j, d, h:h + 1]).then_inc(inter_ready, 1)
                    if u in (TAPS - 1, CONV - 1):
                        conv_out(2 + u // TAPS)

            @block.vector
            def _(dve):
                c = s.dve_c
                c.link(dve, dve.memset(state[:, :, :, :], 0.0))
                dve.wait_ge(masks_set, 2)

                def decay(v):
                    j, d, h = out_unit(v)
                    dve.wait_ge(scores_done, v + 1)
                    dve.scalar_tensor_tensor(dec[:, v % 2, :], s.bank[v % 2][:, P:2 * P], s.E[:, j, d, h:h + 1],
                                             neg_mask[:, d, :], ALU.add, ALU.add).then_inc(dec_ready, 1)

                def weights(v):
                    dve.wait_ge(exp_ready, v + 1)
                    if v >= 2:
                        dve.wait_ge(num_done, v - 1)
                    dve.tensor_tensor(pt[:, v % 2, :], s.bank[v % 2][:, 0:P], dec[:, v % 2, :], ALU.mult).then_inc(pt_ready, 1)

                for u, (j, d, h) in enumerate(units):
                    v = u - U0
                    if 0 <= v + 1 < NV:
                        decay(v + 1)
                    if u < CONV:
                        m, tap = u % 2, u // 2
                        w = s.convw[:, tap * KC + m:tap * KC + m + 1]
                        rows = s.upad[:, m, :, tap:tap + GRID]
                        to = s.y[:, m, :].rearrange("p (r w) -> p r w", w=GRID)
                        if tap == 0:
                            c.then(dve.tensor_scalar(to, rows, w, s.vec[:, VEC["conv_b"] + m:VEC["conv_b"] + m + 1],
                                                     ALU.mult, ALU.add))
                        else:
                            c.wait(dve)
                            c.then(dve.scalar_tensor_tensor(to, rows, w, to, ALU.mult, ALU.add))
                    if 0 <= v + 1 < NV:
                        weights(v + 1)
                    if v >= 0:
                        dve.wait_ge(inter_ready, v + 1)
                        H = hsum[:, v % 2, :]
                        dve.tensor_tensor(H, s.bank[2 + v % 2][:, 0:W], inter[:, v % 2, :], ALU.add).then_inc(combined, 1)
                        dve.wait_ge(combined, v + 1)
                        c.link(dve, dve.tensor_scalar(dn[:, v % 2, 0:1], H[:, DV:W], -1.0, s.EN[:, j, d, h:h + 1],
                                                      ALU.mult, ALU.max))
                        c.link(dve, dve.tensor_tensor(dn[:, v % 2, 0:1], dn[:, v % 2, 0:1], H[:, DV:W], ALU.max))
                        c.link(dve, dve.reciprocal(dn[:, v % 2, 1:2], dn[:, v % 2, 0:1]))
                        t = tile_of(j, d)
                        to = s.h[:, t, h * DV:(h + 1) * DV]
                        first = j < (bwd_tile(t) if not d else t + NC)
                        if first:
                            c.then(dve.tensor_scalar(to, H[:, 0:DV], dn[:, v % 2, 1:2], None, ALU.mult))
                        else:
                            c.then(dve.scalar_tensor_tensor(to, H[:, 0:DV], dn[:, v % 2, 1:2], to, ALU.mult, ALU.add))
                    if u < US:
                        dve.wait_ge(local_done, u + 1)
                        C = state[lanes(h), d, h // 2, :]
                        dve.scalar_tensor_tensor(C, C, s.EA[lanes(h), j, d, h:h + 1], s.bank[4 + u % 2][lanes(h), 0:W],
                                                 ALU.mult, ALU.add).then_inc(state_moved, 1)


def stage_mix(s):
    nc, A = s.nc, s.A
    N = 512
    with nc.sbuf_tensor("sqh", [P, NT, D_V], F32) as sqh, nc.sbuf_tensor("norm_g", [P, D_V], F32) as norm_g, \
            nc.sbuf_tensor("hs", [P, NT * H1], F32) as hs, nc.sbuf_tensor("sqy", [P, KC, T], F32) as sqy, \
            nc.sbuf_tensor("rstd_y", [P, T], F32) as rstd_y:
        ng_in, sq_ready, gate_ready, h_inv, h_root = (sem(s, f"x_{x}") for x in ("ng_in", "sq_ready", "gate_ready", "h_inv", "h_root"))
        h_ready, turned, moved_v, moved_a = (sem(s, f"x_{x}") for x in ("h_ready", "turned", "moved_v", "moved_a"))
        mean_done, centred, squared, var_done, y_inv, y_root, y_ready = (sem(s, f"x_{x}") for x in ("mean_done", "centred", "squared", "var_done", "y_inv", "y_root", "y_ready"))
        with nc.Block() as block:
            @block.sync
            def _(sp):
                sp.dma_start(norm_g[:, :], A["mlstm_norm_g"].rearrange("a h v -> a (h v)").to_broadcast([P, D_V])).then_inc(ng_in, 16)

            @block.gpsimd
            def _(pool):
                pool.tensor_tensor(sqh[:, :, :], s.h, s.h, ALU.mult).then_inc(sq_ready, 1)
                pool.wait_ge(ng_in, 16)
                for t in range(NT):
                    pool.tensor_tensor(s.sig_o[:, t, :], s.sig_o[:, t, :], norm_g[:, :], ALU.mult).then_inc(gate_ready, 1)

            @block.tensor
            def _(pe):
                for n in range(2):
                    for m in range(KC):
                        last = pe.matmul(s.bank[n][:, :], s.ones[:, :], s.y[:, m, n * N:(n + 1) * N],
                                         start=(m == 0), stop=(m == KC - 1))
                last.then_inc(mean_done, 1)
                for n in range(2):
                    for m in range(KC):
                        pe.wait_ge(squared, n * KC + m + 1)
                        last = pe.matmul(s.bank[2 + n][:, :], s.ones[:, :], sqy[:, m, n * N:(n + 1) * N],
                                         start=(m == 0), stop=(m == KC - 1))
                    last.then_inc(var_done, 1)
                for i in range(2 * H1):
                    g, k = divmod(i, H1)
                    if k == 0:
                        pe.wait_ge(h_ready, 4 * H1 * (g + 1))
                    if i >= 4:
                        pe.wait_ge((moved_v, moved_a)[i % 2], (i - 4) // 2 + 1)
                    for t in range(4):
                        last = pe.transpose(s.bank[4 + i % 4][:, t * P:(t + 1) * P], s.h[:, g * 4 + t, k * P:(k + 1) * P], s.ident[:, :])
                    last.then_inc(turned, 1)

            @block.vector
            def _(dve):
                c = s.dve_c
                dve.wait_ge(mean_done, 1)
                for n in range(2):
                    for m in range(KC):
                        y = s.y[:, m, n * N:(n + 1) * N]
                        dve.scalar_tensor_tensor(y, s.bank[n][:, :], -1.0 / D_CONV, y, ALU.mult, ALU.add).then_inc(centred, 1)
                dve.wait_ge(sq_ready, 1)
                c.link(dve, dve.tensor_reduce(hs[:, :], sqh[:, :, :].rearrange("p t (h v) -> p (t h) v", h=H1), AX_X, ALU.add))
                c.link(dve, dve.tensor_scalar(hs[:, :], hs[:, :], 1.0 / DV, EPS, ALU.mult, ALU.add))
                dve.reciprocal(hs[:, :], hs[:, :]).then_inc(h_inv, 1)
                dve.wait_ge(var_done, 2)
                for n in range(2):
                    r = rstd_y[:, n * N:(n + 1) * N]
                    c.link(dve, dve.tensor_scalar(r, s.bank[2 + n][:, :], 1.0 / D_CONV, EPS, ALU.mult, ALU.add))
                    dve.reciprocal(r, r).then_inc(y_inv, 1)
                dve.wait_ge(h_root, 1)
                for t in range(NT):
                    dve.wait_ge(gate_ready, t + 1)
                    for h in range(H1):
                        cols = slice(h * DV, (h + 1) * DV)
                        dve.scalar_tensor_tensor(s.h[:, t, cols], s.h[:, t, cols], hs[:, t * H1 + h:t * H1 + h + 1],
                                                 s.sig_o[:, t, cols], ALU.mult, ALU.mult).then_inc(h_ready, 1)
                dve.wait_ge(y_root, 1)
                for n in range(2):
                    for m in range(KC):
                        y = s.y[:, m, n * N:(n + 1) * N]
                        dve.tensor_tensor(y, y, rstd_y[:, n * N:(n + 1) * N], ALU.mult).then_inc(y_ready, 1)
                for i in range(0, 2 * H1, 2):
                    g, k = divmod(i, H1)
                    dve.wait_ge(turned, i + 1)
                    dve.tensor_copy(s.hT[:, k, g * N:(g + 1) * N], s.bank[4 + i % 4][:, :]).then_inc(moved_v, 1)

            @block.scalar
            def _(act):
                for n in range(2):
                    for m in range(KC):
                        act.wait_ge(centred, n * KC + m + 1)
                        act.activation(sqy[:, m, n * N:(n + 1) * N], s.y[:, m, n * N:(n + 1) * N], ACT.Square).then_inc(squared, 1)
                act.wait_ge(h_inv, 1)
                act.activation(hs[:, :], hs[:, :], ACT.Sqrt).then_inc(h_root, 1)
                act.wait_ge(y_inv, 2)
                act.activation(rstd_y[:, :], rstd_y[:, :], ACT.Sqrt).then_inc(y_root, 1)
                for i in range(1, 2 * H1, 2):
                    g, k = divmod(i, H1)
                    act.wait_ge(turned, i + 1)
                    act.activation(s.hT[:, k, g * N:(g + 1) * N], s.bank[4 + i % 4][:, :], ACT.Copy).then_inc(moved_a, 1)
                for n in range(2):
                    for m in range(KC):
                        act.wait_ge(y_ready, n * KC + m + 1)
                        y = s.y[:, m, n * N:(n + 1) * N]
                        g, b = VEC["conv_ln_g"] + m, VEC["conv_ln_b"] + m
                        s.act_c.then(act.activation(y, y, ACT.Silu, scale=s.vec[:, g:g + 1], bias=s.vec[:, b:b + 1]))


def stage_out(s, name, src_T, w_src, post, x_src=None, bias_src=None):
    nc = s.nc
    with nc.sbuf_tensor(f"{name}_w", [P, KD, D], F32) as w, nc.sbuf_tensor(f"{name}_y", [P, NT if post is not None else 1, D], F32) as y, \
            nc.sbuf_tensor(f"{name}_b", [P, D], F32) as b:
        w_in, b_in, x_in = sem(s, f"{name}_w_in"), sem(s, f"{name}_b_in"), sem(s, f"{name}_x_in")
        done, moved = sem(s, f"{name}_done"), sem(s, f"{name}_moved")
        with nc.Block() as block:
            @block.sync
            def _(sp):
                src = w_src.rearrange("(k p) n -> p k n", p=P)
                for k in range(0, KD, 2):
                    sp.dma_start(w[:, k:k + 2, :], src[:, k:k + 2, :]).then_inc(w_in, 16)
                if bias_src is not None:
                    sp.dma_start(b[:, :], bias_src.to_broadcast([P, D])).then_inc(b_in, 16)
                if x_src is not None:
                    for t in range(NT):
                        sp.dma_start(s.x[:, t, :], x_src[t * P:(t + 1) * P, :]).then_inc(x_in, 16)
                    sp.wait_ge(x_in, 16 * NT)

            @block.tensor
            def _(pe):
                pe.wait_ge(w_in, 16 * KD // 2)
                for i in range(2 * NT):
                    t, n = divmod(i, 2)
                    if i >= 8:
                        pe.wait_ge(moved, i - 7)
                    for k in range(KD):
                        last = pe.matmul(s.bank[i % 8][:, :], src_T[:, k, t * P:(t + 1) * P], w[:, k, n * 512:(n + 1) * 512],
                                         start=(k == 0), stop=(k == KD - 1))
                    last.then_inc(done, 1)

            @block.vector
            def _(dve):
                if bias_src is not None:
                    dve.wait_ge(b_in, 16)
                elif x_src is not None:
                    dve.wait_ge(x_in, 16 * NT)
                for i in range(2 * NT):
                    t, n = divmod(i, 2)
                    dve.wait_ge(done, i + 1)
                    cols = slice(n * 512, (n + 1) * 512)
                    other = b[:, cols] if bias_src is not None else s.x[:, t, cols]
                    to = y[:, t, cols] if post is not None else s.x[:, t, cols]
                    dve.tensor_tensor(to, s.bank[i % 8][:, :], other, ALU.add).then_inc(moved, 1)
        if post is not None:
            stage_post(s, name, y, post)


def stage_post(s, name, y, post):
    nc = s.nc
    with nc.sbuf_tensor(f"{name}_psq", [P, 2, D], F32) as sq, nc.sbuf_tensor(f"{name}_pss", [P, NT], F32) as ss:
        summed, inverted, rooted, scaled = (sem(s, f"{name}_p_{x}") for x in ("summed", "inverted", "rooted", "scaled"))
        with nc.Block() as block:
            @block.scalar
            def _(act):
                for t in range(NT):
                    if t >= 2:
                        act.wait_ge(summed, t - 1)
                    act.activation(sq[:, t % 2, :], y[:, t, :], ACT.Square, accum_out=ss[:, t:t + 1]).then_inc(summed, 1)
                act.wait_ge(inverted, 1)
                act.activation(ss[:, :], ss[:, :], ACT.Sqrt).then_inc(rooted, 1)

            @block.vector
            def _(dve):
                dve.wait_ge(summed, NT)
                s.dve_c.link(dve, dve.tensor_scalar(ss[:, :], ss[:, :], 1.0 / D, EPS, ALU.mult, ALU.add))
                dve.reciprocal(ss[:, :], ss[:, :]).then_inc(inverted, 1)
                dve.wait_ge(rooted, 1)
                for t in range(NT):
                    dve.scalar_tensor_tensor(y[:, t, :], y[:, t, :], ss[:, t:t + 1], s.gpost[:, post, :],
                                             ALU.mult, ALU.mult).then_inc(scaled, 1)

            @block.gpsimd
            def _(pool):
                for t in range(NT):
                    pool.wait_ge(scaled, t + 1)
                    s.pool_c.then(pool.tensor_tensor(s.x[:, t, :], s.x[:, t, :], y[:, t, :], ALU.add))


class Moe:

    def __init__(self, s, name, E, K, F):
        self.name, self.E, self.K, self.F = name, E, K, F
        self.NB = T * K // P + E
        nc = s.nc
        self.rows = nc.dram_tensor(f"{name}_rows", (T, D), F32, kind="Internal").ap()
        self.acc = nc.dram_tensor(f"{name}_acc", (T + P, D), F32, kind="Internal").ap()
        self.table = nc.dram_tensor(f"{name}_table", (self.NB * P, 3), F32, kind="Internal").ap()


def stage_route1(s, mo, gate, mask):
    nc, A = s.nc, s.A
    E = mo.E
    with nc.sbuf_tensor("w_router", [P, KD, E], F32) as w, nc.sbuf_tensor("b_router", [P, E], F32) as b, \
            nc.sbuf_tensor("score", [P, NT, E], F32) as score, nc.sbuf_tensor("biased", [P, NT, E], F32) as biased, \
            nc.sbuf_tensor("rest", [P, NT, E], F32) as rest, nc.sbuf_tensor("top", [P, NT, 8], F32) as top, \
            nc.sbuf_tensor("wsum", [P, NT], F32) as wsum:
        w_in, logits_done, scored = sem(s, "r_w_in"), sem(s, "r_logits_done"), sem(s, "r_scored")
        with nc.Block() as block:
            @block.sync
            def _(sp):
                sp.dma_start(w[:, :, :], A["w_router"][0].rearrange("(k p) e -> p k e", p=P)).then_inc(w_in, 16)
                sp.dma_start(b[:, :], A["b_router"][0:1, :].to_broadcast([P, E])).then_inc(w_in, 16)

            @block.tensor
            def _(pe):
                pe.wait_ge(w_in, 32)
                for t in range(NT):
                    for k in range(KD):
                        last = pe.matmul(s.bank[0][:, t * E:(t + 1) * E], s.hT[:, k, t * P:(t + 1) * P], w[:, k, :],
                                         start=(k == 0), stop=(k == KD - 1))
                last.then_inc(logits_done, 1)

            @block.scalar
            def _(act):
                act.wait_ge(logits_done, 1)
                act.activation(score[:, :, :], s.bank[0][:, :].rearrange("p (t e) -> p t e", e=E), ACT.Sigmoid).then_inc(scored, 1)

            @block.vector
            def _(dve):
                c = s.dve_c
                dve.wait_ge(w_in, 32)
                dve.wait_ge(scored, 1)
                for t in range(NT):
                    c.link(dve, dve.tensor_tensor(biased[:, t, :], score[:, t, :], b[:, :], ALU.add))
                    c.link(dve, dve.max(top[:, t, :], biased[:, t, :]))
                    c.then(dve.match_replace(out=rest[:, t, :], in_to_replace=top[:, t, :], in_values=biased[:, t, :], imm_value=NEG))
                c.wait(dve)
                c.link(dve, dve.tensor_tensor(mask[:, :, :], rest[:, :, :], biased[:, :, :], ALU.not_equal))
                c.link(dve, dve.tensor_tensor(gate[:, :, :], score[:, :, :], mask[:, :, :], ALU.mult))
                c.link(dve, dve.tensor_reduce(wsum[:, :], gate[:, :, :], AX_X, ALU.add))
                c.link(dve, dve.reciprocal(wsum[:, :], wsum[:, :]))
                for t in range(NT):
                    c.then(dve.tensor_scalar(gate[:, t, :], gate[:, t, :], wsum[:, t:t + 1], ROUTE_SCALE, ALU.mult, ALU.mult))
                c.wait(dve)


def stage_dispatch(s, mo, gate, mask, start, idx_g, idx_s, row_w):
    nc = s.nc
    E, K, NB, name = mo.E, mo.K, mo.NB, mo.name
    with nc.sbuf_tensor(f"{name}_key", [P, NT, E], F32) as key, nc.sbuf_tensor(f"{name}_blocks", [P, E], F32) as blocks, \
            nc.sbuf_tensor(f"{name}_count", [P, E], F32) as count, nc.sbuf_tensor(f"{name}_ends", [P, E + 1], F32) as ends, \
            nc.sbuf_tensor(f"{name}_base", [P, E], F32) as base, nc.sbuf_tensor(f"{name}_keys", [P, NT, 8], F32) as keys, \
            nc.sbuf_tensor(f"{name}_dest", [P, NT, K], I32) as dest, nc.sbuf_tensor(f"{name}_pair", [P, NT, K, 3], F32) as pair, \
            nc.sbuf_tensor(f"{name}_hit", [P, E], F32) as hit, nc.sbuf_tensor(f"{name}_tok_i", [P, NT], I32) as tok_i, \
            nc.sbuf_tensor(f"{name}_empty_i", [P, P], I32) as empty_i, nc.sbuf_tensor(f"{name}_empty", [P, P, 3], F32) as empty, \
            nc.sbuf_tensor(f"{name}_back", [P, P, 3], F32) as back:
        ranks_done, keys_ready, empty_ready, table_set = (sem(s, f"{name}_{x}") for x in ("ranks_done", "keys_ready", "empty_ready", "table_set"))
        scattered, read_back, turned, iotas = (sem(s, f"{name}_{x}") for x in ("scattered", "read_back", "tab_turned", "iotas"))
        with nc.Block() as block:
            @block.gpsimd
            def _(pool):
                pool.iota(tok_i[:, :], pattern=[[P, NT]], base=0, channel_multiplier=1).then_inc(iotas, 1)
                pool.iota(empty_i[:, :], pattern=[[1, P]], base=T, channel_multiplier=0).then_inc(iotas, 1)
                pool.wait_ge(table_set, 16)
                pool.wait_ge(keys_ready, 1)
                for t in range(NT):
                    for k in range(K):
                        pool.indirect_dma_start(mo.table, bass.IndirectOffsetOnAxis(ap=dest[:, t, k:k + 1], axis=0),
                                                pair[:, t, k, :], None, bounds_check=NB * P - 1).then_inc(scattered, 16)

            @block.sync
            def _(sp):
                sp.wait_ge(empty_ready, 1)
                sp.dma_start(mo.table.rearrange("(b s) c -> b (s c)", s=P),
                             empty[0:NB, :, :].rearrange("b s c -> b (s c)")).then_inc(table_set, 16)
                sp.wait_ge(scattered, 16 * NT * K)
                sp.dma_start(back[0:NB, :, :].rearrange("b s c -> b (s c)"),
                             mo.table.rearrange("(b s) c -> b (s c)", s=P)).then_inc(read_back, 16)

            @block.tensor
            def _(pe):
                for t in range(NT):
                    for u in range(t):
                        pe.matmul(s.bank[0][:, t * E:(t + 1) * E], s.ones[:, :], mask[:, u, :], start=(u == 0), stop=False)
                    pe.matmul(s.bank[0][:, t * E:(t + 1) * E], s.tri_le[:, :], mask[:, t, :], start=(t == 0), stop=True)
                for t in range(NT):
                    last = pe.matmul(s.bank[1][:, 0:E], s.ones[:, :], mask[:, t, :], start=(t == 0), stop=(t == NT - 1))
                last.then_inc(ranks_done, 1)
                pe.wait_ge(read_back, 16)
                for c in range(3):
                    last = pe.transpose(s.bank[2][:, c * P:c * P + NB], back[0:NB, :, c], s.ident[0:NB, 0:NB])
                last.then_inc(turned, 1)

            @block.vector
            def _(dve):
                c = s.dve_c
                dve.wait_ge(iotas, 2)
                c.then(dve.memset(empty[:, :, 0:3:2], 0.0))
                for col in range(2):
                    for k in range(K):
                        c.then(dve.tensor_copy(pair[:, :, k, col], tok_i[:, :]))
                c.wait(dve)
                dve.tensor_copy(empty[:, :, 1], empty_i[:, :]).then_inc(empty_ready, 1)
                dve.wait_ge(ranks_done, 1)
                c.then(dve.memset(ends[:, 0:1], 0.0))
                c.then(dve.memset(blocks[:, :], 1.0))
                c.link(dve, dve.tensor_copy(count[:, :], s.bank[1][:, 0:E]))
                for j in range(1, NT):
                    c.link(dve, dve.scalar_tensor_tensor(blocks[:, :], count[:, :], float(j * P), blocks[:, :], ALU.is_gt, ALU.add))
                c.link(dve, dve.tensor_tensor_scan(ends[:, 1:E + 1], s.ones[:, 0:E], blocks[:, :], 0.0, ALU.mult, ALU.add))
                c.then(dve.tensor_copy(start[:, :], ends[:, :]))
                c.link(dve, dve.tensor_scalar(base[:, :], ends[:, 0:E], float(P), None, ALU.mult))
                for t in range(NT):
                    c.link(dve, dve.tensor_tensor(key[:, t, :], s.bank[0][:, t * E:(t + 1) * E], base[:, :], ALU.add))
                    c.link(dve, dve.tensor_tensor(key[:, t, :], key[:, t, :], mask[:, t, :], ALU.mult))
                    c.link(dve, dve.max(keys[:, t, :], key[:, t, :]))
                    c.then(dve.tensor_scalar(dest[:, t, :], keys[:, t, 0:K], -1.0, None, ALU.add))
                    for k in range(K):
                        c.link(dve, dve.scalar_tensor_tensor(hit[:, :], key[:, t, :], keys[:, t, k:k + 1], gate[:, t, :],
                                                             ALU.is_equal, ALU.mult, accum_out=pair[:, t, k, 2:3]))
                c.wait(dve)
                dve.sem_inc(keys_ready, 1)
                dve.wait_ge(turned, 1)
                c.then(dve.memset(idx_g[:, NB:NB + 2], 0))
                c.then(dve.tensor_copy(idx_g[:, 0:NB], s.bank[2][:, 0:NB]))
                c.then(dve.tensor_copy(idx_s[:, :], s.bank[2][:, P:P + NB]))
                c.then(dve.tensor_copy(row_w[:, :], s.bank[2][:, 2 * P:2 * P + NB]))
                c.wait(dve)


def stage_experts(s, mo, start, idx_g, idx_s, row_w, wg, wu, wd, gain, shift):
    nc = s.nc
    E, F, NB, name = mo.E, mo.F, mo.NB, mo.name
    KF = F // P
    with nc.sbuf_tensor(f"{name}_wg", [P, 2, KD, F], F32) as wg_sb, nc.sbuf_tensor(f"{name}_wu", [P, 2, KD, F], F32) as wu_sb, \
            nc.sbuf_tensor(f"{name}_wd", [P, 2, KF, D], F32) as wd_sb, nc.sbuf_tensor(f"{name}_xg", [P, D], F32) as xg, \
            nc.sbuf_tensor(f"{name}_xgT", [P, KD, P], F32) as xgT, nc.sbuf_tensor(f"{name}_silu", [P, KF, P], F32) as silu, \
            nc.sbuf_tensor(f"{name}_hidT", [P, KF, P], F32) as hidT, nc.sbuf_tensor(f"{name}_y_blk", [P, D], F32) as y_blk, \
            nc.sbuf_tensor(f"{name}_ig_now", [P, 1], I32) as ig_now, nc.sbuf_tensor(f"{name}_is_now", [P, 1], I32) as is_now:
        w_ready = [sem(s, f"{name}_w_ready{b}") for b in range(2)]
        gathered, turned, xt_ready_v, xt_ready_a = (sem(s, f"{name}_{x}") for x in ("gathered", "turned", "xt_ready_v", "xt_ready_a"))
        gu_done, silu_ready, hid_ready, down_done = (sem(s, f"{name}_{x}") for x in ("gu_done", "silu_ready", "hid_ready", "down_done"))
        y_ready_v, y_ready_a, added, ig_set, is_set, ig_seen, y_zero = (sem(s, f"{name}_{x}") for x in ("y_ready_v", "y_ready_a", "added", "ig_set", "is_set", "ig_seen", "y_zero"))
        HEAD = 1
        N_LOAD = 5
        bx = [s.bank[0], s.bank[1]]
        bg, bu = s.bank[2:4], s.bank[4:6]
        by = s.bank[6:8]

        def first_block(eng, e):
            return eng.value_load(start[0:1, bass.ds(e, 1)], min_val=0, max_val=NB)

        def blocks_of(eng, e, body):
            lo = first_block(eng, e)
            hi = first_block(eng, e + 1)
            with eng.Fori(lo, hi) as g:
                body(g)

        with nc.Block() as block:
            @block.sync
            def _(sp):
                def load(e, b):
                    for k in range(0, KD, 4):
                        sp.dma_start(wg_sb[:, b, k:k + 4, :], wg[bass.ds(e, 1), k * P:(k + 4) * P, :].rearrange("o (k p) f -> p (o k) f", p=P)).then_inc(w_ready[b], 16)
                        sp.dma_start(wu_sb[:, b, k:k + 4, :], wu[bass.ds(e, 1), k * P:(k + 4) * P, :].rearrange("o (k p) f -> p (o k) f", p=P)).then_inc(w_ready[b], 16)
                    sp.dma_start(wd_sb[:, b, :, :], wd[bass.ds(e, 1), :, :].rearrange("o (k p) d -> p (o k) d", p=P)).then_inc(w_ready[b], 16)
                for b in range(2):
                    load(b, b)
                with sp.Fori(1, E // 2) as ep:
                    for b in range(2):
                        sp.wait_ge(down_done, first_block(sp, 2 * ep + b - 1) + HEAD)
                        load(2 * ep + b, b)

            @block.gpsimd
            def _(pool):
                def gather(g):
                    pool.tensor_copy(ig_now[:, :], idx_g[:, bass.ds(g, 1)]).then_inc(ig_set, 1)
                    pool.wait_ge(ig_set, g + 1)
                    pool.sem_inc(ig_seen, 1)
                    pool.indirect_dma_start(xg[:, :], None, mo.rows, bass.IndirectOffsetOnAxis(ap=ig_now[:, 0:1], axis=0)).then_inc(gathered, 16)

                def follow(g):
                    pool.wait_ge(turned, g + 1)
                    pool.wait_ge(gathered, 16 * (g + 1))
                    gather(g + 1)

                def one(g):
                    follow(g + 1)
                    pool.wait_ge(added, 16 * (g + 1))
                    pool.tensor_copy(is_now[:, :], idx_s[:, bass.ds(g, 1)]).then_inc(is_set, 1)
                    pool.wait_ge(is_set, 1)
                    pool.wait_ge(is_set, g + 1)
                    pool.wait_ge(y_ready_v, g + 1 + HEAD)
                    pool.wait_ge(y_ready_a, g + 1 + HEAD)
                    pool.indirect_dma_start(mo.acc, bass.IndirectOffsetOnAxis(ap=is_now[:, 0:1], axis=0), y_blk[:, :], None,
                                            compute_op=ALU.add).then_inc(added, 16)

                pool.memset(y_blk[:, :], 0.0).then_inc(y_zero, 1)
                pool.wait_ge(y_zero, 1)
                pool.dma_start(mo.acc[T:T + P, :], y_blk[:, :]).then_inc(added, 16)
                gather(0)
                follow(0)
                with pool.Fori(0, E) as e:
                    blocks_of(pool, e, one)
                end = first_block(pool, E)
                pool.wait_ge(gathered, 16 * (end + 2))
                pool.wait_ge(added, 16 * (end + 1))

            @block.tensor
            def _(pe):
                for counter in (gu_done, down_done):
                    pe.sem_inc(counter, HEAD)

                def turn(g):
                    pe.wait_ge(gathered, 16 * (g + 1))
                    pe.wait_ge(xt_ready_v, 4 * g + HEAD)
                    pe.wait_ge(xt_ready_a, 4 * g + HEAD)
                    for k in range(KD):
                        last = pe.transpose(bx[k % 2][:, (k // 2) * P:(k // 2 + 1) * P], xg[:, k * P:(k + 1) * P], s.ident[:, :])
                    last.then_inc(turned, 1)

                def one(g, b, ep):
                    pe.wait_ge(w_ready[b], 16 * N_LOAD * (ep + 1))
                    pe.wait_ge(xt_ready_v, 4 * (g + 1) + HEAD)
                    pe.wait_ge(xt_ready_a, 4 * (g + 1) + HEAD)
                    for f in range(KF):
                        pe.wait_ge(hid_ready, KF * g + HEAD)
                        for w, to in ((wg_sb, bg[f]), (wu_sb, bu[f])):
                            for k in range(KD):
                                last = pe.matmul(to[:, 0:P], w[:, b, k, f * P:(f + 1) * P], xgT[:, k, :],
                                                 start=(k == 0), stop=(k == KD - 1))
                            last.then_inc(gu_done, 1)
                    turn(g + 1)
                    pe.wait_ge(hid_ready, KF * (g + 1) + HEAD)
                    pe.wait_ge(y_ready_v, g + HEAD)
                    pe.wait_ge(y_ready_a, g + HEAD)
                    for n in range(2):
                        for f in range(KF):
                            last = pe.matmul(by[n][:, :], hidT[:, f, :], wd_sb[:, b, f, n * 512:(n + 1) * 512],
                                             start=(f == 0), stop=(f == KF - 1))
                    last.then_inc(down_done, 1)

                turn(0)
                with pe.Fori(0, E // 2) as ep:
                    for b in range(2):
                        blocks_of(pe, 2 * ep + b, lambda g, b=b: one(g, b, ep))

            @block.scalar
            def _(act):
                for counter in (xt_ready_a, y_ready_a):
                    act.sem_inc(counter, HEAD)

                def take(g):
                    act.wait_ge(turned, g + 1)
                    act.wait_ge(gu_done, 2 * KF * g + HEAD)
                    for k in range(1, KD, 2):
                        act.activation(xgT[:, k, :], bx[1][:, (k // 2) * P:(k // 2 + 1) * P], ACT.Identity, scale=gain(k),
                                       bias=shift(k) if shift else 0.0).then_inc(xt_ready_a, 1)

                def one(g):
                    for f in range(KF):
                        act.wait_ge(gu_done, 2 * KF * g + 2 * f + 1 + HEAD)
                        act.wait_ge(hid_ready, KF * g + HEAD)
                        act.activation(silu[:, f, :], bg[f][:, 0:P], ACT.Silu).then_inc(silu_ready, 1)
                    take(g + 1)
                    act.wait_ge(down_done, g + 1 + HEAD)
                    act.wait_ge(added, 16 * (g + 1))
                    act.activation(y_blk[:, 512:D], by[1][:, :], ACT.Copy, scale=row_w[:, bass.ds(g, 1)]).then_inc(y_ready_a, 1)

                take(0)
                with act.Fori(0, E) as e:
                    blocks_of(act, e, one)

            @block.vector
            def _(dve):
                for counter in (xt_ready_v, y_ready_v, hid_ready):
                    dve.sem_inc(counter, HEAD)

                def take(g):
                    dve.wait_ge(turned, g + 1)
                    dve.wait_ge(gu_done, 2 * KF * g + HEAD)
                    for k in range(0, KD, 2):
                        of = bx[0][:, (k // 2) * P:(k // 2 + 1) * P]
                        if shift:
                            dve.tensor_scalar(xgT[:, k, :], of, gain(k), shift(k), ALU.mult, ALU.add).then_inc(xt_ready_v, 1)
                        else:
                            dve.tensor_scalar(xgT[:, k, :], of, gain(k), None, ALU.mult).then_inc(xt_ready_v, 1)

                def one(g):
                    for f in range(KF):
                        dve.wait_ge(gu_done, 2 * KF * g + 2 * f + 2 + HEAD)
                        dve.wait_ge(silu_ready, KF * g + f + 1)
                        dve.wait_ge(down_done, g + HEAD)
                        dve.tensor_tensor(hidT[:, f, :], bu[f][:, 0:P], silu[:, f, :], ALU.mult).then_inc(hid_ready, 1)
                    take(g + 1)
                    dve.wait_ge(down_done, g + 1 + HEAD)
                    dve.wait_ge(added, 16 * (g + 1))
                    dve.tensor_scalar(y_blk[:, 0:512], by[0][:, :], row_w[:, bass.ds(g, 1)], None, ALU.mult).then_inc(y_ready_v, 1)

                take(0)
                with dve.Fori(0, E) as e:
                    blocks_of(dve, e, one)


def stage_shared(s, mo):
    nc, A = s.nc, s.A
    F = F1
    KF = F // P
    with nc.sbuf_tensor("ws", [P, 2, KD, F], F32) as ws, nc.sbuf_tensor("wsd", [P, KF, D], F32) as wsd, \
            nc.sbuf_tensor("sh_silu", [P, 2, 512], F32) as silu, nc.sbuf_tensor("sh_hid", [P, KF, T], F32) as hid, \
            nc.sbuf_tensor("sh_y", [P, NT, D], F32) as y:
        w_in, gu_done, silu_ready, hid_ready, down_done, moved, stored = (
            sem(s, f"sh_{x}") for x in ("w_in", "gu_done", "silu_ready", "hid_ready", "down_done", "moved", "stored"))
        with nc.Block() as block:
            @block.sync
            def _(sp):
                for i, n in enumerate(("ws_gate", "ws_up")):
                    src = A[n][0].rearrange("(k p) f -> p k f", p=P)
                    for k in range(0, KD, 4):
                        sp.dma_start(ws[:, i, k:k + 4, :], src[:, k:k + 4, :]).then_inc(w_in, 16)
                sp.dma_start(wsd[:, :, :], A["ws_down"][0].rearrange("(k p) d -> p k d", p=P)).then_inc(w_in, 16)
                for t in range(NT):
                    sp.wait_ge(moved, 2 * (t + 1))
                    sp.dma_start(mo.acc[t * P:(t + 1) * P, :], y[:, t, :]).then_inc(stored, 16)
                sp.wait_ge(stored, 16 * NT)

            @block.tensor
            def _(pe):
                pe.wait_ge(w_in, 80)
                for i in range(2 * KF):
                    n, f = divmod(i, KF)
                    if i >= 2:
                        pe.wait_ge(hid_ready, i - 1)
                    for g in range(2):
                        for k in range(KD):
                            last = pe.matmul(s.bank[2 * (i % 2) + g][:, :], ws[:, g, k, f * P:(f + 1) * P], s.hT[:, k, n * 512:(n + 1) * 512],
                                             start=(k == 0), stop=(k == KD - 1))
                        last.then_inc(gu_done, 1)
                for i in range(2 * NT):
                    t, n = divmod(i, 2)
                    if t % 4 == 0:
                        pe.wait_ge(hid_ready, KF * (t // 4 + 1))
                    if i >= 4:
                        pe.wait_ge(moved, i - 3)
                    for f in range(KF):
                        last = pe.matmul(s.bank[4 + i % 4][:, :], hid[:, f, t * P:(t + 1) * P], wsd[:, f, n * 512:(n + 1) * 512],
                                         start=(f == 0), stop=(f == KF - 1))
                    last.then_inc(down_done, 1)

            @block.scalar
            def _(act):
                for i in range(2 * KF):
                    act.wait_ge(gu_done, 2 * i + 1)
                    if i >= 2:
                        act.wait_ge(hid_ready, i - 1)
                    act.activation(silu[:, i % 2, :], s.bank[2 * (i % 2)][:, :], ACT.Silu).then_inc(silu_ready, 1)

            @block.vector
            def _(dve):
                for i in range(2 * KF):
                    n, f = divmod(i, KF)
                    dve.wait_ge(gu_done, 2 * i + 2)
                    dve.wait_ge(silu_ready, i + 1)
                    dve.tensor_tensor(hid[:, f, n * 512:(n + 1) * 512], s.bank[2 * (i % 2) + 1][:, :], silu[:, i % 2, :],
                                      ALU.mult).then_inc(hid_ready, 1)
                for i in range(2 * NT):
                    t, n = divmod(i, 2)
                    dve.wait_ge(down_done, i + 1)
                    dve.tensor_copy(y[:, t, n * 512:(n + 1) * 512], s.bank[4 + i % 4][:, :]).then_inc(moved, 1)


def ffn1(s):
    nc, A = s.nc, s.A
    mo = Moe(s, "moe1", E1, TOP1, F1)
    gain, shift = (lambda k: s.mod[:, 3, k, 0:1]), (lambda k: s.mod[:, 2, k, 0:1])
    stage_norm(s, "norm_f", s.x, NT, s.hT, gain, shift, rows_to=mo.rows)
    stage_shared(s, mo)
    with ExitStack() as tables:
        tab = lambda name, shape, dt: tables.enter_context(nc.sbuf_tensor(name, shape, dt))
        start = tab("start1", [P, mo.E + 1], I32)
        idx_g, idx_s = tab("idx_g1", [P, mo.NB + 2], I32), tab("idx_s1", [P, mo.NB], I32)
        row_w = tab("row_w1", [P, mo.NB], F32)
        with nc.sbuf_tensor("gate1", [P, NT, mo.E], F32) as gate, nc.sbuf_tensor("mask1", [P, NT, mo.E], F32) as mask:
            stage_route1(s, mo, gate, mask)
            stage_dispatch(s, mo, gate, mask, start, idx_g, idx_s, row_w)
        stage_experts(s, mo, start, idx_g, idx_s, row_w, A["we_gate"][0], A["we_up"][0], A["we_down"][0], gain, shift)
    with nc.sbuf_tensor("acc_tok", [P, NT, D], F32) as acc:
        acc_in = sem(s, "acc1_in")
        with nc.Block() as block:
            @block.sync
            def _(sp):
                for t in range(NT):
                    sp.dma_start(acc[:, t, :], mo.acc[t * P:(t + 1) * P, :]).then_inc(acc_in, 16)
                sp.wait_ge(acc_in, 16 * NT)
        stage_post(s, "post_f", acc, 1)


H2, HD = 8, 64
D_A = H2 * HD
C2_U, C2_GATE = 3 * D_A, 3 * D_A + 512
CHUNK2 = 64
BACK = 8 * CHUNK2
KEYS = BACK + P
FUTURE, MAX_REL = CHUNK2 - 1, 256
N_REL = FUTURE + MAX_REL + 1
REXT = P - 1 + KEYS
GRP, SG, SP_ = 32, 16, 64
GG = GRP // 2
L2 = 8
NCH = T // L2
NG2, EPG, E2, TOP2, F2 = 4, 4, 16, 2, 256
BIG = 3.0e38
TWO_PI = (6.28125, 0.0019350051879882812, 3.019916050561733e-07)
ROUND = 12582912.0


def stage_qkv(s, qT, kT, v_tok, q_tok, k_tok):
    nc, A = s.nc, s.A
    w_src = A["w_in_2"][0].rearrange("(k p) n -> p k n", p=P)
    toks = (q_tok, k_tok, v_tok)
    with nc.sbuf_tensor("w2_ring", [P, 2, KD, 512], F32) as ring, nc.sbuf_tensor("qk_ss", [P, 2, NT * H2], F32) as ss:
        w_ready = [sem(s, f"a_w{i}") for i in range(3)]
        done, copied_v, copied_a, squared, inverted, rooted = (sem(s, f"a_{x}") for x in ("done", "copied_v", "copied_a", "squared", "inverted", "rooted"))
        normed, turned, moved_v, moved_a = (sem(s, f"a_{x}") for x in ("normed", "turned", "moved_v", "moved_a"))
        sq = (qT, kT)
        flat = lambda x: x[:, :, :].rearrange("p a b -> p (a b)")
        with nc.Block() as block:
            @block.sync
            def _(sp):
                for i in range(3):
                    if i == 2:
                        sp.wait_ge(done, NT)
                    for k in range(0, KD, 4):
                        sp.dma_start(ring[:, i % 2, k:k + 4, :], w_src[:, k:k + 4, i * 512:(i + 1) * 512]).then_inc(w_ready[i], 16)

            @block.tensor
            def _(pe):
                for i in range(3 * NT):
                    g, t = divmod(i, NT)
                    if t == 0:
                        pe.wait_ge(w_ready[g], 32)
                    if i >= 4:
                        pe.wait_ge((copied_v, copied_a)[i % 2], (i - 4) // 2 + 1)
                    for k in range(KD):
                        last = pe.matmul(s.bank[i % 4], s.hT[:, k, t * P:(t + 1) * P], ring[:, g % 2, k, :],
                                         start=(k == 0), stop=(k == KD - 1))
                    last.then_inc(done, 1)
                for i in range(16):
                    g, m, n = i // 8, (i % 8) // 2, i % 2
                    if i % 8 == 0:
                        pe.wait_ge(normed, g + 1)
                    if i >= 4:
                        pe.wait_ge((moved_v, moved_a)[i % 2], (i - 4) // 2 + 1)
                    for t in range(4):
                        last = pe.transpose(s.bank[4 + i % 4][:, t * P:(t + 1) * P], toks[g][:, n * 4 + t, m * P:(m + 1) * P], s.ident[:, :])
                    last.then_inc(turned, 1)

            @block.gpsimd
            def _(pool):
                for g in range(2):
                    pool.wait_ge(copied_v, NT // 2 * (g + 1))
                    pool.wait_ge(copied_a, NT // 2 * (g + 1))
                    pool.tensor_tensor(flat(sq[g]), flat(toks[g]), flat(toks[g]), ALU.mult).then_inc(squared, 1)

            @block.vector
            def _(dve):
                c = s.dve_c

                def copies(g):
                    for t in range(0, NT, 2):
                        dve.wait_ge(done, g * NT + t + 1)
                        dve.tensor_copy(toks[g][:, t, :], s.bank[(g * NT + t) % 4]).then_inc(copied_v, 1)

                def norms(g):
                    dve.wait_ge(squared, g + 1)
                    c.link(dve, dve.tensor_reduce(ss[:, g, :], flat(sq[g]).rearrange("p (a e) -> p a e", e=HD), AX_X, ALU.add))
                    c.link(dve, dve.tensor_scalar(ss[:, g, :], ss[:, g, :], 1.0 / HD, EPS, ALU.mult, ALU.add))
                    dve.reciprocal(ss[:, g, :], ss[:, g, :]).then_inc(inverted, 1)
                    dve.wait_ge(rooted, g + 1)
                    x = flat(toks[g]).rearrange("p (a e) -> p a e", e=HD)
                    r = ss[:, g, :].rearrange("p (a o) -> p a o", o=1).to_broadcast([P, NT * H2, HD])
                    dve.tensor_tensor(x, x, r, ALU.mult).then_inc(normed, 1)

                copies(0)
                copies(1)
                norms(0)
                copies(2)
                norms(1)
                for i in range(0, 16, 2):
                    g, m, n = i // 8, (i % 8) // 2, i % 2
                    dve.wait_ge(turned, i + 1)
                    dve.tensor_scalar((qT, kT)[g][:, m, n * 512:(n + 1) * 512], s.bank[4 + i % 4], s.vec2[:, 16 + g:17 + g],
                                      HD ** -0.5 if g == 0 else 1.0, ALU.mult, ALU.mult).then_inc(moved_v, 1)

            @block.scalar
            def _(act):
                def copies(g):
                    for t in range(1, NT, 2):
                        act.wait_ge(done, g * NT + t + 1)
                        act.activation(toks[g][:, t, :], s.bank[(g * NT + t) % 4], ACT.Copy).then_inc(copied_a, 1)

                copies(0)
                copies(1)
                act.wait_ge(inverted, 1)
                act.activation(ss[:, 0, :], ss[:, 0, :], ACT.Sqrt).then_inc(rooted, 1)
                copies(2)
                act.wait_ge(inverted, 2)
                act.activation(ss[:, 1, :], ss[:, 1, :], ACT.Sqrt).then_inc(rooted, 1)
                act.activation(s.gain_q[:, :], s.vec2[:, 16:17], ACT.Copy, scale=HD ** -0.5).then_inc(s.gain_q_set, 1)
                act.wait_ge(s.gain_q_set, 1)
                for i in range(1, 16, 2):
                    g, m, n = i // 8, (i % 8) // 2, i % 2
                    act.wait_ge(turned, i + 1)
                    act.activation((qT, kT)[g][:, m, n * 512:(n + 1) * 512], s.bank[4 + i % 4], ACT.Copy,
                                   scale=s.gain_q[:, :] if g == 0 else s.vec2[:, 17:18]).then_inc(moved_a, 1)


def stage_bias(s, bias):
    nc, A = s.nc, s.A
    rext = nc.dram_tensor("rel_ext", (H2, REXT + 1), F32, kind="Internal")
    with nc.sbuf_tensor("rext", [H2, REXT + 1], F32) as row:
        rel_in, ext_ready, stored, loaded = (sem(s, f"b_{x}") for x in ("rel_in", "ext_ready", "stored", "loaded"))
        lo = P - 1 - FUTURE
        with nc.Block() as block:
            @block.sync
            def _(sp):
                sp.dma_start(row[:, lo:lo + N_REL], A["rel_bias_2"][0]).then_inc(rel_in, 16)
                sp.wait_ge(ext_ready, 2)
                sp.dma_start(rext.ap(), row[:, :]).then_inc(stored, 16)
                sp.wait_ge(stored, 16)
                src = rext.ap()
                for h in range(H2):
                    view = bass.AP(src.tensor, h * (REXT + 1), [[1, P], [1, KEYS]])
                    sp.dma_start(bias[:, h, :], view).then_inc(loaded, 16)

            @block.vector
            def _(dve):
                dve.wait_ge(rel_in, 16)
                dve.tensor_copy(row[:, 0:lo], row[:, lo:lo + 1].to_broadcast([H2, lo])).then_inc(ext_ready, 1)
                hi = lo + N_REL
                dve.tensor_copy(row[:, hi:REXT + 1], row[:, hi - 1:hi].to_broadcast([H2, REXT + 1 - hi])).then_inc(ext_ready, 1)
                dve.wait_ge(loaded, 16 * H2)
                s.dve_c.then(dve.memset(bias[0:CHUNK2, :, 0:CHUNK2], NEG))
                s.dve_c.then(dve.memset(bias[CHUNK2:P, :, KEYS - CHUNK2:KEYS], NEG))


def stage_attention(s, qT, kT, v_tok, bias, y_tok, yT):
    nc = s.nc
    units = [(i, h) for i in range(NT) for h in range(H2)]
    NU = len(units)
    with nc.sbuf_tensor("lg", [P, 2, KEYS], F32) as lg, nc.sbuf_tensor("pr", [P, 2, KEYS], F32) as pr, \
            nc.sbuf_tensor("prT", [P, 2, KEYS], F32) as prT, nc.sbuf_tensor("mx", [P, 2, 4], F32) as mx:
        scored, biased, maxed, exped, turned, moved, attended, taken = (sem(s, f"t_{x}") for x in ("scored", "biased", "maxed", "exped", "turned", "moved", "attended", "taken"))
        y_turned, y_moved = sem(s, "t_y_turned"), sem(s, "t_y_moved")

        def span(i):
            n = min(i + 1, KEYS // P) * P
            return n, (i + 1) * P - n

        with nc.Block() as block:
            @block.tensor
            def _(pe):
                def score(u):
                    i, h = units[u]
                    n, k0 = span(i)
                    lanes = slice((h % 2) * HD, (h % 2) * HD + HD)
                    if u >= 2:
                        pe.wait_ge(biased, u - 1)
                    for a in range(0, n, 512):
                        w = min(512, n - a)
                        last = pe.matmul(s.bank[2 * (u % 2) + a // 512][:, 0:w], qT[lanes, h // 2, i * P:(i + 1) * P],
                                         kT[lanes, h // 2, k0 + a:k0 + a + w], start=True, stop=True)
                    last.then_inc(scored, 1)

                score(0)
                score(1)
                for u, (i, h) in enumerate(units):
                    n, k0 = span(i)
                    pe.wait_ge(exped, u + 1)
                    if u >= 1:
                        pe.wait_ge(moved, u)
                    for a in range(n // P):
                        last = pe.transpose(s.psum[:, 4 * 512 + a * P:4 * 512 + (a + 1) * P], pr[:, u % 2, a * P:(a + 1) * P], s.ident[:, :])
                    last.then_inc(turned, 1)
                    if u + 2 < NU:
                        score(u + 2)
                    pe.wait_ge(moved, u + 1)
                    if u >= 2:
                        pe.wait_ge(taken, u - 1)
                    for a in range(n // P):
                        last = pe.matmul(s.bank[6 + u % 2][:, 0:HD], prT[:, u % 2, a * P:(a + 1) * P], v_tok[:, k0 // P + a, h * HD:(h + 1) * HD],
                                         start=(a == 0), stop=(a == n // P - 1))
                    last.then_inc(attended, 1)
                pe.wait_ge(taken, NU)
                for i in range(8):
                    m, n = divmod(i, 2)
                    if i >= 4:
                        pe.wait_ge(y_moved, i - 3)
                    for t in range(4):
                        last = pe.transpose(s.bank[i % 4][:, t * P:(t + 1) * P], y_tok[:, n * 4 + t, m * P:(m + 1) * P], s.ident[:, :])
                    last.then_inc(y_turned, 1)

            @block.vector
            def _(dve):
                c = s.dve_c

                def logits(u):
                    i, h = units[u]
                    n, _ = span(i)
                    dve.wait_ge(scored, u + 1)
                    if u >= 2:
                        dve.wait_ge(exped, u - 1)
                    b = bias[:, h, 0:n][:, ::-1]
                    o = 1024 * (u % 2)
                    dve.tensor_tensor(lg[:, u % 2, 0:n], s.psum[:, o:o + n], b, ALU.add).then_inc(biased, 1)
                    dve.wait_ge(biased, u + 1)
                    dve.tensor_reduce(mx[:, u % 2, 0:1], lg[:, u % 2, 0:n], AX_X, ALU.max, negate=True).then_inc(maxed, 1)

                logits(0)
                for u, (i, h) in enumerate(units):
                    if u + 1 < NU:
                        logits(u + 1)
                    dve.wait_ge(exped, u + 1)
                    c.link(dve, dve.reciprocal(mx[:, u % 2, 2:3], mx[:, u % 2, 1:2]))
                    dve.wait_ge(attended, u + 1)
                    dve.tensor_scalar(y_tok[:, i, h * HD:(h + 1) * HD], s.bank[6 + u % 2][:, 0:HD], mx[:, u % 2, 2:3], None,
                                      ALU.mult).then_inc(taken, 1)
                for i in range(8):
                    m, n = divmod(i, 2)
                    dve.wait_ge(y_turned, i + 1)
                    dve.tensor_copy(yT[:, m, n * 512:(n + 1) * 512], s.bank[i % 4]).then_inc(y_moved, 1)

            @block.scalar
            def _(act):
                def exp(u):
                    n, _ = span(units[u][0])
                    act.wait_ge(maxed, u + 1)
                    if u >= 2:
                        act.wait_ge(turned, u - 1)
                        act.wait_ge(taken, u - 1)
                    act.activation(pr[:, u % 2, 0:n], lg[:, u % 2, 0:n], ACT.Exp, bias=mx[:, u % 2, 0:1],
                                   accum_out=mx[:, u % 2, 1:2]).then_inc(exped, 1)

                exp(0)
                for u, (i, h) in enumerate(units):
                    n, _ = span(i)
                    act.wait_ge(turned, u + 1)
                    if u >= 2:
                        act.wait_ge(attended, u - 1)
                    act.activation(prT[:, u % 2, 0:n], s.psum[:, 2048:2048 + n], ACT.Copy).then_inc(moved, 1)
                    if u + 1 < NU:
                        exp(u + 1)


def attention2(s, yT):
    nc = s.nc
    s.gain_q_set = sem(s, "gain_q_set")
    with ExitStack() as ctx:
        sb = lambda name, shape: ctx.enter_context(nc.sbuf_tensor(name, shape, F32))
        s.gain_q = sb("gain_q", [P, 1])
        qT, kT, v_tok = sb("qT2", [P, 4, T]), sb("kT2", [P, 4, T]), sb("v2_tok", [P, NT, D_A])
        q_tok = s.x[:, 0:NT // 2, :].rearrange("p t (a n) -> p (t a) n", a=2)
        k_tok = s.x[:, NT // 2:NT, :].rearrange("p t (a n) -> p (t a) n", a=2)
        stage_qkv(s, qT, kT, v_tok, q_tok, k_tok)
        bias = sb("bias2", [P, H2, KEYS])
        stage_bias(s, bias)
        stage_attention(s, qT, kT, v_tok, bias, q_tok, yT)


def keep_rows(s, dst, name):
    kept = sem(s, name)
    with s.nc.Block() as block:
        @block.sync
        def _(sp):
            for t in range(NT):
                sp.dma_start(dst[t * P:(t + 1) * P, :], s.x[:, t, :]).then_inc(kept, 16)
            sp.wait_ge(kept, 16 * NT)


def bank_group(i):
    return 2 * (i % GG) + i // GG


def groups_of(i):
    g = bank_group(4 * i)
    return slice(g, g + 7, 2)


def stage_ssm_tables(s, t):
    nc, A = s.nc, s.A
    V, WT, TM, EC, ES, MG, dskip = t["V"], t["WT"], t["TM"], t["EC"], t["ES"], t["MG"], t["dskip"]
    with ExitStack() as ctx:
        sb = lambda name, shape: ctx.enter_context(nc.sbuf_tensor(name, shape, F32))
        lam = sb("lam", [GG, 3, P])
        step2 = sb("step2", [GG, 2])
        par = sb("par", [P, 16, GG])
        PW = sb("pw", [P, 2, L2 + 1, GG])
        B = sb("ssm_b", [P, 2, GG, SG])
        BB = sb("ssm_bb", [P, 2, GG, SG])
        X = sb("ssm_cx", [P, 4, P])
        CT = sb("ssm_ct", [P, 2, GG, SG])
        K16 = t["R"][0:SG].rearrange("p r g n -> p (r g n)").rearrange("p (g n) -> p g n", n=P)
        tmp = [sb(f"ssm_t{i}", [P, GG * NCH // 2]) for i in range(2)]
        ins, b_in, c_in, d_in = (sem(s, f"s_{x}") for x in ("ins", "b_in", "c_in", "d_in"))
        spread, lam_turned, act_in, act_out, c_turned, tm_zero, tm_set = (sem(s, f"s_{x}") for x in ("spread", "lam_turned", "act_in", "act_out", "c_turned", "tm_zero", "tm_set"))
        vk_ready, k_done, k_moved, w_built, w_turned, w_moved = (sem(s, f"s_{x}") for x in ("vk_ready", "k_done", "k_moved", "w_built", "w_turned", "w_moved"))
        WN = t["SP"]
        p = lambda i: par[:, i, :]
        LRE, LIM, STEP, MAG, ANG, SH, CH, AR, AI, FR, FI, T0, T1, T2, M8, NR = range(16)
        with nc.Block() as block:
            @block.sync
            def _(sp):
                sp.dma_start(lam[:, 0, :], A["ssm_lambda_re_2"][0].rearrange("(g two) p -> g (two p)", two=2)).then_inc(ins, 16)
                sp.dma_start(lam[:, 1, :], A["ssm_lambda_im_2"][0].rearrange("(g two) p -> g (two p)", two=2)).then_inc(ins, 16)
                sp.dma_start(step2[:, :], A["ssm_log_step_2"][0].rearrange("(g two) -> g two", two=2)).then_inc(ins, 16)
                for r, n in enumerate(("ssm_b_re_2", "ssm_b_im_2")):
                    sp.dma_start(B[:, r, :, :], A[n][0].rearrange("(g two) p c -> (two p) g c", two=2)).then_inc(b_in, 16)
                for r, n in enumerate(("ssm_c_re_2", "ssm_c_im_2")):
                    src = A[n][0].rearrange("(g two) c p -> g c two p", two=2)
                    for g in range(GG):
                        q = (g % 8) * SG
                        sp.dma_start(X[q:q + SG, 2 * r + g // 8, :].rearrange("c (two p) -> c two p", two=2), src[g]).then_inc(c_in, 16)
                sp.dma_start(dskip[:, :], A["ssm_d_2"].to_broadcast([P, 512])).then_inc(d_in, 16)
                sp.wait_ge(k_moved, 8)
                sp.wait_ge(tm_zero, 1)
                for j in range(L2):
                    sp.dma_start(TM[j * SG:(j + 1) * SG, :, j * SG:P], K16[:, :, 0:P - j * SG]).then_inc(tm_set, 16)
                sp.wait_ge(tm_set, 16 * L2)
                sp.wait_ge(d_in, 16)

            @block.gpsimd
            def _(pool):
                pool.memset(TM[:, :, :], 0.0).then_inc(tm_zero, 1)

            @block.tensor
            def _(pe):
                pe.wait_ge(spread, 1)
                pe.wait_ge(ins, 48)
                for i in range(3):
                    last = pe.transpose(s.bank[0][:, i * GG:(i + 1) * GG], lam[:, i, :], s.ident[0:GG, 0:GG])
                last.then_inc(lam_turned, 1)
                pe.wait_ge(c_in, 16 * 2 * GG)
                for i in range(4):
                    last = pe.transpose(s.bank[1][:, i * P:(i + 1) * P], X[:, i, :], s.ident[:, :])
                last.then_inc(c_turned, 1)
                pe.wait_ge(vk_ready, 1)
                for i in range(GRP):
                    g = bank_group(i)
                    lanes = slice((g % 2) * SP_, (g % 2) * SP_ + SP_)
                    to = s.bank[i // 4][0:SG, (i % 4) * P:(i % 4 + 1) * P]
                    for r in range(2):
                        last = pe.matmul(to, BB[lanes, r, g // 2, :], V[lanes, r, g // 2, 0:L2, :].rearrange("p d c -> p (d c)"),
                                         start=(r == 0), stop=(r == 1))
                    if i % 4 == 3:
                        last.then_inc(k_done, 1)
                pe.wait_ge(w_built, 1)
                for i in range(8):
                    pe.wait_ge(k_moved, i + 1)
                    for a in range(4):
                        r, g = divmod(i * 4 + a, GG)
                        last = pe.transpose(s.bank[i][:, a * P:(a + 1) * P], WN[:, r, g, :], s.ident[:, :])
                    last.then_inc(w_turned, 1)

            @block.scalar
            def _(act):
                c = s.act_c
                act.wait_ge(act_in, 1)
                c.link(act, act.activation(p(STEP), p(STEP), ACT.Exp))
                act.sem_inc(act_out, 1)
                act.wait_ge(act_in, 2)
                c.link(act, act.activation(p(MAG), p(T0), ACT.Exp))
                c.link(act, act.activation(p(SH), p(T1), ACT.Sin))
                c.link(act, act.activation(p(CH), p(T2), ACT.Sin))
                act.sem_inc(act_out, 1)
                for i in range(8):
                    act.wait_ge(w_turned, i + 1)
                    act.activation(WT[:, :, :].rearrange("p a n -> p (a n)")[:, i * 512:(i + 1) * 512], s.bank[i], ACT.Copy).then_inc(w_moved, 1)

            @block.vector
            def _(dve):
                c = s.dve_c
                mul = lambda o, a, b: c.link(dve, dve.tensor_tensor(o, a, b, ALU.mult))
                add = lambda o, a, b: c.link(dve, dve.tensor_tensor(o, a, b, ALU.add))
                sub = lambda o, a, b: c.link(dve, dve.tensor_tensor(o, a, b, ALU.subtract))

                def complex_mul(re, im, ar, ai, br, bi, t0, t1, neg_im=False):
                    mul(t0, ar, br)
                    mul(t1, ai, bi)
                    sub(re, t0, t1)
                    mul(t0, ar, bi)
                    mul(t1, ai, br)
                    add(im, t0, t1)
                    if neg_im:
                        c.link(dve, dve.tensor_scalar(im, im, -1.0, None, ALU.mult))

                dve.wait_ge(ins, 48)
                c.link(dve, dve.tensor_copy(lam[:, 2, :].rearrange("g (two p) -> g two p", two=2),
                                            step2[:, :].rearrange("g (two o) -> g two o", o=1).to_broadcast([GG, 2, SP_])))
                dve.sem_inc(spread, 1)
                dve.wait_ge(lam_turned, 1)
                c.link(dve, dve.tensor_copy(par[:, 0:3, :], s.bank[0][:, 0:3 * GG].rearrange("p (i g) -> p i g", i=3)))
                dve.sem_inc(act_in, 1)
                dve.wait_ge(act_out, 1)
                mul(p(T0), p(LRE), p(STEP))
                mul(p(ANG), p(LIM), p(STEP))
                c.link(dve, dve.tensor_scalar(p(NR), p(ANG), 1.0 / (2.0 * math.pi), ROUND, ALU.mult, ALU.add))
                c.link(dve, dve.tensor_scalar(p(NR), p(NR), -ROUND, None, ALU.add))
                for part in TWO_PI:
                    c.link(dve, dve.scalar_tensor_tensor(p(ANG), p(NR), -part, p(ANG), ALU.mult, ALU.add))
                c.link(dve, dve.tensor_scalar(p(T1), p(ANG), 0.5, None, ALU.mult))
                c.link(dve, dve.tensor_scalar(p(T2), p(T1), -1.0, None, ALU.mult))
                c.link(dve, dve.tensor_tensor(p(T2), p(T2), p(T1), ALU.max))
                c.link(dve, dve.tensor_scalar(p(T2), p(T2), -1.0, float(math.pi / 2), ALU.mult, ALU.add))
                dve.sem_inc(act_in, 1)
                dve.wait_ge(act_out, 2)
                mul(p(T0), p(SH), p(SH))
                mul(p(T1), p(SH), p(CH))
                c.link(dve, dve.tensor_scalar(p(CH), p(T0), -2.0, 1.0, ALU.mult, ALU.add))
                c.link(dve, dve.tensor_scalar(p(SH), p(T1), 2.0, None, ALU.mult))
                mul(p(AR), p(MAG), p(CH))
                mul(p(AI), p(MAG), p(SH))
                c.link(dve, dve.tensor_scalar(p(NR), p(AR), -1.0, None, ALU.add))
                mul(p(T0), p(LRE), p(LRE))
                mul(p(T1), p(LIM), p(LIM))
                add(p(T0), p(T0), p(T1))
                c.link(dve, dve.reciprocal(p(T2), p(T0)))
                mul(p(T0), p(NR), p(LRE))
                mul(p(T1), p(AI), p(LIM))
                add(p(T0), p(T0), p(T1))
                mul(p(FR), p(T0), p(T2))
                mul(p(T0), p(AI), p(LRE))
                mul(p(T1), p(NR), p(LIM))
                sub(p(T0), p(T0), p(T1))
                mul(p(FI), p(T0), p(T2))
                c.then(dve.memset(PW[:, 0, 0, :], 1.0))
                c.link(dve, dve.memset(PW[:, 1, 0, :], 0.0))
                for d in range(1, L2 + 1):
                    complex_mul(PW[:, 0, d, :], PW[:, 1, d, :], PW[:, 0, d - 1, :], PW[:, 1, d - 1, :], p(AR), p(AI), p(T0), p(T1))
                mul(p(M8), p(MAG), p(MAG))
                mul(p(M8), p(M8), p(M8))
                mul(p(M8), p(M8), p(M8))
                for _ in range(3):
                    complex_mul(p(T2), p(NR), p(CH), p(SH), p(CH), p(SH), p(T0), p(T1))
                    c.link(dve, dve.tensor_copy(p(CH), p(T2)))
                    c.link(dve, dve.tensor_copy(p(SH), p(NR)))
                dve.wait_ge(b_in, 32)
                wide = lambda x, n: x.rearrange("p (g o) -> p g o", o=1).to_broadcast([P, GG, n])
                small = lambda i, n: tmp[i][:, 0:GG * n].rearrange("p (g c) -> p g c", g=GG)
                complex_mul(BB[:, 0], BB[:, 1], B[:, 0], B[:, 1], wide(p(FR), SG), wide(p(FI), SG), small(0, SG), small(1, SG))
                dve.wait_ge(c_turned, 1)
                c.link(dve, dve.tensor_copy(CT[:, :, :, :].rearrange("p r g c -> p (r g c)"), s.bank[1]))
                for d in range(L2 + 1):
                    complex_mul(V[:, 0, :, d, :], V[:, 1, :, d, :], CT[:, 0], CT[:, 1], wide(PW[:, 0, d, :], SG), wide(PW[:, 1, d, :], SG),
                                small(0, SG), small(1, SG), neg_im=True)
                dve.sem_inc(vk_ready, 1)
                for j in range(L2):
                    W = [WN[:, r].rearrange("p g (j c) -> p g j c", j=L2)[:, :, j, :] for r in range(2)]
                    complex_mul(W[0], W[1], BB[:, 0], BB[:, 1], wide(PW[:, 0, L2 - 1 - j, :], SG), wide(PW[:, 1, L2 - 1 - j, :], SG),
                                small(0, SG), small(1, SG))
                dve.sem_inc(w_built, 1)
                for i in range(8):
                    dve.wait_ge(k_done, i + 1)
                    dve.tensor_copy(K16[:, groups_of(i), :], s.bank[i][0:SG, :].rearrange("p (g n) -> p g n", g=4)).then_inc(k_moved, 1)
                c.then(dve.memset(EC[:, :, 0:1], 1.0))
                c.link(dve, dve.memset(ES[:, :, 0:1], 0.0))
                n = 1
                while n < NCH:
                    part = lambda i: tmp[i][:, 0:GG * n].rearrange("p (g c) -> p g c", g=GG)
                    complex_mul(EC[:, :, n:2 * n], ES[:, :, n:2 * n], EC[:, :, 0:n], ES[:, :, 0:n], wide(p(CH), n), wide(p(SH), n),
                                part(0), part(1))
                    complex_mul(p(T2), p(NR), p(CH), p(SH), p(CH), p(SH), p(T0), p(T1))
                    c.link(dve, dve.tensor_copy(p(CH), p(T2)))
                    c.link(dve, dve.tensor_copy(p(SH), p(NR)))
                    n *= 2
                c.link(dve, dve.tensor_copy(MG[:, :, :], wide(p(M8), NCH)))
                c.link(dve, dve.memset(MG[:, :, 0:1], 0.0))
                dve.wait_ge(w_moved, 8)


def stage_ssm(s, t, yT):
    nc, A = s.nc, s.A
    V, WT, TM, EC, ES, MG, R, SP, dskip = (t[n] for n in ("V", "WT", "TM", "EC", "ES", "MG", "R", "SP", "dskip"))
    U = s.x[:, 0:4, :].rearrange("p a n -> p (a n)").rearrange("p (g j c) -> p g j c", g=GRP, j=L2)
    UT = s.x[:, 4:8, :].rearrange("p a n -> p (a n)").rearrange("p (g n) -> p g n", g=GRP)
    wu = SP[:, :, :, :].rearrange("p r g n -> p (r g n)").rearrange("p (k n) -> p k n", k=KD)
    Y = WT[:, :, :].rearrange("p a n -> p (a n)").rearrange("p (t c) -> p t c", t=L2)
    zT = R[:, :, :, :].rearrange("p r g n -> p (r g n)").rearrange("p (m t) -> p m t", m=4)
    tmp = WT[:, :, :].rearrange("p a n -> p (a n)")
    rot = t["rot"]
    wglu = MG[:, :, :].rearrange("p g n -> p (g n)").rearrange("p (k n) -> p k n", k=4)
    wu_in, u_done, u_moved, u_turned, ut_moved, du_ready = (sem(s, f"u_{x}") for x in ("wu_in", "u_done", "u_moved", "u_turned", "ut_moved", "du_ready"))
    loc_done, rotated, sp_ready, y_done, y_ready, gelu_ready = (sem(s, f"u_{x}") for x in ("loc_done", "rotated", "sp_ready", "y_done", "y_ready", "gelu_ready"))
    z_turned, z_moved, glu_in, glu_done, glu_sig, scanned, wu_free = (sem(s, f"u_{x}") for x in ("z_turned", "z_moved", "glu_in", "glu_done", "glu_sig", "scanned", "wu_free"))
    with nc.Block() as block:
        @block.sync
        def _(sp):
            src = A["w_in_2"][0].rearrange("(k p) n -> p k n", p=P)
            for k in range(0, KD, 4):
                sp.dma_start(wu[:, k:k + 4, :], src[:, k:k + 4, C2_U:C2_U + 512]).then_inc(wu_in, 16)
            sp.wait_ge(scanned, 2)
            sp.dma_start(wglu, A["w_glu_2"][0].rearrange("(k p) n -> p k n", p=P)).then_inc(glu_in, 16)

        @block.gpsimd
        def _(pool):
            pool.wait_ge(u_turned, 8)
            d = dskip[:, :].rearrange("p (g c) -> p g c", g=GRP)
            for j in range(L2):
                pool.tensor_tensor(U[:, :, j, :], U[:, :, j, :], d, ALU.mult).then_inc(du_ready, 1)

        @block.tensor
        def _(pe):
            pe.wait_ge(wu_in, 32)
            for j in range(L2):
                for k in range(KD):
                    last = pe.matmul(s.bank[j], s.hT[:, k, j:T:L2], wu[:, k, :], start=(k == 0), stop=(k == KD - 1))
                last.then_inc(u_done, 1)
            pe.wait_ge(u_moved, L2)
            for i in range(8):
                for a in range(4):
                    g = 4 * i + a
                    last = pe.transpose(s.bank[i][:, a * P:(a + 1) * P], U[:, g].rearrange("p j c -> p (j c)"), s.ident[:, :])
                last.then_inc(u_turned, 1)
            for i in range(8):
                pe.wait_ge(ut_moved, 8)
                for a in range(2):
                    gg = 2 * i + a
                    for r in range(2):
                        for two in range(2):
                            to = s.bank[i][two * SP_:(two + 1) * SP_, (2 * a + r) * P:(2 * a + r + 1) * P]
                            last = pe.matmul(to, WT[:, r * GG + gg, two * SP_:(two + 1) * SP_], UT[:, 2 * gg + two, :], start=True, stop=True)
                last.then_inc(loc_done, 1)
            pe.wait_ge(sp_ready, 2)
            for i in range(8):
                pe.wait_ge(rotated, 8)
                for a in range(4):
                    g = bank_group(4 * i + a)
                    lanes = slice((g % 2) * SP_, (g % 2) * SP_ + SP_)
                    to = s.bank[i][:, a * P:(a + 1) * P]
                    pe.matmul(to, UT[:, g, :], TM[:, g, :], start=True, stop=False)
                    for r in range(2):
                        last = pe.matmul(to, SP[lanes, r, g // 2, :], V[lanes, r, g // 2, 1:L2 + 1, :].rearrange("p d c -> p (d c)"),
                                         start=False, stop=(r == 1))
                last.then_inc(y_done, 1)
            for j in range(L2):
                pe.wait_ge(gelu_ready, j + 1)
                pe.wait_ge(y_ready, 8)
                for m in range(4):
                    last = pe.transpose(s.bank[j][:, m * P:(m + 1) * P], Y[:, j, m * P:(m + 1) * P], s.ident[:, :])
                last.then_inc(z_turned, 1)
            pe.wait_ge(z_moved, L2)
            pe.wait_ge(glu_in, 16)
            for i in range(8):
                m, n = divmod(i, 2)
                for k in range(4):
                    last = pe.matmul(s.bank[i], wglu[:, k, m * P:(m + 1) * P], zT[:, k, n * 512:(n + 1) * 512], start=(k == 0), stop=(k == 3))
                last.then_inc(glu_done, 1)

        @block.vector
        def _(dve):
            c = s.dve_c
            for j in range(L2):
                dve.wait_ge(u_done, j + 1)
                dve.tensor_copy(U[:, :, j, :], s.bank[j].rearrange("p (g c) -> p g c", g=GRP)).then_inc(u_moved, 1)
            for i in range(8):
                dve.wait_ge(u_turned, i + 1)
                dve.tensor_copy(UT[:, 4 * i:4 * i + 4, :].rearrange("p g n -> p (g n)"), s.bank[i]).then_inc(ut_moved, 1)
            t0, t1 = (rot[:, i * 256:(i + 1) * 256].rearrange("p (a n) -> p a n", a=2) for i in range(2))
            for i in range(8):
                dve.wait_ge(loc_done, i + 1)
                got = s.bank[i].rearrange("p (a r n) -> p a r n", a=2, r=2)
                gs = slice(2 * i, 2 * i + 2)
                c.then(dve.tensor_tensor(t0, got[:, :, 0, :], EC[:, gs, :], ALU.mult))
                c.link(dve, dve.tensor_tensor(t1, got[:, :, 1, :], ES[:, gs, :], ALU.mult))
                c.link(dve, dve.tensor_tensor(R[:, 0, gs, :], t0, t1, ALU.add))
                c.then(dve.tensor_tensor(t0, got[:, :, 1, :], EC[:, gs, :], ALU.mult))
                c.link(dve, dve.tensor_tensor(t1, got[:, :, 0, :], ES[:, gs, :], ALU.mult))
                dve.tensor_tensor(R[:, 1, gs, :], t0, t1, ALU.subtract).then_inc(rotated, 1)
                dve.wait_ge(rotated, i + 1)
            f = lambda x: x.rearrange("p g n -> p (g n)")
            for r in range(2):
                dve.tensor_tensor_scan(f(SP[:, r]), f(MG[:, :, :]), f(R[:, r]), 0.0, ALU.mult, ALU.add).then_inc(scanned, 1)
            dve.wait_ge(scanned, 2)
            n = NCH - 1
            a, b = (tmp[:, i * 2048:(i + 1) * 2048].rearrange("p (g n) -> p g n", g=GG)[:, :, 0:n] for i in range(2))
            c.then(dve.tensor_tensor(a, SP[:, 0, :, 0:n], EC[:, :, 0:n], ALU.mult))
            c.link(dve, dve.tensor_tensor(b, SP[:, 1, :, 0:n], ES[:, :, 0:n], ALU.mult))
            c.link(dve, dve.tensor_tensor(a, a, b, ALU.subtract))
            c.link(dve, dve.tensor_tensor(b, SP[:, 0, :, 0:n], ES[:, :, 0:n], ALU.mult))
            c.link(dve, dve.tensor_tensor(R[:, 0, :, 0:n], SP[:, 1, :, 0:n], EC[:, :, 0:n], ALU.mult))
            c.link(dve, dve.tensor_tensor(SP[:, 1, :, 1:NCH], R[:, 0, :, 0:n], b, ALU.add))
            c.then(dve.memset(SP[:, :, :, 0:1], 0.0))
            c.link(dve, dve.tensor_copy(SP[:, 0, :, 1:NCH], a))
            dve.sem_inc(sp_ready, 2)
            dve.wait_ge(du_ready, L2)
            for i in range(8):
                dve.wait_ge(y_done, i + 1)
                to = Y.rearrange("p t (g c) -> p g t c", g=GRP)[:, groups_of(i)]
                dve.tensor_tensor(to, s.bank[i].rearrange("p (g t c) -> p g t c", g=4, t=L2), U[:, groups_of(i)], ALU.add).then_inc(y_ready, 1)
            for j in range(L2):
                dve.wait_ge(z_turned, j + 1)
                dve.tensor_copy(zT[:, :, j:T:L2], s.bank[j].rearrange("p (m n) -> p m n", m=4)).then_inc(z_moved, 1)
            for i in range(8):
                m, n = divmod(i, 2)
                dve.wait_ge(glu_sig, i + 1)
                cols = slice(n * 512, (n + 1) * 512)
                c.then(dve.tensor_tensor(yT[:, m, cols], yT[:, m, cols], zT[:, m, cols], ALU.mult))

        @block.scalar
        def _(act):
            act.wait_ge(y_ready, 8)
            for j in range(L2):
                act.activation(Y[:, j, :], Y[:, j, :], ACT.Gelu_apprx_tanh).then_inc(gelu_ready, 1)
            for i in range(8):
                m, n = divmod(i, 2)
                act.wait_ge(glu_done, i + 1)
                b = VEC["b_glu_2"] + m
                act.activation(yT[:, m, n * 512:(n + 1) * 512], s.bank[i], ACT.Sigmoid, bias=s.vec[:, b:b + 1]).then_inc(glu_sig, 1)


def ssm2(s):
    nc = s.nc
    yT = s.x[:, 4:8, :]
    with ExitStack() as ctx:
        sb = lambda name, shape: ctx.enter_context(nc.sbuf_tensor(name, shape, F32))
        t = {"V": sb("ssm_V", [P, 2, GG, L2 + 1, SG]), "WT": sb("ssm_WT", [P, 2 * GG, P]), "TM": sb("ssm_TM", [P, GRP, P]),
             "EC": sb("ssm_EC", [P, GG, NCH]), "ES": sb("ssm_ES", [P, GG, NCH]), "MG": sb("ssm_MG", [P, GG, NCH]),
             "dskip": sb("ssm_d", [P, 512])}
        t["SP"] = sb("ssm_SP", [P, 2, GG, NCH])
        t["R"] = s.x[:, 0:4, :].rearrange("p a n -> p (a n)").rearrange("p (r g n) -> p r g n", r=2, g=GG)
        stage_ssm_tables(s, t)
        t["R"] = sb("ssm_R", [P, 2, GG, NCH])
        t["rot"] = sb("ssm_rot", [P, 512])
        stage_ssm(s, t, yT)


def stage_branches(s, yaT, ysT, mT):
    nc, A = s.nc, s.A
    with nc.sbuf_tensor("g_ring", [P, 2, KD, 2, 256], F32) as ring, nc.sbuf_tensor("wb_ring", [P, 2, KD, 256], F32) as wb, \
            nc.sbuf_tensor("branch_sig", [P, 2, 2, 512], F32) as sig, nc.sbuf_tensor("branch_tmp", [P, 2, 512], F32) as tmp:
        w_ready = [sem(s, f"n_w{i}") for i in range(4)]
        done, sigged, merged = sem(s, "n_done"), sem(s, "n_sigged"), sem(s, "n_merged")
        w_src = A["w_in_2"][0].rearrange("(k p) n -> p k n", p=P)
        wb_src = A["w_branch_2"][0].rearrange("(k p) n -> p k n", p=P)
        with nc.Block() as block:
            @block.sync
            def _(sp):
                for q in range(4):
                    if q >= 2:
                        sp.wait_ge(merged, 4 * (q - 1))
                    c0 = q * 256
                    for b in range(2):
                        sp.dma_start(ring[:, q % 2, :, b, :], w_src[:, :, C2_GATE + b * D + c0:C2_GATE + b * D + c0 + 256]).then_inc(w_ready[q], 16)
                    sp.dma_start(wb[:, q % 2], wb_src[:, :, c0:c0 + 256]).then_inc(w_ready[q], 16)

            @block.tensor
            def _(pe):
                for i in range(2 * KD):
                    m, n = divmod(i, 2)
                    q, c0 = m // 2, (m % 2) * P
                    if i % 4 == 0:
                        pe.wait_ge(w_ready[q], 48)
                    if i >= 2:
                        pe.wait_ge(merged, i - 1)
                    cols = slice(n * 512, (n + 1) * 512)
                    for b in range(2):
                        for k in range(KD):
                            last = pe.matmul(s.bank[4 * (i % 2) + b], ring[:, q % 2, k, b, c0:c0 + P], s.hT[:, k, cols],
                                             start=(k == 0), stop=(k == KD - 1))
                        last.then_inc(done, 1)
                    for b, y in enumerate((yaT, ysT)):
                        for k in range(4):
                            last = pe.matmul(s.bank[4 * (i % 2) + 2 + b], wb[:, q % 2, 4 * b + k, c0:c0 + P], y[:, k, cols],
                                             start=(k == 0), stop=(k == 3))
                        last.then_inc(done, 1)

            @block.scalar
            def _(act):
                for i in range(2 * KD):
                    m = i // 2
                    for b in range(2):
                        act.wait_ge(done, 4 * i + b + 1)
                        if i >= 2:
                            act.wait_ge(merged, i - 1)
                        v = VEC["b_gate_2"] + b * KD + m
                        act.activation(sig[:, i % 2, b, :], s.bank[4 * (i % 2) + b], ACT.Sigmoid, bias=s.vec[:, v:v + 1]).then_inc(sigged, 1)

            @block.vector
            def _(dve):
                c = s.dve_c
                for i in range(2 * KD):
                    m, n = divmod(i, 2)
                    dve.wait_ge(done, 4 * i + 4)
                    dve.wait_ge(sigged, 2 * i + 2)
                    to = mT[:, m, n * 512:(n + 1) * 512]
                    c.then(dve.tensor_tensor(tmp[:, i % 2, :], s.bank[4 * (i % 2) + 2], sig[:, i % 2, 0, :], ALU.mult))
                    c.link(dve, dve.tensor_tensor(to, s.bank[4 * (i % 2) + 3], sig[:, i % 2, 1, :], ALU.mult))
                    dve.tensor_tensor(to, to, tmp[:, i % 2, :], ALU.add).then_inc(merged, 1)


def stage_route2(s, mo, gate, mask):
    nc, A = s.nc, s.A
    NL = NG2 + E2
    with nc.sbuf_tensor("w_r2", [P, KD, NL], F32) as w, nc.sbuf_tensor("b_r2", [P, NL], F32) as b, \
            nc.sbuf_tensor("l2", [P, NT, NL], F32) as lg, nc.sbuf_tensor("pg", [P, NT, 16], F32) as pg, \
            nc.sbuf_tensor("rest2", [P, NT, 16], F32) as rest, nc.sbuf_tensor("top2", [P, NT, 8], F32) as top, \
            nc.sbuf_tensor("find", [P, NT, 8], F32) as find, nc.sbuf_tensor("gm", [P, NT, NG2], F32) as gm, \
            nc.sbuf_tensor("eg", [P, NT, NG2], F32) as eg, nc.sbuf_tensor("el", [P, NT, E2], F32) as el, \
            nc.sbuf_tensor("sums2", [P, 3, NT], F32) as sums, nc.sbuf_tensor("off", [P, NT, NG2], F32) as off:
        w_in, logits_done, to_exp, exped = (sem(s, f"q_{x}") for x in ("w_in", "logits_done", "to_exp", "exped"))
        one = lambda x, n: x.rearrange("p (t o) -> p t o", o=1).to_broadcast([P, NT, n])
        with nc.Block() as block:
            @block.sync
            def _(sp):
                sp.dma_start(w[:, :, 0:NG2], A["w_group_router_2"][0].rearrange("(k p) e -> p k e", p=P)).then_inc(w_in, 16)
                sp.dma_start(w[:, :, NG2:NL], A["w_expert_router_2"][0].rearrange("(k p) e -> p k e", p=P)).then_inc(w_in, 16)
                sp.dma_start(b[:, 0:NG2], A["group_bias_2"].to_broadcast([P, NG2])).then_inc(w_in, 16)
                sp.dma_start(b[:, NG2:NL], A["expert_bias_2"].to_broadcast([P, E2])).then_inc(w_in, 16)

            @block.tensor
            def _(pe):
                pe.wait_ge(w_in, 64)
                for t in range(NT):
                    for k in range(KD):
                        last = pe.matmul(s.bank[0][:, t * NL:(t + 1) * NL], s.hT[:, k, t * P:(t + 1) * P], w[:, k, :],
                                         start=(k == 0), stop=(k == KD - 1))
                last.then_inc(logits_done, 1)

            @block.scalar
            def _(act):
                act.wait_ge(to_exp, 1)
                act.activation(eg[:, :, :], eg[:, :, :], ACT.Exp).then_inc(exped, 1)
                act.wait_ge(to_exp, 2)
                act.activation(gate[:, :, :], gate[:, :, :], ACT.Exp).then_inc(exped, 1)

            @block.vector
            def _(dve):
                c = s.dve_c
                L = lambda ins: c.link(dve, ins)
                dve.wait_ge(w_in, 64)
                dve.wait_ge(logits_done, 1)
                L(dve.tensor_tensor(lg[:, :, :], s.bank[0][:, 0:NT * NL].rearrange("p (t e) -> p t e", t=NT),
                                    b[:, :].rearrange("p (o e) -> p o e", o=1).to_broadcast([P, NT, NL]), ALU.add))
                L(dve.memset(pg[:, :, :], -BIG))
                L(dve.memset(find[:, :, :], -BIG))
                L(dve.tensor_copy(pg[:, :, 0:NG2], lg[:, :, 0:NG2]))
                for t in range(NT):
                    L(dve.max(top[:, t, :], pg[:, t, :]))
                L(dve.tensor_copy(find[:, :, 0:1], top[:, :, 0:1]))
                for t in range(NT):
                    L(dve.match_replace(out=rest[:, t, :], in_to_replace=find[:, t, :], in_values=pg[:, t, :], imm_value=BIG))
                L(dve.tensor_tensor(gm[:, :, :], rest[:, :, 0:NG2], pg[:, :, 0:NG2], ALU.not_equal))
                L(dve.tensor_tensor(eg[:, :, :], lg[:, :, 0:NG2], top[:, :, 0:1].to_broadcast([P, NT, NG2]), ALU.subtract))
                dve.sem_inc(to_exp, 1)
                L(dve.tensor_scalar(off[:, :, :], gm[:, :, :], -1.0, BIG, ALU.add, ALU.mult))
                for t in range(NT):
                    for g in range(NG2):
                        L(dve.tensor_scalar(el[:, t, g * EPG:(g + 1) * EPG], lg[:, t, NG2 + g * EPG:NG2 + (g + 1) * EPG],
                                            gm[:, t, g:g + 1], off[:, t, g:g + 1], ALU.mult, ALU.add))
                for t in range(NT):
                    L(dve.max(top[:, t, :], el[:, t, :]))
                L(dve.tensor_copy(find[:, :, 0:TOP2], top[:, :, 0:TOP2]))
                for t in range(NT):
                    L(dve.match_replace(out=rest[:, t, :], in_to_replace=find[:, t, :], in_values=el[:, t, :], imm_value=BIG))
                L(dve.tensor_tensor(mask[:, :, :], rest[:, :, :], el[:, :, :], ALU.not_equal))
                L(dve.tensor_tensor(mask[:, :, :].rearrange("p t (g e) -> p (t g) e", g=NG2), mask[:, :, :].rearrange("p t (g e) -> p (t g) e", g=NG2),
                                    gm[:, :, :].rearrange("p t (g o) -> p (t g) o", o=1).to_broadcast([P, NT * NG2, EPG]), ALU.mult))
                L(dve.tensor_tensor(gate[:, :, :], el[:, :, :], top[:, :, 0:1].to_broadcast([P, NT, E2]), ALU.subtract))
                dve.sem_inc(to_exp, 1)
                dve.wait_ge(exped, 2)
                L(dve.tensor_tensor(gate[:, :, :], gate[:, :, :], mask[:, :, :], ALU.mult))
                L(dve.tensor_reduce(sums[:, 0, :], gate[:, :, :], AX_X, ALU.add))
                L(dve.tensor_reduce(sums[:, 1, :], eg[:, :, :], AX_X, ALU.add))
                L(dve.tensor_tensor(sums[:, 2, :], sums[:, 0, :], sums[:, 1, :], ALU.mult))
                L(dve.reciprocal(sums[:, 0, :], sums[:, 2, :]))
                L(dve.tensor_tensor(gate[:, :, :], gate[:, :, :], one(sums[:, 0, :], E2), ALU.mult))


def ffn2(s):
    nc, A = s.nc, s.A
    mo = Moe(s, "moe2", E2, TOP2, F2)
    v = VEC["ffn_norm_gain_2"]
    gain = lambda k: s.vec[:, v + k:v + k + 1]
    stage_norm(s, "norm_g", s.x, NT, s.hT, gain, None, rows_to=mo.rows)
    keep_rows(s, mo.acc, "x3_kept")
    out_stored = sem(s, "out_stored")
    with ExitStack() as tables:
        tab = lambda name, shape, dt: tables.enter_context(nc.sbuf_tensor(name, shape, dt))
        start = tab("start2", [P, mo.E + 1], I32)
        idx_g, idx_s = tab("idx_g2", [P, mo.NB + 2], I32), tab("idx_s2", [P, mo.NB], I32)
        row_w = tab("row_w2", [P, mo.NB], F32)
        with nc.sbuf_tensor("gate2", [P, NT, mo.E], F32) as gate, nc.sbuf_tensor("mask2", [P, NT, mo.E], F32) as mask:
            stage_route2(s, mo, gate, mask)
            stage_dispatch(s, mo, gate, mask, start, idx_g, idx_s, row_w)
        stage_experts(s, mo, start, idx_g, idx_s, row_w, A["w_e_gate_2"][0], A["w_e_up_2"][0], A["w_e_down_2"][0], gain, None)
    with nc.Block() as block:
        @block.sync
        def _(sp):
            sp.dma_start(s.out[0], mo.acc[0:T, :]).then_inc(out_stored, 16)
            sp.wait_ge(out_stored, 16)


def block2(s):
    nc, A = s.nc, s.A
    x_kept = nc.dram_tensor("x2_kept", (T, D), F32, kind="Internal").ap()
    v = VEC["mix_norm_gain_2"]
    stage_norm(s, "norm_2", s.x, NT, s.hT, lambda k: s.vec[:, v + k:v + k + 1], None)
    keep_rows(s, x_kept, "x2_kept_sem")
    with nc.sbuf_tensor("yaT", [P, 4, T], F32) as yaT:
        attention2(s, yaT)
        ssm2(s)
        ysT = s.x[:, 4:8, :]
        with nc.sbuf_tensor("mT", [P, KD, T], F32) as mT:
            stage_branches(s, yaT, ysT, mT)
            stage_out(s, "out_2", mT, A["w_out_2"][0], None, x_src=x_kept)
    return_sems(s)
    ffn2(s)


def program(nc, A, out):
    s = setup(nc, A, out)
    stage_condition(s)
    mixer_inputs(s)
    stage_gates(s)
    stage_mlstm(s)
    stage_mix(s)
    s.mixer.close()
    stage_out(s, "out_1", s.hT, A["w_out"][0], 0, A["x"][0], A["b_out"][0:1, :])
    return_sems(s)
    ffn1(s)
    return_sems(s)
    block2(s)


def kernel(**inputs):
    import numpy as _np
    import concourse.bacc as _bacc
    from concourse import mybir as _mybir
    from concourse.bass_utils import run_bass_kernel_spmd as _run

    nc = _bacc.Bacc("TRN2", target_bir_lowering=False, num_devices=1)
    arrays, args = {}, {}
    for name, value in inputs.items():
        a = _np.ascontiguousarray(value)
        arrays[f"in_{name}"] = a
        args[name] = nc.dram_tensor(f"in_{name}", a.shape, _mybir.dt.from_np(a.dtype), kind="ExternalInput").ap()
    out = nc.dram_tensor("out_0_dram", (1, T, D), F32, kind="ExternalOutput").ap()
    program(nc, args, out)
    r = _run(nc, [arrays], core_ids=[0])
    return r.results[0]["out_0_dram"]
```

```python
import math
from contextlib import ExitStack

import concourse.bass as bass
from concourse import mybir

F32 = mybir.dt.float32
F32R = mybir.dt.float32r
I32 = mybir.dt.int32
ACT = mybir.ActivationFunctionType
ALU = mybir.AluOpType
AX_X = mybir.AxisListType.X

P = 128
D = 1024
KD = D // P
T = 1024
NT = T // P
CTX = 256
NC = CTX // P
EPS = 1e-6
NEG = -1.0e30

H1, DK, DV = 4, 64, 128
D_QK, D_V = H1 * DK, H1 * DV
C_QK, C_V, C_O, C_GT = 0, 2 * D_QK, 2 * D_QK + D_V, 2 * D_QK + 2 * D_V
N_GT = 4 * H1
C_GA = C_GT + N_GT
D_CONV = 512
C_GB = C_GA + D_CONV
KC = D_CONV // P
TAPS = 31
GRID = 64
ROWS = T // GRID
PAD = TAPS // 2
STEPS = NC + NT
NCOL = STEPS * 2 * H1
E1, F1, TOP1 = 64, 256, 8
ROUTE_SCALE = 2.5


class Chain:

    def __init__(self, nc, name):
        self.sem, self.n = nc.alloc_semaphore(name), 0

    def then(self, ins):
        self.n += 1
        return ins.then_inc(self.sem, 1)

    def wait(self, eng):
        eng.wait_ge(self.sem, self.n)

    def link(self, eng, ins):
        self.then(ins)
        self.wait(eng)


class State:
    pass


def setup(nc, A, out):
    s = State()
    s.nc, s.A, s.out = nc, A, out
    sb = lambda name, shape, dt=F32: nc.alloc_sbuf_tensor(name, shape, dt)
    s.psum = nc.alloc_psum_tensor("psum", [P, 8 * 512], F32)
    s.bank = [s.psum[:, i * 512:(i + 1) * 512] for i in range(8)]
    s.ident = sb("ident", [P, P])
    s.ones = sb("ones", [P, P])
    s.tri_le = sb("tri_le", [P, P])
    s.tri_ge = sb("tri_ge", [P, P])
    s.vec = sb("vec", [P, P])
    s.vec2 = sb("vec2", [P, 18])
    s.convw = sb("convw", [P, TAPS * KC])
    s.cond = sb("cond", [P, KD, 2])
    s.mod = sb("mod", [P, 4, KD, 2])
    s.gpost = sb("gpost", [P, 2, D])
    with nc.sbuf_tensor("x_cut", [P, NT, D], F32) as s.x_cut:
        pass
    s.x = sb("x", [P, NT, D])
    with nc.sbuf_tensor("hT_cut", [P, KD, T], F32) as s.hT_cut:
        pass
    s.hT = sb("hT", [P, KD, T])
    s.x_sums = sb("x_sums", [P, NT])
    s.act_c = Chain(nc, "act_own")
    s.dve_c = Chain(nc, "dve_own")
    s.pool_c = Chain(nc, "pool_own")
    s.sems = []
    return s


COL_BANK = {0: 1, 1: 6, 3: 7, 4: 0}

VEC = {"b_ada": 0, "g_pre_mix": 48, "g_pre_ffn": 56, "mix_norm_gain_2": 64, "ffn_norm_gain_2": 72,
       "b_qk": 80, "b_gab": 84, "b_gate_2": 92, "b_glu_2": 108, "conv_b": 112, "conv_ln_g": 116,
       "conv_ln_b": 120, "spare": 124}


def sem(s, name):
    s.sems.append(s.nc.alloc_semaphore(name))
    return s.sems[-1]


def return_sems(s):
    s.nc.clear_and_free_semaphores(s.sems)
    s.sems = []
    s.nc.all_engine_barrier()


def rows_of(ap, n):
    return ap.rearrange("a (r p) -> (a r) p", p=P)


def stage_condition(s):
    nc, A = s.nc, s.A
    with nc.sbuf_tensor("v1", [P, P], F32) as v1, nc.sbuf_tensor("v2", [18, P], F32) as v2, \
            nc.sbuf_tensor("v3", [TAPS * KC, P], F32) as v3, \
            nc.sbuf_tensor("wada", [P, 2, KD, D], F32) as wada, \
            nc.sbuf_tensor("c_part", [P, 2, D], F32) as part:
        cond = s.cond
        vecs_in, x_in = sem(s, "vecs_in"), sem(s, "x_in")
        s.x_in = x_in
        wada_in0, wada_in1 = sem(s, "wada_in0"), [sem(s, f"wada_in1_{i}") for i in range(KD // 2)]
        part_ready = sem(s, "c_part_ready")
        consts_set, vecs_turned, vecs_ready = sem(s, "consts_set"), sem(s, "vecs_turned"), sem(s, "vecs_ready")
        cond_ready, ada_done = sem(s, "cond_ready"), sem(s, "ada_done")
        w_src = A["w_ada"][0].rearrange("(k p) (s n) -> s p k n", p=P, n=D)
        N_VEC = 20
        with nc.Block() as block:
            @block.sync
            def _(sp):
                def vec(dst, src):
                    sp.dma_start(dst, src).then_inc(vecs_in, 16)
                for k in range(0, KD, 2):
                    sp.dma_start(wada[:, 0, k:k + 2], w_src[0][:, k:k + 2]).then_inc(wada_in0, 16)
                vec(v1[0:48, :], rows_of(A["b_ada"], 48))
                for n in ("g_pre_mix", "g_pre_ffn", "mix_norm_gain_2", "ffn_norm_gain_2"):
                    vec(v1[VEC[n]:VEC[n] + 8, :], rows_of(A[n], 8))
                vec(v1[80:84, :], rows_of(A["b_in"][:, 0:512], 4))
                vec(v1[84:92, :], rows_of(A["b_in"][:, C_GA:C_GA + 1024], 8))
                vec(v1[92:108, :], rows_of(A["b_gate_2"], 16))
                vec(v1[108:112, :], rows_of(A["b_glu_2"], 4))
                for n in ("conv_b", "conv_ln_g", "conv_ln_b"):
                    vec(v1[VEC[n]:VEC[n] + 4, :], rows_of(A[n], 4))
                vec(v1[124:128, :], rows_of(A["conv_b"], 4))
                vec(v2[0:8, :], rows_of(A["c"], 8))
                vec(v2[8:16, :], A["c_ctx"].rearrange("(r p) -> r p", p=P))
                for r, n in ((16, "q_gain_2"), (17, "k_gain_2")):
                    for h in range(2):
                        vec(v2[r:r + 1, h * 64:h * 64 + 64], A[n])
                vec(v3[:, :], A["conv_w"][0].rearrange("w (m p) -> (w m) p", p=P))
                for k in range(0, KD, 2):
                    sp.dma_start(wada[:, 1, k:k + 2], w_src[1][:, k:k + 2]).then_inc(wada_in1[k // 2], 16)
                for t in range(NT):
                    sp.dma_start(s.x[:, t, :], A["x"][0, t * P:(t + 1) * P, :]).then_inc(x_in, 16)

            @block.gpsimd
            def _(pool):
                c = s.pool_c
                c.then(pool.memset(s.ident[:, :], 0.0))
                c.then(pool.memset(s.ones[:, :], 1.0))
                c.then(pool.memset(s.tri_le[:, :], 1.0))
                c.then(pool.memset(s.tri_ge[:, :], 1.0))
                c.wait(pool)
                pool.affine_select(out=s.ident[:, :], in_=s.ident[:, :], compare_op=ALU.not_equal, fill=1.0,
                                   base=0, pattern=[[-1, P]], channel_multiplier=1).then_inc(consts_set, 1)
                pool.affine_select(out=s.tri_le[:, :], in_=s.tri_le[:, :], compare_op=ALU.is_ge, fill=0.0,
                                   base=0, pattern=[[1, P]], channel_multiplier=-1).then_inc(consts_set, 1)
                pool.affine_select(out=s.tri_ge[:, :], in_=s.tri_ge[:, :], compare_op=ALU.is_ge, fill=0.0,
                                   base=0, pattern=[[-1, P]], channel_multiplier=1).then_inc(consts_set, 1)

            @block.tensor
            def _(pe):
                pe.wait_ge(consts_set, 3)
                pe.wait_ge(vecs_in, 16 * N_VEC)
                pe.transpose(s.bank[0][:, 0:P], v1[:, :], s.ident[:, :])
                pe.transpose(s.bank[0][:, 128:146], v2[:, :], s.ident[0:18, 0:18])
                pe.transpose(s.bank[0][:, 256:256 + TAPS * KC], v3[:, :],
                             s.ident[0:TAPS * KC, 0:TAPS * KC]).then_inc(vecs_turned, 1)
                pe.wait_ge(cond_ready, 1)
                pe.wait_ge(wada_in0, 16 * (KD // 2))
                for m in range(KD):
                    for k in range(KD):
                        last = pe.matmul(s.bank[COL_BANK[0]][:, 2 * m:2 * m + 2], wada[:, 0, k, m * P:(m + 1) * P], cond[:, k, :],
                                         start=(k == 0), stop=(k == KD - 1))
                last.then_inc(ada_done, 1)
                pe.wait_ge(part_ready, 1)
                for m in range(KD):
                    for j in range(2):
                        last = pe.matmul(s.bank[COL_BANK[1]][:, 16 + 2 * m + j:17 + 2 * m + j], part[:, j, m * P:(m + 1) * P], s.ones[:, 0:1],
                                         start=True, stop=True)
                last.then_inc(ada_done, 1)

            @block.scalar
            def _(act):
                act.wait_ge(vecs_ready, 1)
                act.activation(cond[:, :, :].rearrange("p k j -> p j k"),
                               s.vec2[:, 0:16].rearrange("p (j k) -> p j k", j=2), ACT.Silu).then_inc(cond_ready, 1)

            @block.vector
            def _(dve):
                c = s.dve_c
                dve.wait_ge(vecs_turned, 1)
                c.then(dve.tensor_copy(s.vec[:, :], s.bank[0][:, 0:P]))
                c.then(dve.tensor_copy(s.convw[:, :], s.bank[0][:, 256:256 + TAPS * KC]))
                dve.tensor_copy(s.vec2[:, :], s.bank[0][:, 128:146]).then_inc(vecs_ready, 1)
                dve.wait_ge(cond_ready, 1)
                for k in range(KD):
                    if k % 2 == 0:
                        dve.wait_ge(wada_in1[k // 2], 16)
                    c.wait(dve)
                    for j in range(2):
                        w, scale = wada[:, 1, k, :], cond[:, k, j:j + 1]
                        if k == 0:
                            c.then(dve.tensor_scalar(part[:, j, :], w, scale, None, ALU.mult))
                        else:
                            c.then(dve.scalar_tensor_tensor(part[:, j, :], w, scale, part[:, j, :], ALU.mult, ALU.add))
                c.wait(dve)
                dve.sem_inc(part_ready, 1)
                for i in range(2):
                    dve.wait_ge(ada_done, i + 1)
                    to = s.mod[:, i]
                    got = s.bank[COL_BANK[i]][:, 16 * i:16 * i + 16].rearrange("p (m j) -> p m j", j=2)
                    column = lambda v: s.vec[:, v:v + KD].rearrange("p (m o) -> p m o", o=1).to_broadcast([P, KD, 2])
                    c.link(dve, dve.tensor_tensor(to, got, column(8 * i), ALU.add))
                    if i == 1:
                        c.then(dve.scalar_tensor_tensor(to, to, 1.0, column(VEC["g_pre_mix"]), ALU.add, ALU.mult))


class LaterSections:

    TILES, KH = 8, KD // 2

    def __init__(self, s, at, slots, part, gain_row):
        self.s, self.at, self.slots, self.part, self.gain_row = s, at, slots, part, gain_row
        self.ada_in = [sem(s, f"ada_in{i}") for i in range(2)]
        self.rows_in, self.gain_in = sem(s, "ada_rows_in"), sem(s, "ada_gain_in")
        self.ada_used, self.finished = sem(s, "ada_used"), sem(s, "ada_finished")

    def load(self, pool):
        A, s = self.s.A, self.s
        src = A["w_ada"][0].rearrange("(h k p) n -> h p k n", p=P, h=2)
        for h in range(2):
            c0 = (2 + 3 * h) * D
            pool.dma_start(s.gpost[:, h, :], A["b_ada"][0:1, c0:c0 + D].to_broadcast([P, D])).then_inc(self.rows_in, 16)
        n_gain = 0
        for q in range(2 * self.TILES):
            j, kh = divmod(q, 2)
            if q >= 2:
                pool.wait_ge(self.ada_used, q - 1)
            c0 = 2 * D + j * 512
            pool.dma_start(self.slots[q % 2], src[kh][:, :, c0:c0 + 512]).then_inc(self.ada_in[q % 2], 16)
            if kh == 0 and (2 + j // 2) % 3 == 2:
                if n_gain:
                    pool.wait_ge(self.finished, n_gain if n_gain < 3 else self.TILES - 1)
                name = ("g_post_mix", "g_post_ffn")[n_gain // 2]
                pool.dma_start(self.gain_row[:, :], A[name][0:1, (j % 2) * 512:(j % 2) * 512 + 512].to_broadcast([P, 512])).then_inc(self.gain_in, 16)
                n_gain += 1

    def multiply(self, dve, q):
        s, c = self.s, self.s.dve_c
        j, kh = divmod(q, 2)
        dve.wait_ge(self.ada_in[q % 2], 16 * (q // 2 + 1))
        if kh == 0 and j >= 2:
            dve.wait_ge(self.tile_done, self.at[j - 2] + 1)
        to = self.part[:, j % 2, :]
        for k in range(self.KH):
            w, scale = self.slots[q % 2][:, k, :], s.cond[:, kh * self.KH + k, 0:1]
            if kh == 0 and k == 0:
                c.link(dve, dve.tensor_scalar(to, w, scale, None, ALU.mult))
            else:
                c.link(dve, dve.scalar_tensor_tensor(to, w, scale, to, ALU.mult, ALU.add))
        dve.sem_inc(self.ada_used, 1)

    def tensor(self, pe, j, bank):
        s = self.s
        pe.wait_ge(self.ada_used, 2 * (j + 1))
        if (2 + j // 2) % 3 == 2:
            return pe.matmul(bank[:, :], s.ones[:, :], self.part[:, j % 2, :], start=True, stop=True)
        for m in range(4):
            last = pe.matmul(bank[:, m:m + 1], self.part[:, j % 2, m * P:(m + 1) * P], s.ones[:, 0:1], start=True, stop=True)
        return last

    def finish(self, dve, j, bank):
        s, c = self.s, self.s.dve_c
        section, half = 2 + j // 2, j % 2
        if section % 3 == 2:
            h = section // 3
            dve.wait_ge(self.rows_in, 32)
            dve.wait_ge(self.gain_in, 16 * (2 * h + half + 1))
            to = s.gpost[:, h, half * 512:(half + 1) * 512]
            c.link(dve, dve.tensor_tensor(to, bank[:, :], to, ALU.add))
            c.link(dve, dve.tensor_tensor(to, to, self.gain_row[:, :], ALU.mult))
        else:
            col = lambda v: s.vec[:, v + 4 * half:v + 4 * half + 4]
            to = s.mod[:, section - 1, 4 * half:4 * half + 4, 0]
            c.link(dve, dve.tensor_tensor(to, bank[:, 0:4], col(8 * section), ALU.add))
            if section == 4:
                c.link(dve, dve.scalar_tensor_tensor(to, to, 1.0, col(VEC["g_pre_ffn"]), ALU.add, ALU.mult))
        dve.sem_inc(self.finished, 1)


def stage_norm(s, name, src, n_tiles, dst, gain, shift, loaded=None, rows_to=None, sums=None, keep=None):
    nc = s.nc
    G = min(4, n_tiles)
    with nc.sbuf_tensor(f"{name}_sq", [P, 2, D], F32) as sq, \
            nc.sbuf_tensor(f"{name}_xn", [P, n_tiles, D], F32) as xn, \
            nc.sbuf_tensor(f"{name}_ss", [P, n_tiles], F32) as ss, \
            nc.sbuf_tensor(f"{name}_rs", [P, n_tiles], F32) as rs:
        summed, inverted, rooted = sem(s, f"{name}_summed"), sem(s, f"{name}_inverted"), sem(s, f"{name}_rooted")
        normed, turned, moved_a, moved_v = (sem(s, f"{name}_{x}") for x in ("normed", "turned", "moved_a", "moved_v"))
        with nc.Block() as block:
            kept, src_kept = sem(s, f"{name}_kept"), sem(s, f"{name}_src_kept")

            @block.sync
            def _(sp):
                if keep is not None:
                    for t in range(n_tiles):
                        sp.dma_start(keep[t * P:(t + 1) * P, :], src[:, t, :]).then_inc(src_kept, 16)
                if rows_to is not None:
                    for t in range(n_tiles):
                        sp.wait_ge(normed, t + 1)
                        sp.dma_start(rows_to[t * P:(t + 1) * P, :], xn[:, t, :]).then_inc(kept, 16)
                    sp.wait_ge(kept, 16 * n_tiles)
                if keep is not None:
                    sp.wait_ge(src_kept, 16 * n_tiles)

            @block.scalar
            def _(act):
                if loaded is not None:
                    act.wait_ge(loaded, 16 * n_tiles)
                for t in range(n_tiles if sums is None else 0):
                    if t >= 2:
                        act.wait_ge(summed, t - 1)
                    act.activation(sq[:, t % 2, :], src[:, t, :], ACT.Square,
                                   accum_out=ss[:, t:t + 1]).then_inc(summed, 1)
                act.wait_ge(inverted, 1)
                act.activation(rs[:, :], ss[:, :], ACT.Sqrt).then_inc(rooted, 1)
                for i in range(1, KD * n_tiles // G, 2):
                    g, k = divmod(i, KD)
                    act.wait_ge(turned, i + 1)
                    act.activation(dst[:, k, g * G * P:(g + 1) * G * P], s.bank[i % 8][:, 0:G * P], ACT.Identity,
                                   scale=gain(k), bias=shift(k) if shift else 0.0).then_inc(moved_a, 1)

            @block.vector
            def _(dve):
                c = s.dve_c
                if sums is None:
                    dve.wait_ge(summed, n_tiles)
                c.link(dve, dve.tensor_scalar(ss[:, :], (ss if sums is None else sums)[:, :], 1.0 / D, EPS, ALU.mult, ALU.add))
                dve.reciprocal(ss[:, :], ss[:, :]).then_inc(inverted, 1)
                dve.wait_ge(rooted, 1)
                for t in range(n_tiles):
                    dve.tensor_scalar(xn[:, t, :], src[:, t, :], rs[:, t:t + 1], None, ALU.mult).then_inc(normed, 1)
                for i in range(0, KD * n_tiles // G, 2):
                    g, k = divmod(i, KD)
                    dve.wait_ge(turned, i + 1)
                    to, of = dst[:, k, g * G * P:(g + 1) * G * P], s.bank[i % 8][:, 0:G * P]
                    if shift:
                        dve.tensor_scalar(to, of, gain(k), shift(k), ALU.mult, ALU.add).then_inc(moved_v, 1)
                    else:
                        dve.tensor_scalar(to, of, gain(k), None, ALU.mult).then_inc(moved_v, 1)

            @block.tensor
            def _(pe):
                for i in range(KD * n_tiles // G):
                    g, k = divmod(i, KD)
                    if k == 0:
                        pe.wait_ge(normed, G * (g + 1))
                    if i >= 8:
                        pe.wait_ge((moved_v, moved_a)[i % 2], (i - 8) // 2 + 1)
                    for j in range(G):
                        last = pe.transpose(s.bank[i % 8][:, j * P:(j + 1) * P],
                                            xn[:, g * G + j, k * P:(k + 1) * P], s.ident[:, :])
                    last.then_inc(turned, 1)


def project_plan():
    plan = [("qk", m, n) for n in range(3) for m in range(4) if n < 2 or m >= 2]
    plan += [("v", t, 0) for t in range(STEPS)] + [("kt", t, 0) for t in range(STEPS)]
    plan += [("gt", t, 0) for t in range(STEPS)]
    plan += [("o", t, 0) for t in range(NT)]
    plan += [(kind, m, n) for m in range(KC) for n in range(2) for kind in ("gb", "ga")]
    for j, before in reversed(list(enumerate((8, 10, 12, 14, 16, 18, 42, 45)))):
        plan.insert(before, ("ada", j, 0))
    return plan


def stage_project(s):
    nc, A = s.nc, s.A
    plan = project_plan()
    by_act = ("kt", "gb")
    place = []
    count = {True: 0, False: 0}
    for kind, _, _ in plan:
        count[kind in by_act] += 1
        place.append(count[kind in by_act])
    first = {kind: min(i for i, p in enumerate(plan) if p[0] == kind) for kind in ("qk", "v", "kt", "gt", "o", "ga", "gb")}
    last_of = {kind: max(i for i, p in enumerate(plan) if p[0] == kind) for kind in ("qk", "v", "kt", "gt", "o", "ga", "gb")}
    with nc.sbuf_tensor("w_ring", [P, 2, KD, 512], F32) as ring:
        w_in = A["w_in"][0].rearrange("(k p) n -> p k n", p=P)
        biases_in, sig_free = sem(s, "biases_in"), sem(s, "sig_free")
        w_ready = {k: sem(s, f"w_{k}_in") for k in ("qk", "v", "gt", "o", "gab0", "gab1")}
        tile_done, moved_v, moved_a = sem(s, "proj_tile_done"), sem(s, "proj_moved_v"), sem(s, "proj_moved_a")
        o_added, sig_ready, pads_set = sem(s, "o_added"), sem(s, "sig_ready"), sem(s, "pads_set")
        b_v, b_o = s.x[:, 0, 0:512], s.x[:, 0, 512:1024]
        sig = s.x[:, 1, :].rearrange("p (b n) -> p b n", b=2)
        with nc.Block() as block, nc.sbuf_tensor("b_gt", [P, 2, N_GT], F32) as b_gt, \
                nc.sbuf_tensor("w_gt", [P, KD, N_GT], F32) as w_gt, \
                nc.sbuf_tensor("ada_slot", [P, KD // 2, 512], F32) as slot, nc.sbuf_tensor("ada_part", [P, 2, 512], F32) as part, \
                nc.sbuf_tensor("ada_gain", [P, 512], F32) as gain_row:
            at = [i for i, entry in enumerate(plan) if entry[0] == "ada"]
            spare = s.x[:, 2:4, :].rearrange("p t (a n) -> p (t a) n", n=512)
            later = LaterSections(s, at, (spare, slot[:, :, :]), part, gain_row)
            later.tile_done = tile_done
            parts_at = {at[j] - lead: 2 * j + kh for j in range(len(at)) for kh, lead in ((0, 2), (1, 1))}

            @block.sync
            def _(sp):
                def load(slot, c0, signal, to=0, n=512):
                    for k in range(0, KD, 4):
                        sp.dma_start(ring[:, slot, k:k + 4, to:to + n], w_in[:, k:k + 4, c0:c0 + n]).then_inc(signal, 16)
                load(0, C_QK, w_ready["qk"])
                load(1, C_V, w_ready["v"])
                sp.dma_start(w_gt[:, :, :], w_in[:, :, C_GT:C_GT + N_GT]).then_inc(w_ready["gt"], 16)
                sp.dma_start(b_v, A["b_in"][0:1, C_V:C_V + 512].to_broadcast([P, 512])).then_inc(biases_in, 16)
                sp.dma_start(b_o, A["b_in"][0:1, C_O:C_O + 512].to_broadcast([P, 512])).then_inc(biases_in, 16)
                sp.dma_start(b_gt[:, 0, :], A["b_in"][0:1, C_GT:C_GT + N_GT].to_broadcast([P, N_GT])).then_inc(biases_in, 16)
                sp.dma_start(b_gt[:, 1, :], A["b_gate"].rearrange("a b h -> a (b h)").to_broadcast([P, N_GT])).then_inc(biases_in, 16)
                sp.wait_ge(tile_done, last_of["qk"] + 1)
                load(0, C_O, w_ready["o"])
                sp.wait_ge(tile_done, last_of["v"] + 1)
                load(1, C_GA, w_ready["gab0"], 0, 256)
                load(1, C_GB, w_ready["gab0"], 256, 256)
                sp.wait_ge(tile_done, last_of["o"] + 1)
                load(0, C_GA + 256, w_ready["gab1"], 0, 256)
                load(0, C_GB + 256, w_ready["gab1"], 256, 256)

            @block.tensor
            def _(pe):
                for i, (kind, a, n) in enumerate(plan):
                    bank = s.bank[i % 8]
                    if i >= 8:
                        pe.wait_ge(moved_a if plan[i - 8][0] in by_act else moved_v, place[i - 8])
                    if kind in ("qk", "v", "gt", "o") and i == first[kind]:
                        pe.wait_ge(w_ready[kind], 16 if kind == "gt" else 32)
                    if (kind, n) == ("gb", 0) and a in (0, 2):
                        pe.wait_ge(w_ready[f"gab{a // 2}"], 64)
                    if kind == "ada":
                        last = later.tensor(pe, a, bank)
                    elif kind in ("v", "gt", "o"):
                        h = s.hcT[:, :, (a - NT) * P:(a - NT + 1) * P] if a >= NT else s.hT[:, :, a * P:(a + 1) * P]
                        w = w_gt[:, :, :] if kind == "gt" else ring[:, {"v": 1, "o": 0}[kind]]
                        for k in range(KD):
                            last = pe.matmul(bank[:, 0:N_GT if kind == "gt" else 512], h[:, k], w[:, k],
                                             start=(k == 0), stop=(k == KD - 1))
                    elif kind == "kt":
                        if i == first["kt"]:
                            pe.wait_ge(moved_v, place[last_of["qk"]])
                        for m in range(2):
                            last = pe.transpose(bank[:, m * P:(m + 1) * P], s.qkT[:, 2 + m, a * P:(a + 1) * P], s.ident[:, :])
                    else:
                        width = CTX if n == 2 else 512
                        h = s.hcT if n == 2 else s.hT[:, :, n * 512:(n + 1) * 512]
                        if kind == "qk":
                            w, c0 = ring[:, 0], a * P
                        else:
                            w, c0 = ring[:, 1 - a // 2], (a % 2) * P + (256 if kind == "gb" else 0)
                        for k in range(KD):
                            last = pe.matmul(bank[:, 0:width], w[:, k, c0:c0 + P], h[:, k, :],
                                             start=(k == 0), stop=(k == KD - 1))
                    last.then_inc(tile_done, 1)

            @block.vector
            def _(dve):
                dve.wait_ge(biases_in, 64)
                c = s.dve_c
                c.link(dve, dve.tensor_tensor(b_gt[:, 0, :], b_gt[:, 0, :], b_gt[:, 1, :], ALU.add))
                n_sig = 0
                for i, (kind, a, n) in enumerate(plan):
                    if i in parts_at:
                        later.multiply(dve, parts_at[i])
                    if kind in by_act:
                        continue
                    bank = s.bank[i % 8]
                    dve.wait_ge(tile_done, i + 1)
                    if kind == "ada":
                        later.finish(dve, a, bank)
                        dve.sem_inc(moved_v, 1)
                        continue
                    if kind == "qk":
                        width = CTX if n == 2 else 512
                        bias = s.vec[:, VEC["b_qk"] + a:VEC["b_qk"] + a + 1]
                        moved = dve.tensor_scalar(s.qkT[:, a, n * 512:n * 512 + width], bank[:, 0:width], bias,
                                                  DK ** -0.5 if a >= 2 else 1.0, ALU.add, ALU.mult)
                    elif kind == "v":
                        moved = dve.tensor_tensor(s.v_aug[:, a, :, 0:DV], bank[:, :].rearrange("p (h v) -> p h v", h=H1),
                                                  b_v.rearrange("p (h v) -> p h v", h=H1), ALU.add)
                    elif kind == "gt":
                        moved = dve.tensor_tensor(s.gates[:, a, :], bank[:, 0:N_GT], b_gt[:, 0, :], ALU.add)
                    elif kind == "o":
                        c.then(dve.tensor_tensor(s.sig_o[:, a, :], bank[:, :], b_o, ALU.add))
                        c.wait(dve)
                        moved = dve.sem_inc(moved_v, 1)
                        dve.sem_inc(o_added, 1)
                        continue
                    else:
                        if n_sig == 0:
                            dve.wait_ge(pads_set, 1)
                        dve.wait_ge(sig_ready, n_sig + 1)
                        bias = s.vec[:, VEC["b_gab"] + a:VEC["b_gab"] + a + 1]
                        to = s.upad[:, a, n * ROWS // 2:(n + 1) * ROWS // 2, PAD:PAD + GRID]
                        moved = dve.scalar_tensor_tensor(to, bank[:, :].rearrange("p (r w) -> p r w", w=GRID), bias,
                                                         sig[:, n_sig % 2, :].rearrange("p (r w) -> p r w", w=GRID),
                                                         ALU.add, ALU.mult)
                        n_sig += 1
                    moved.then_inc(moved_v, 1)

            @block.scalar
            def _(act):
                n_sig = 0
                for i, (kind, a, n) in enumerate(plan):
                    if kind == "o":
                        act.wait_ge(o_added, a + 1)
                        s.act_c.then(act.activation(s.sig_o[:, a, :], s.sig_o[:, a, :], ACT.Sigmoid))
                    if kind not in by_act:
                        continue
                    bank = s.bank[i % 8]
                    act.wait_ge(tile_done, i + 1)
                    if kind == "kt":
                        act.activation(s.k_tok[:, a, :], bank[:, 0:2 * P], ACT.Copy).then_inc(moved_a, 1)
                    else:
                        if n_sig >= 2:
                            act.wait_ge(moved_v, place[first["ga"]] + n_sig - 2)
                        bias = s.vec[:, VEC["b_gab"] + 4 + a:VEC["b_gab"] + 5 + a]
                        act.activation(sig[:, n_sig % 2, :], bank[:, :], ACT.Sigmoid, bias=bias).then_inc(moved_a, 1)
                        act.wait_ge(moved_a, place[i])
                        act.sem_inc(sig_ready, 1)
                        n_sig += 1

            @block.gpsimd
            def _(pool):
                c = s.pool_c
                c.then(pool.memset(s.v_aug[:, :, :, DV:DV + 1], 1.0))
                pool.memset(s.upad[:, :, :, :], 0.0).then_inc(pads_set, 1)
                later.load(pool)


def fwd_tile(j):
    return (j + NT) % STEPS


def bwd_tile(j):
    return STEPS - 1 - j


def stage_gates(s):
    nc = s.nc
    V = {n: nc.sbuf_tensor(f"g_{n}", [P, STEPS, 2, H1], F32) for n in ("LI", "FG", "AB", "MN", "BT", "TOT", "CM", "MT", "tmp", "tmp2")}
    with ExitStack() as ctx:
        V = {n: ctx.enter_context(v) for n, v in V.items()}
        ET = ctx.enter_context(nc.sbuf_tensor("g_ET", [NCOL, 3, P], F32))
        abs_ready, logs_ready, lf_ready, sums_done = (sem(s, f"g_{x}") for x in ("abs_ready", "logs_ready", "lf_ready", "sums_done"))
        e_ready, e_turned, e_max, scans_ready, scans_turned = (sem(s, f"g_{x}") for x in ("e_ready", "e_turned", "e_max", "scans_ready", "scans_turned"))
        mt_ready, mt_turned, exps_ready = (sem(s, f"g_{x}") for x in ("mt_ready", "mt_turned", "exps_ready"))
        flat = lambda t: t[:, :, :, :].rearrange("p j d h -> p (j d h)")
        s_of = lambda b, w=NCOL: b[:, 0:w]
        with nc.Block() as block:
            @block.vector
            def _(dve):
                c = s.dve_c
                G = s.gates
                for to, g0 in ((V["LI"], 0), (V["FG"], H1)):
                    c.then(dve.tensor_copy(to[:, 0:NC, 0, :], G[:, NT:STEPS, g0:g0 + H1]))
                    c.then(dve.tensor_copy(to[:, NC:STEPS, 0, :], G[:, 0:NT, g0:g0 + H1]))
                    for j in range(STEPS):
                        c.then(dve.tensor_copy(to[:, j, 1, :], G[:, bwd_tile(j), 2 * H1 + g0:3 * H1 + g0]))
                c.wait(dve)
                c.then(dve.tensor_scalar(flat(V["MN"]), flat(V["FG"]), 0.0, None, ALU.min))
                c.link(dve, dve.tensor_scalar(flat(V["AB"]), flat(V["FG"]), -1.0, None, ALU.mult))
                dve.tensor_tensor(flat(V["AB"]), flat(V["AB"]), flat(V["FG"]), ALU.max).then_inc(abs_ready, 1)
                dve.wait_ge(logs_ready, 1)
                dve.tensor_tensor(flat(V["FG"]), flat(V["MN"]), flat(V["AB"]), ALU.subtract).then_inc(lf_ready, 1)
                dve.wait_ge(sums_done, 1)
                for d in range(2):
                    got = s.bank[d][:, 0:NCOL].rearrange("p (j d h) -> p j d h", j=STEPS, d=2)
                    c.then(dve.tensor_copy(V["BT"][:, :, d, :], got[:, :, d, :]))
                c.then(dve.tensor_copy(flat(V["TOT"]), s.bank[2][:, 0:NCOL]))
                c.wait(dve)
                dve.tensor_tensor(flat(s.E), flat(V["LI"]), flat(V["BT"]), ALU.subtract).then_inc(e_ready, 1)
                dve.wait_ge(e_turned, 1)
                c.link(dve, dve.tensor_copy(ET[:, 0, :], s.bank[3][0:NCOL, 0:P]))
                dve.tensor_tensor_scan(ET[:, 1, :], ET[:, 0, :], ET[:, 0, :], NEG, ALU.max, ALU.max).then_inc(scans_ready, 1)
                dve.tensor_tensor_scan(ET[:, 2, ::-1], ET[:, 0, ::-1], ET[:, 0, ::-1], NEG, ALU.max, ALU.max).then_inc(scans_ready, 1)
                dve.wait_ge(scans_turned, 1)
                for d in range(2):
                    got = s.bank[4][:, d * P:d * P + NCOL].rearrange("p (j d h) -> p j d h", j=STEPS, d=2)
                    c.then(dve.tensor_copy(V["CM"][:, :, d, :], got[:, :, d, :]))
                c.link(dve, dve.memset(s.M[:, 0], 0.0))
                dve.wait_ge(e_max, 1)
                for j in range(STEPS):
                    c.link(dve, dve.tensor_tensor(s.MX[:, j], s.M[:, j], s.EM[:, j], ALU.max))
                    c.link(dve, dve.tensor_tensor(s.M[:, j + 1], V["TOT"][:, j], s.MX[:, j], ALU.add))
                M = s.M[:, 0:STEPS].rearrange("p j d h -> p (j d h)")
                c.link(dve, dve.tensor_tensor(flat(V["MT"]), M, flat(V["CM"]), ALU.max))
                c.link(dve, dve.tensor_scalar(flat(V["tmp"]), flat(V["MT"]), -1.0, None, ALU.mult))
                c.then(dve.tensor_tensor(flat(s.EI), M, flat(V["MT"]), ALU.subtract))
                c.then(dve.tensor_tensor(flat(s.EN), flat(V["tmp"]), flat(V["BT"]), ALU.subtract))
                c.then(dve.tensor_tensor(flat(s.WS), flat(s.E), flat(s.MX), ALU.subtract))
                c.then(dve.tensor_tensor(flat(s.EA), M, flat(s.MX), ALU.subtract))
                c.wait(dve)
                dve.sem_inc(mt_ready, 1)
                dve.wait_ge(mt_turned, 1)
                c.link(dve, dve.tensor_copy(s.NMT[:, :], s.bank[5][0:NCOL, 0:P]))
                dve.wait_ge(exps_ready, 4)

            @block.scalar
            def _(act):
                c = s.act_c
                act.wait_ge(abs_ready, 1)
                c.link(act, act.activation(flat(V["AB"]), flat(V["AB"]), ACT.Exp, scale=-1.0))
                act.activation(flat(V["AB"]), flat(V["AB"]), ACT.Ln, bias=1.0).then_inc(logs_ready, 1)
                act.wait_ge(mt_ready, 1)
                for t in (s.EI, s.EN, s.WS, s.EA):
                    act.activation(flat(t), flat(t), ACT.Exp).then_inc(exps_ready, 1)

            @block.tensor
            def _(pe):
                pe.wait_ge(lf_ready, 1)
                lf = flat(V["FG"])
                pe.matmul(s.bank[0][:, 0:NCOL], s.tri_le[:, :], lf, start=True, stop=True)
                pe.matmul(s.bank[1][:, 0:NCOL], s.tri_ge[:, :], lf, start=True, stop=True)
                pe.matmul(s.bank[2][:, 0:NCOL], s.ones[:, :], lf, start=True, stop=True).then_inc(sums_done, 1)
                pe.wait_ge(e_ready, 1)
                pe.transpose(s.bank[3][0:NCOL, 0:P], flat(s.E), s.ident[:, :]).then_inc(e_turned, 1)
                pe.wait_ge(scans_ready, 2)
                pe.transpose(s.bank[4][:, 0:NCOL], ET[:, 1, :], s.ident[0:NCOL, 0:NCOL])
                pe.transpose(s.bank[4][:, P:P + NCOL], ET[:, 2, :], s.ident[0:NCOL, 0:NCOL]).then_inc(scans_turned, 1)
                pe.wait_ge(mt_ready, 1)
                pe.transpose(s.bank[5][0:NCOL, 0:P], flat(V["tmp"]), s.ident[:, :]).then_inc(mt_turned, 1)

            @block.gpsimd
            def _(pool):
                pool.wait_ge(e_ready, 1)
                pool.partition_all_reduce(flat(s.EM), flat(s.E), P, bass.bass_isa.ReduceOp.max).then_inc(e_max, 1)


def mixer_inputs(s):
    nc, A = s.nc, s.A
    s.mixer = ExitStack()
    sb = lambda name, shape: s.mixer.enter_context(nc.sbuf_tensor(name, shape, F32))
    s.hcT = sb("hcT", [P, KD, CTX])
    with nc.sbuf_tensor("ctx_tok", [P, NC, D], F32) as ctx_tok:
        ctx_in = sem(s, "ctx_in")
        with nc.Block() as block:
            @block.sync
            def _(sp):
                for t in range(NC):
                    sp.dma_start(ctx_tok[:, t, :], A["ctx"][0, t * P:(t + 1) * P, :]).then_inc(ctx_in, 16)
        stage_norm(s, "norm_c", ctx_tok, NC, s.hcT, lambda k: s.mod[:, 1, k, 1:2], lambda k: s.mod[:, 0, k, 1:2], ctx_in)
    stage_norm(s, "norm_x", s.x, NT, s.hT, lambda k: s.mod[:, 1, k, 0:1], lambda k: s.mod[:, 0, k, 0:1], s.x_in)
    s.gates = sb("gates", [P, STEPS, N_GT])
    s.qkT = sb("qkT", [P, 4, T + CTX])
    s.k_tok = sb("k_tok", [P, STEPS, D_QK])
    s.v_aug = sb("v_aug", [P, STEPS, H1, DV + 1])
    s.sig_o = s.x[:, NT // 2:NT, :].rearrange("p t (a n) -> p (t a) n", a=2)
    s.upad = sb("upad", [P, KC, ROWS, GRID + 2 * PAD])
    stage_project(s)
    s.E, s.EM, s.MX, s.EI, s.EN, s.WS, s.EA = (sb(n, [P, STEPS, 2, H1]) for n in ("E", "EM", "MX", "EI", "EN", "WS", "EA"))
    s.M = sb("M", [P, STEPS + 1, 2, H1])
    s.NMT = sb("NMT", [NCOL, P])


def stage_mlstm(s):
    nc = s.nc
    units = [(j, d, h) for j in range(STEPS) for d in range(2) for h in range(H1)]
    U0 = NC * 2 * H1
    US = (STEPS - 1) * 2 * H1
    NV = len(units) - U0
    CONV = 2 * TAPS
    W = DV + 1
    s.h = s.x[:, 0:NT // 2, :].rearrange("p t (a n) -> p (t a) n", a=2)
    s.y = s.hT[:, KD // 2:KD, :]
    out_unit = lambda v: units[U0 + v]
    tile_of = lambda j, d: bwd_tile(j) if d else fwd_tile(j)
    with nc.sbuf_tensor("neg_mask", [P, 2, P], F32) as neg_mask, \
            nc.sbuf_tensor("dec", [P, 2, P], F32) as dec, nc.sbuf_tensor("pt", [P, 2, P], F32) as pt, \
            nc.sbuf_tensor("wv", [P, 2, W], F32) as wv, nc.sbuf_tensor("c_state", [P, 2, 2, W], F32) as state, \
            nc.sbuf_tensor("inter", [P, 2, W], F32) as inter, nc.sbuf_tensor("hsum", [P, 2, W], F32) as hsum, \
            nc.sbuf_tensor("dn", [P, 2, 2], F32) as dn, nc.sbuf_tensor("diag", [P, 2, P], F32) as diag:
        masks_set, scores_done, dec_ready, exp_ready, pt_ready = (sem(s, f"m_{x}") for x in ("masks_set", "scores_done", "dec_ready", "exp_ready", "pt_ready"))
        wv_ready, local_done, state_moved = (sem(s, f"m_{x}") for x in ("wv_ready", "local_done", "state_moved"))
        num_done, inter_ready, combined = (sem(s, f"m_{x}") for x in ("num_done", "inter_ready", "combined"))
        diag_ready, conv_done, conv_moved = (sem(s, f"m_{x}") for x in ("diag_ready", "conv_done", "conv_moved"))

        def lanes(h):
            return slice((h % 2) * DK, (h % 2) * DK + DK)

        with nc.Block() as block:
            @block.gpsimd
            def _(pool):
                c = s.pool_c
                c.link(pool, pool.memset(neg_mask[:, :, :], 0.0))
                pool.affine_select(out=neg_mask[:, 0, :], in_=neg_mask[:, 0, :], compare_op=ALU.is_ge, fill=NEG,
                                   base=0, pattern=[[1, P]], channel_multiplier=-1).then_inc(masks_set, 1)
                pool.affine_select(out=neg_mask[:, 1, :], in_=neg_mask[:, 1, :], compare_op=ALU.is_ge, fill=NEG,
                                   base=0, pattern=[[-1, P]], channel_multiplier=1).then_inc(masks_set, 1)
                for u, (j, d, h) in enumerate(units):
                    if u < US:
                        if u >= 2:
                            pool.wait_ge(local_done, u - 1)
                        pool.tensor_scalar(wv[:, u % 2, :], s.v_aug[:, tile_of(j, d), h, :], s.WS[:, j, d, h:h + 1],
                                           None, ALU.mult).then_inc(wv_ready, 1)
                    if u < CONV:
                        if u >= 2:
                            pool.wait_ge(conv_done, u - 1)
                        col = (u % TAPS) * KC + 2 + u // TAPS
                        pool.tensor_scalar(diag[:, u % 2, :], s.ident[:, :], s.convw[:, col:col + 1], None,
                                           ALU.mult).then_inc(diag_ready, 1)

            @block.tensor
            def _(pe):
                def scores(v):
                    j, d, h = out_unit(v)
                    t0 = tile_of(j, d) * P
                    if v >= 2:
                        pe.wait_ge(pt_ready, v - 1)
                    bank = s.bank[v % 2]
                    pe.matmul(bank[:, 0:P], s.qkT[lanes(h), 2 + h // 2, t0:t0 + P], s.qkT[lanes(h), h // 2, t0:t0 + P],
                              start=True, stop=True)
                    r = (j * 2 + d) * H1 + h
                    pe.matmul(bank[:, P:2 * P], s.ident[0:NCOL, r:r + 1].to_broadcast([NCOL, P]), s.NMT[:, :],
                              start=True, stop=True).then_inc(scores_done, 1)

                for u, (j, d, h) in enumerate(units):
                    v = u - U0
                    if v == -2:
                        scores(0)
                    if v == -1:
                        scores(1)
                    if u < US:
                        pe.wait_ge(wv_ready, u + 1)
                        if u >= 2:
                            pe.wait_ge(state_moved, u - 1)
                        pe.matmul(s.bank[4 + u % 2][lanes(h), 0:W], s.k_tok[:, tile_of(j, d), h * DK:(h + 1) * DK],
                                  wv[:, u % 2, :], start=True, stop=True).then_inc(local_done, 1)
                    if v >= 0:
                        t0 = tile_of(j, d) * P
                        bank = s.bank[2 + v % 2]
                        if v >= 2:
                            pe.wait_ge(combined, v - 1)
                        pe.wait_ge(state_moved, u - 2 * H1 + 1)
                        pe.matmul(bank[:, 256:256 + W], s.qkT[lanes(h), h // 2, t0:t0 + P], state[lanes(h), d, h // 2, :],
                                  start=True, stop=True)
                        pe.wait_ge(pt_ready, v + 1)
                        pe.matmul(bank[:, 0:W], pt[:, v % 2, :], s.v_aug[:, tile_of(j, d), h, :],
                                  start=True, stop=True).then_inc(num_done, 1)
                        if v + 2 < NV:
                            scores(v + 2)
                    if u < CONV:
                        m, tap = 2 + u // TAPS, u % TAPS
                        pe.wait_ge(diag_ready, u + 1)
                        if u == TAPS:
                            pe.wait_ge(conv_moved, 2)
                        for n in range(2):
                            rows = s.upad[:, m, n * ROWS // 2:(n + 1) * ROWS // 2, tap:tap + GRID]
                            last = pe.matmul(s.bank[6 + n][:, :].rearrange("p (r w) -> p r w", w=GRID), diag[:, u % 2, :], rows,
                                             start=(tap == 0), stop=(tap == TAPS - 1))
                        last.then_inc(conv_done, 1)

            @block.scalar
            def _(act):
                def exp(v):
                    act.wait_ge(dec_ready, v + 1)
                    act.activation(dec[:, v % 2, :], dec[:, v % 2, :], ACT.Exp).then_inc(exp_ready, 1)

                def conv_out(m):
                    act.wait_ge(conv_done, TAPS * (m - 1))
                    bias = s.vec[:, VEC["conv_b"] + m:VEC["conv_b"] + m + 1]
                    for n in range(2):
                        act.activation(s.y[:, m, n * 512:(n + 1) * 512], s.bank[6 + n][:, :], ACT.Identity,
                                       bias=bias).then_inc(conv_moved, 1)

                for u, (j, d, h) in enumerate(units):
                    v = u - U0
                    if 0 <= v + 1 < NV:
                        exp(v + 1)
                    if v >= 0:
                        act.wait_ge(num_done, v + 1)
                        if v >= 2:
                            act.wait_ge(combined, v - 1)
                        act.activation(inter[:, v % 2, :], s.bank[2 + v % 2][:, 256:256 + W], ACT.Copy,
                                       scale=s.EI[:, j, d, h:h + 1]).then_inc(inter_ready, 1)
                    if u in (TAPS - 1, CONV - 1):
                        conv_out(2 + u // TAPS)

            @block.vector
            def _(dve):
                c = s.dve_c
                c.link(dve, dve.memset(state[:, :, :, :], 0.0))
                dve.wait_ge(masks_set, 2)

                def decay(v):
                    j, d, h = out_unit(v)
                    dve.wait_ge(scores_done, v + 1)
                    dve.scalar_tensor_tensor(dec[:, v % 2, :], s.bank[v % 2][:, P:2 * P], s.E[:, j, d, h:h + 1],
                                             neg_mask[:, d, :], ALU.add, ALU.add).then_inc(dec_ready, 1)

                def weights(v):
                    dve.wait_ge(exp_ready, v + 1)
                    if v >= 2:
                        dve.wait_ge(num_done, v - 1)
                    dve.tensor_tensor(pt[:, v % 2, :], s.bank[v % 2][:, 0:P], dec[:, v % 2, :], ALU.mult).then_inc(pt_ready, 1)

                for u, (j, d, h) in enumerate(units):
                    v = u - U0
                    if 0 <= v + 1 < NV:
                        decay(v + 1)
                    if u < CONV:
                        m, tap = u % 2, u // 2
                        w = s.convw[:, tap * KC + m:tap * KC + m + 1]
                        rows = s.upad[:, m, :, tap:tap + GRID]
                        to = s.y[:, m, :].rearrange("p (r w) -> p r w", w=GRID)
                        if tap == 0:
                            c.then(dve.tensor_scalar(to, rows, w, s.vec[:, VEC["conv_b"] + m:VEC["conv_b"] + m + 1],
                                                     ALU.mult, ALU.add))
                        else:
                            c.wait(dve)
                            c.then(dve.scalar_tensor_tensor(to, rows, w, to, ALU.mult, ALU.add))
                    if 0 <= v + 1 < NV:
                        weights(v + 1)
                    if v >= 0:
                        dve.wait_ge(inter_ready, v + 1)
                        H = hsum[:, v % 2, :]
                        dve.tensor_tensor(H, s.bank[2 + v % 2][:, 0:W], inter[:, v % 2, :], ALU.add).then_inc(combined, 1)
                        dve.wait_ge(combined, v + 1)
                        c.link(dve, dve.tensor_scalar(dn[:, v % 2, 0:1], H[:, DV:W], -1.0, s.EN[:, j, d, h:h + 1],
                                                      ALU.mult, ALU.max))
                        c.link(dve, dve.tensor_tensor(dn[:, v % 2, 0:1], dn[:, v % 2, 0:1], H[:, DV:W], ALU.max))
                        c.link(dve, dve.reciprocal(dn[:, v % 2, 1:2], dn[:, v % 2, 0:1]))
                        t = tile_of(j, d)
                        to = s.h[:, t, h * DV:(h + 1) * DV]
                        first = j < (bwd_tile(t) if not d else t + NC)
                        if first:
                            c.then(dve.tensor_scalar(to, H[:, 0:DV], dn[:, v % 2, 1:2], None, ALU.mult))
                        else:
                            c.then(dve.scalar_tensor_tensor(to, H[:, 0:DV], dn[:, v % 2, 1:2], to, ALU.mult, ALU.add))
                    if u < US:
                        dve.wait_ge(local_done, u + 1)
                        C = state[lanes(h), d, h // 2, :]
                        dve.scalar_tensor_tensor(C, C, s.EA[lanes(h), j, d, h:h + 1], s.bank[4 + u % 2][lanes(h), 0:W],
                                                 ALU.mult, ALU.add).then_inc(state_moved, 1)


def stage_mix(s):
    nc, A = s.nc, s.A
    N = 512
    with nc.sbuf_tensor("sqh", [P, NT, D_V], F32) as sqh, nc.sbuf_tensor("norm_g", [P, D_V], F32) as norm_g, \
            nc.sbuf_tensor("hs", [P, NT * H1], F32) as hs, nc.sbuf_tensor("sqy", [P, KC, T], F32) as sqy, \
            nc.sbuf_tensor("rstd_y", [P, T], F32) as rstd_y:
        ng_in, sq_ready, gate_ready, h_inv, h_root = (sem(s, f"x_{x}") for x in ("ng_in", "sq_ready", "gate_ready", "h_inv", "h_root"))
        h_ready, turned, moved_v, moved_a = (sem(s, f"x_{x}") for x in ("h_ready", "turned", "moved_v", "moved_a"))
        mean_done, centred, squared, var_done, y_inv, y_root, y_ready = (sem(s, f"x_{x}") for x in ("mean_done", "centred", "squared", "var_done", "y_inv", "y_root", "y_ready"))
        with nc.Block() as block:
            @block.sync
            def _(sp):
                sp.dma_start(norm_g[:, :], A["mlstm_norm_g"].rearrange("a h v -> a (h v)").to_broadcast([P, D_V])).then_inc(ng_in, 16)

            @block.gpsimd
            def _(pool):
                pool.tensor_tensor(sqh[:, :, :], s.h, s.h, ALU.mult).then_inc(sq_ready, 1)
                pool.wait_ge(ng_in, 16)
                for t in range(NT):
                    pool.tensor_tensor(s.sig_o[:, t, :], s.sig_o[:, t, :], norm_g[:, :], ALU.mult).then_inc(gate_ready, 1)

            @block.tensor
            def _(pe):
                for n in range(2):
                    for m in range(KC):
                        last = pe.matmul(s.bank[n][:, :], s.ones[:, :], s.y[:, m, n * N:(n + 1) * N],
                                         start=(m == 0), stop=(m == KC - 1))
                last.then_inc(mean_done, 1)
                for n in range(2):
                    for m in range(KC):
                        pe.wait_ge(squared, n * KC + m + 1)
                        last = pe.matmul(s.bank[2 + n][:, :], s.ones[:, :], sqy[:, m, n * N:(n + 1) * N],
                                         start=(m == 0), stop=(m == KC - 1))
                    last.then_inc(var_done, 1)
                for i in range(2 * H1):
                    g, k = divmod(i, H1)
                    if k == 0:
                        pe.wait_ge(h_ready, 4 * H1 * (g + 1))
                    if i >= 4:
                        pe.wait_ge((moved_v, moved_a)[i % 2], (i - 4) // 2 + 1)
                    for t in range(4):
                        last = pe.transpose(s.bank[4 + i % 4][:, t * P:(t + 1) * P], s.h[:, g * 4 + t, k * P:(k + 1) * P], s.ident[:, :])
                    last.then_inc(turned, 1)

            @block.vector
            def _(dve):
                c = s.dve_c
                dve.wait_ge(mean_done, 1)
                for n in range(2):
                    for m in range(KC):
                        y = s.y[:, m, n * N:(n + 1) * N]
                        dve.scalar_tensor_tensor(y, s.bank[n][:, :], -1.0 / D_CONV, y, ALU.mult, ALU.add).then_inc(centred, 1)
                dve.wait_ge(sq_ready, 1)
                c.link(dve, dve.tensor_reduce(hs[:, :], sqh[:, :, :].rearrange("p t (h v) -> p (t h) v", h=H1), AX_X, ALU.add))
                c.link(dve, dve.tensor_scalar(hs[:, :], hs[:, :], 1.0 / DV, EPS, ALU.mult, ALU.add))
                dve.reciprocal(hs[:, :], hs[:, :]).then_inc(h_inv, 1)
                dve.wait_ge(var_done, 2)
                for n in range(2):
                    r = rstd_y[:, n * N:(n + 1) * N]
                    c.link(dve, dve.tensor_scalar(r, s.bank[2 + n][:, :], 1.0 / D_CONV, EPS, ALU.mult, ALU.add))
                    dve.reciprocal(r, r).then_inc(y_inv, 1)
                dve.wait_ge(h_root, 1)
                for t in range(NT):
                    dve.wait_ge(gate_ready, t + 1)
                    for h in range(H1):
                        cols = slice(h * DV, (h + 1) * DV)
                        dve.scalar_tensor_tensor(s.h[:, t, cols], s.h[:, t, cols], hs[:, t * H1 + h:t * H1 + h + 1],
                                                 s.sig_o[:, t, cols], ALU.mult, ALU.mult).then_inc(h_ready, 1)
                dve.wait_ge(y_root, 1)
                for n in range(2):
                    for m in range(KC):
                        y = s.y[:, m, n * N:(n + 1) * N]
                        dve.tensor_tensor(y, y, rstd_y[:, n * N:(n + 1) * N], ALU.mult).then_inc(y_ready, 1)
                for i in range(0, 2 * H1, 2):
                    g, k = divmod(i, H1)
                    dve.wait_ge(turned, i + 1)
                    dve.tensor_copy(s.hT[:, k, g * N:(g + 1) * N], s.bank[4 + i % 4][:, :]).then_inc(moved_v, 1)

            @block.scalar
            def _(act):
                for n in range(2):
                    for m in range(KC):
                        act.wait_ge(centred, n * KC + m + 1)
                        act.activation(sqy[:, m, n * N:(n + 1) * N], s.y[:, m, n * N:(n + 1) * N], ACT.Square).then_inc(squared, 1)
                act.wait_ge(h_inv, 1)
                act.activation(hs[:, :], hs[:, :], ACT.Sqrt).then_inc(h_root, 1)
                act.wait_ge(y_inv, 2)
                act.activation(rstd_y[:, :], rstd_y[:, :], ACT.Sqrt).then_inc(y_root, 1)
                for i in range(1, 2 * H1, 2):
                    g, k = divmod(i, H1)
                    act.wait_ge(turned, i + 1)
                    act.activation(s.hT[:, k, g * N:(g + 1) * N], s.bank[4 + i % 4][:, :], ACT.Copy).then_inc(moved_a, 1)
                for n in range(2):
                    for m in range(KC):
                        act.wait_ge(y_ready, n * KC + m + 1)
                        y = s.y[:, m, n * N:(n + 1) * N]
                        g, b = VEC["conv_ln_g"] + m, VEC["conv_ln_b"] + m
                        s.act_c.then(act.activation(y, y, ACT.Silu, scale=s.vec[:, g:g + 1], bias=s.vec[:, b:b + 1]))


class Post:

    def __init__(self, s, name, y, post, stack, loaded=None):
        self.s, self.y, self.gain, self.loaded = s, y, s.gpost[:, post, :], loaded
        self.slots = y.shape[1]
        self.sq = stack.enter_context(s.nc.sbuf_tensor(f"{name}_psq", [P, 2, D], F32))
        self.ss = stack.enter_context(s.nc.sbuf_tensor(f"{name}_pss", [P, NT], F32))
        self.summed, self.inverted, self.rooted, self.scaled, self.x_summed = (
            sem(s, f"{name}_p_{x}") for x in ("summed", "inverted", "rooted", "scaled", "x_summed"))
        self.added = [sem(s, f"{name}_p_added_{x}") for x in ("v", "p")]

    def scalar(self, act, t):
        one = self.ss[:, t:t + 1]
        act.activation(self.sq[:, 0, :], self.y[:, t % self.slots, :], ACT.Square, accum_out=one).then_inc(self.summed, 1)
        act.wait_ge(self.inverted, t + 1)
        act.activation(one, one, ACT.Sqrt).then_inc(self.rooted, 1)

    def sum_x(self, act, t):
        act.wait_ge(self.added[t % 2], t // 2 + 1)
        if t >= 1:
            act.wait_ge(self.x_summed, t)
        act.activation(self.sq[:, 1, :], self.s.x[:, t, :], ACT.Square, accum_out=self.s.x_sums[:, t:t + 1]).then_inc(self.x_summed, 1)

    def add(self, eng, t):
        if self.loaded and t < 2:
            eng.wait_ge(*self.loaded)
        eng.wait_ge(self.scaled, t + 1)
        x = self.s.x[:, t, :]
        eng.tensor_tensor(x, x, self.y[:, t % self.slots, :], ALU.add).then_inc(self.added[t % 2], 1)

    def vector(self, dve, t):
        one = self.ss[:, t:t + 1]
        dve.wait_ge(self.summed, t + 1)
        self.s.dve_c.link(dve, dve.tensor_scalar(one, one, 1.0 / D, EPS, ALU.mult, ALU.add))
        dve.reciprocal(one, one).then_inc(self.inverted, 1)
        dve.wait_ge(self.rooted, t + 1)
        y = self.y[:, t % self.slots, :]
        dve.scalar_tensor_tensor(y, y, one, self.gain, ALU.mult, ALU.mult).then_inc(self.scaled, 1)
        if t % 2 == 0:
            self.add(dve, t)

    def gpsimd(self, pool):
        for t in range(1, NT, 2):
            self.add(pool, t)


def stage_out(s, name, src_T, src_low, w_src, post, x_src=None, bias_src=None, src_high=None):
    nc = s.nc
    with ExitStack() as stack:
        sb = lambda n, shape: stack.enter_context(nc.sbuf_tensor(f"{name}_{n}", shape, F32))
        with nc.sbuf_tensor(f"{name}_w_low", [P, KD, D], F32) as w_low:
            pass
        w, w_high = sb("w", [P, KD, D]), sb("w_high", [P, KD, D])
        SLOTS = 4 if post is not None else 1
        y = sb("y", [P, SLOTS, D])
        if src_high is None:
            src_high = sb("src_high", [P, KD, T])
        b = sb("b", [P, D]) if bias_src is not None else None
        sq = sb("sq", [P, D]) if post is None else None
        w_in = [sem(s, f"{name}_w_in{i}") for i in range(KD // 2)]
        b_in, x_in = sem(s, f"{name}_b_in"), sem(s, f"{name}_x_in")
        done, moved, x_summed = sem(s, f"{name}_done"), sem(s, f"{name}_moved"), sem(s, f"{name}_x_summed")
        w_cut, w_ready, src_cut = sem(s, f"{name}_w_cut"), sem(s, f"{name}_w_ready"), sem(s, f"{name}_src_cut")
        src_ready = [sem(s, f"{name}_src_ready_{x}") for x in ("v", "p")]
        R = lambda ap: ap.bitcast(F32R)
        inline = Post(s, name, y, post, stack, (x_in, 16 * NT)) if post is not None else None

        def src_part(eng, k):
            eng.wait_ge(src_cut, k + 1)
            eng.tensor_tensor(R(src_low[:, k, :]), src_T[:, k, :], src_high[:, k, :], ALU.subtract).then_inc(src_ready[k % 2], 1)

        with nc.Block() as block:
            @block.sync
            def _(sp):
                src = w_src.rearrange("(k p) n -> p k n", p=P)
                for k in range(0, KD, 2):
                    sp.dma_start(w[:, k:k + 2, :], src[:, k:k + 2, :]).then_inc(w_in[k // 2], 16)
                if bias_src is not None:
                    sp.dma_start(b[:, :], bias_src.to_broadcast([P, D])).then_inc(b_in, 16)
                if x_src is not None:
                    for t in range(NT):
                        sp.dma_start(s.x[:, t, :], x_src[t * P:(t + 1) * P, :]).then_inc(x_in, 16)
                    sp.wait_ge(x_in, 16 * NT)

            @block.tensor
            def _(pe):
                for i in range(2 * NT):
                    t, n = divmod(i, 2)
                    if i >= 8:
                        pe.wait_ge(moved, i - 7)
                    for k in range(KD):
                        if i == 0:
                            pe.wait_ge(w_ready, k // 2 + 1)
                            pe.wait_ge(src_ready[k % 2], k // 2 + 1)
                        to = s.bank[i % 8]
                        rows, cols = slice(t * P, (t + 1) * P), slice(n * 512, (n + 1) * 512)
                        pe.matmul(to, R(src_high[:, k, rows]), R(w_high[:, k, cols]), start=(k == 0), stop=False)
                        pe.matmul(to, R(src_high[:, k, rows]), R(w_low[:, k, cols]), start=False, stop=False)
                        last = pe.matmul(to, R(src_low[:, k, rows]), R(w_high[:, k, cols]), start=False, stop=(k == KD - 1))
                    last.then_inc(done, 1)

            @block.scalar
            def _(act):
                for k in range(KD):
                    act.activation(R(src_high[:, k, :]), src_T[:, k, :], ACT.Copy).then_inc(src_cut, 1)
                    if k % 2 == 1:
                        act.wait_ge(w_in[k // 2], 16)
                        act.activation(R(w_high[:, k - 1:k + 1, :]), w[:, k - 1:k + 1, :], ACT.Copy).then_inc(w_cut, 1)
                for t in range(NT):
                    act.wait_ge(moved, 2 * (t + 1))
                    if inline:
                        inline.scalar(act, t)
                        if t >= 1:
                            inline.sum_x(act, t - 1)
                    else:
                        if t >= 1:
                            act.wait_ge(x_summed, t)
                        act.activation(sq[:, :], s.x[:, t, :], ACT.Square, accum_out=s.x_sums[:, t:t + 1]).then_inc(x_summed, 1)
                if inline:
                    inline.sum_x(act, NT - 1)

            @block.gpsimd
            def _(pool):
                for k in range(1, KD, 2):
                    src_part(pool, k)
                if inline:
                    inline.gpsimd(pool)

            @block.vector
            def _(dve):
                for k in range(0, KD, 2):
                    src_part(dve, k)
                    dve.wait_ge(w_cut, k // 2 + 1)
                    dve.tensor_tensor(R(w_low[:, k:k + 2, :]), w[:, k:k + 2, :], w_high[:, k:k + 2, :], ALU.subtract).then_inc(w_ready, 1)
                if bias_src is not None:
                    dve.wait_ge(b_in, 16)
                elif x_src is not None:
                    dve.wait_ge(x_in, 16 * NT)
                for i in range(2 * NT):
                    t, n = divmod(i, 2)
                    dve.wait_ge(done, i + 1)
                    if inline and n == 0 and t >= SLOTS:
                        dve.wait_ge(inline.added[t % 2], (t - SLOTS) // 2 + 1)
                    cols = slice(n * 512, (n + 1) * 512)
                    other = b[:, cols] if bias_src is not None else s.x[:, t, cols]
                    to = y[:, t % SLOTS, cols] if post is not None else s.x[:, t, cols]
                    dve.tensor_tensor(to, s.bank[i % 8][:, :], other, ALU.add).then_inc(moved, 1)
                    if inline and n == 1 and t >= 1:
                        inline.vector(dve, t - 1)
                if inline:
                    inline.vector(dve, NT - 1)


class Moe:

    def __init__(self, s, name, E, K, F):
        self.name, self.E, self.K, self.F = name, E, K, F
        self.NB = T * K // P + E
        nc = s.nc
        self.rows = nc.dram_tensor(f"{name}_rows", (T, D), F32, kind="Internal").ap()
        self.acc = nc.dram_tensor(f"{name}_acc", (T + P, D), F32, kind="Internal").ap()
        self.table = nc.dram_tensor(f"{name}_table", (self.NB * P, 3), F32, kind="Internal").ap()

    N_LOAD = 5

    def hold_weights(self, s, buffers, w_gate, w_up, w_down):
        tensor = lambda n, shape: buffers.enter_context(s.nc.sbuf_tensor(f"{self.name}_{n}", shape, F32))
        KF = self.F // P
        self.wg, self.wu, self.wd = tensor("wg", [P, 2, KD, self.F]), tensor("wu", [P, 2, KD, self.F]), tensor("wd", [P, 2, KF, D])
        self.w_ready = [sem(s, f"{self.name}_w_ready{b}") for b in range(2)]
        self.sources = (w_gate, w_up, w_down)

    def load(self, sp, e, b):
        w_gate, w_up, w_down = self.sources
        for k in range(0, KD, 4):
            for to, src in ((self.wg, w_gate), (self.wu, w_up)):
                sp.dma_start(to[:, b, k:k + 4, :], src[bass.ds(e, 1), k * P:(k + 4) * P, :].rearrange("o (k p) f -> p (o k) f", p=P)).then_inc(self.w_ready[b], 16)
        sp.dma_start(self.wd[:, b, :, :], w_down[bass.ds(e, 1), :, :].rearrange("o (k p) d -> p (o k) d", p=P)).then_inc(self.w_ready[b], 16)


def stage_route1(s, mo, gate, mask, shared):
    nc, A = s.nc, s.A
    E = mo.E
    with nc.sbuf_tensor("w_router", [P, KD, E], F32) as w, nc.sbuf_tensor("b_router", [P, E], F32) as b, \
            nc.sbuf_tensor("score", [P, NT, E], F32) as score, nc.sbuf_tensor("biased", [P, NT, E], F32) as biased, \
            nc.sbuf_tensor("rest", [P, NT, E], F32) as rest, nc.sbuf_tensor("top", [P, NT, 8], F32) as top, \
            nc.sbuf_tensor("wsum", [P, NT], F32) as wsum:
        w_in, logits_done, scored = sem(s, "r_w_in"), sem(s, "r_logits_done"), sem(s, "r_scored")
        with nc.Block() as block:
            @block.sync
            def _(sp):
                sp.dma_start(w[:, :, :], A["w_router"][0].rearrange("(k p) e -> p k e", p=P)).then_inc(w_in, 16)
                sp.dma_start(b[:, :], A["b_router"][0:1, :].to_broadcast([P, E])).then_inc(w_in, 16)
                shared.load(sp)

            @block.tensor
            def _(pe):
                pe.wait_ge(w_in, 32)
                for t in range(NT):
                    for k in range(KD):
                        last = pe.matmul(s.bank[0][:, t * E:(t + 1) * E], s.hT[:, k, t * P:(t + 1) * P], w[:, k, :],
                                         start=(k == 0), stop=(k == KD - 1))
                last.then_inc(logits_done, 1)

            @block.scalar
            def _(act):
                act.wait_ge(logits_done, 1)
                act.activation(score[:, :, :], s.bank[0][:, :].rearrange("p (t e) -> p t e", e=E), ACT.Sigmoid).then_inc(scored, 1)

            @block.vector
            def _(dve):
                c = s.dve_c
                dve.wait_ge(w_in, 32)
                dve.wait_ge(scored, 1)
                for t in range(NT):
                    c.link(dve, dve.tensor_tensor(biased[:, t, :], score[:, t, :], b[:, :], ALU.add))
                    c.link(dve, dve.max(top[:, t, :], biased[:, t, :]))
                    c.then(dve.match_replace(out=rest[:, t, :], in_to_replace=top[:, t, :], in_values=biased[:, t, :], imm_value=NEG))
                c.wait(dve)
                c.link(dve, dve.tensor_tensor(mask[:, :, :], rest[:, :, :], biased[:, :, :], ALU.not_equal))
                c.link(dve, dve.tensor_tensor(gate[:, :, :], score[:, :, :], mask[:, :, :], ALU.mult))
                c.link(dve, dve.tensor_reduce(wsum[:, :], gate[:, :, :], AX_X, ALU.add))
                c.link(dve, dve.reciprocal(wsum[:, :], wsum[:, :]))
                for t in range(NT):
                    c.then(dve.tensor_scalar(gate[:, t, :], gate[:, t, :], wsum[:, t:t + 1], ROUTE_SCALE, ALU.mult, ALU.mult))
                c.wait(dve)


def stage_dispatch(s, mo, gate, mask, start, idx_g, idx_s, row_w, side=None):
    nc = s.nc
    E, K, NB, name = mo.E, mo.K, mo.NB, mo.name
    with nc.sbuf_tensor(f"{name}_key", [P, NT, E], F32) as key, nc.sbuf_tensor(f"{name}_blocks", [P, E], F32) as blocks, \
            nc.sbuf_tensor(f"{name}_before", [P, NT + 1, E], F32) as before, nc.sbuf_tensor(f"{name}_ends", [P, E + 1], F32) as ends, \
            nc.sbuf_tensor(f"{name}_base", [P, E], F32) as base, nc.sbuf_tensor(f"{name}_keys", [P, NT, 8], F32) as keys, \
            nc.sbuf_tensor(f"{name}_dest", [P, NT, K], I32) as dest, nc.sbuf_tensor(f"{name}_pair", [P, NT, K, 3], F32) as pair, \
            nc.sbuf_tensor(f"{name}_hit", [P, E], F32) as hit, nc.sbuf_tensor(f"{name}_tok_i", [P, NT], I32) as tok_i, \
            nc.sbuf_tensor(f"{name}_empty_i", [P, P], I32) as empty_i, nc.sbuf_tensor(f"{name}_empty", [P, P, 3], F32) as empty, \
            nc.sbuf_tensor(f"{name}_back", [P, P, 3], F32) as back:
        ranks_done, keys_ready, empty_ready, table_set = (sem(s, f"{name}_{x}") for x in ("ranks_done", "keys_ready", "empty_ready", "table_set"))
        scattered, read_back, turned, iotas = (sem(s, f"{name}_{x}") for x in ("scattered", "read_back", "tab_turned", "iotas"))
        with nc.Block() as block:
            @block.gpsimd
            def _(pool):
                pool.iota(tok_i[:, :], pattern=[[P, NT]], base=0, channel_multiplier=1).then_inc(iotas, 1)
                pool.iota(empty_i[:, :], pattern=[[1, P]], base=T, channel_multiplier=0).then_inc(iotas, 1)
                pool.wait_ge(table_set, 16)
                for t in range(NT):
                    pool.wait_ge(keys_ready, t + 1)
                    for k in range(K):
                        pool.indirect_dma_start(mo.table, bass.IndirectOffsetOnAxis(ap=dest[:, t, k:k + 1], axis=0),
                                                pair[:, t, k, :], None, bounds_check=NB * P - 1).then_inc(scattered, 16)

            @block.sync
            def _(sp):
                sp.wait_ge(empty_ready, 1)
                sp.dma_start(mo.table.rearrange("(b s) c -> b (s c)", s=P),
                             empty[0:NB, :, :].rearrange("b s c -> b (s c)")).then_inc(table_set, 16)
                for e in range(2):
                    mo.load(sp, e, e)
                if side:
                    side.store(sp)
                sp.wait_ge(scattered, 16 * NT * K)
                sp.dma_start(back[0:NB, :, :].rearrange("b s c -> b (s c)"),
                             mo.table.rearrange("(b s) c -> b (s c)", s=P)).then_inc(read_back, 16)

            @block.tensor
            def _(pe):
                pe.matmul(s.bank[0][:, 0:NT * E], s.tri_le[:, :], mask[:, :, :].rearrange("p t e -> p (t e)"), start=True, stop=True)
                pe.matmul(s.bank[1][:, 0:NT * E], s.ones[:, :], mask[:, :, :].rearrange("p t e -> p (t e)"), start=True, stop=True).then_inc(ranks_done, 1)
                if side:
                    side.tensor(pe)
                pe.wait_ge(read_back, 16)
                for c in range(3):
                    last = pe.transpose(s.bank[2][:, c * P:c * P + NB], back[0:NB, :, c], s.ident[0:NB, 0:NB])
                last.then_inc(turned, 1)

            @block.scalar
            def _(act):
                if side:
                    side.scalar(act)

            @block.vector
            def _(dve):
                c = s.dve_c
                dve.wait_ge(iotas, 2)
                c.then(dve.memset(empty[:, :, 0:3:2], 0.0))
                for col in range(2):
                    for k in range(K):
                        c.then(dve.tensor_copy(pair[:, :, k, col], tok_i[:, :]))
                c.wait(dve)
                dve.tensor_copy(empty[:, :, 1], empty_i[:, :]).then_inc(empty_ready, 1)
                dve.wait_ge(ranks_done, 1)
                c.then(dve.memset(ends[:, 0:1], 0.0))
                c.then(dve.memset(blocks[:, :], 1.0))
                c.then(dve.memset(before[:, 0, :], 0.0))
                c.link(dve, dve.tensor_copy(before[:, 1:NT + 1, :], s.bank[1][:, 0:NT * E].rearrange("p (t e) -> p t e", t=NT)))
                for t in range(2, NT + 1):
                    c.link(dve, dve.tensor_tensor(before[:, t, :], before[:, t, :], before[:, t - 1, :], ALU.add))
                for j in range(1, NT):
                    c.link(dve, dve.scalar_tensor_tensor(blocks[:, :], before[:, NT, :], float(j * P), blocks[:, :], ALU.is_gt, ALU.add))
                c.link(dve, dve.tensor_tensor_scan(ends[:, 1:E + 1], s.ones[:, 0:E], blocks[:, :], 0.0, ALU.mult, ALU.add))
                c.then(dve.tensor_copy(start[:, :], ends[:, :]))
                c.link(dve, dve.tensor_scalar(base[:, :], ends[:, 0:E], float(P), None, ALU.mult))
                tiles = [P, NT, E]
                c.link(dve, dve.tensor_tensor(before[:, 0:NT, :], before[:, 0:NT, :], base[:, :].rearrange("p (o e) -> p o e", o=1).to_broadcast(tiles), ALU.add))
                c.link(dve, dve.tensor_tensor(key[:, :, :], s.bank[0][:, 0:NT * E].rearrange("p (t e) -> p t e", t=NT), before[:, 0:NT, :], ALU.add))
                c.link(dve, dve.tensor_tensor(key[:, :, :], key[:, :, :], mask[:, :, :], ALU.mult))
                for t in range(NT):
                    c.link(dve, dve.max(keys[:, t, :], key[:, t, :]))
                    c.then(dve.tensor_scalar(dest[:, t, :], keys[:, t, 0:K], -1.0, None, ALU.add))
                    for k in range(K):
                        c.link(dve, dve.scalar_tensor_tensor(hit[:, :], key[:, t, :], keys[:, t, k:k + 1], gate[:, t, :],
                                                             ALU.is_equal, ALU.mult, accum_out=pair[:, t, k, 2:3]))
                    dve.sem_inc(keys_ready, 1)
                if side:
                    side.vector(dve)
                dve.wait_ge(turned, 1)
                c.then(dve.memset(idx_g[:, NB:NB + 2], 0))
                c.then(dve.tensor_copy(idx_g[:, 0:NB], s.bank[2][:, 0:NB]))
                c.then(dve.tensor_copy(idx_s[:, :], s.bank[2][:, P:P + NB]))
                c.then(dve.tensor_copy(row_w[:, :], s.bank[2][:, 2 * P:2 * P + NB]))
                c.wait(dve)


def stage_experts(s, mo, start, idx_g, idx_s, row_w, gain, shift):
    nc = s.nc
    E, F, NB, name = mo.E, mo.F, mo.NB, mo.name
    KF = F // P
    wg_sb, wu_sb, wd_sb, w_ready = mo.wg, mo.wu, mo.wd, mo.w_ready
    with nc.sbuf_tensor(f"{name}_xg", [P, D], F32) as xg, \
            nc.sbuf_tensor(f"{name}_xgT", [P, KD, P], F32) as xgT, nc.sbuf_tensor(f"{name}_silu", [P, KF, P], F32) as silu, \
            nc.sbuf_tensor(f"{name}_hidT", [P, KF, P], F32) as hidT, nc.sbuf_tensor(f"{name}_y_blk", [P, D], F32) as y_blk, \
            nc.sbuf_tensor(f"{name}_ig_now", [P, 1], I32) as ig_now, nc.sbuf_tensor(f"{name}_is_now", [P, 1], I32) as is_now:
        gathered, turned, xt_ready_v, xt_ready_a = (sem(s, f"{name}_{x}") for x in ("gathered", "turned", "xt_ready_v", "xt_ready_a"))
        gu_done, silu_ready, hid_ready, down_done = (sem(s, f"{name}_{x}") for x in ("gu_done", "silu_ready", "hid_ready", "down_done"))
        y_ready_v, y_ready_a, added, ig_set, is_set, ig_seen, y_zero = (sem(s, f"{name}_{x}") for x in ("y_ready_v", "y_ready_a", "added", "ig_set", "is_set", "ig_seen", "y_zero"))
        HEAD = 1
        bx = [s.bank[0], s.bank[1]]
        bg, bu = s.bank[2:4], s.bank[4:6]
        by = s.bank[6:8]

        def first_block(eng, e):
            return eng.value_load(start[0:1, bass.ds(e, 1)], min_val=0, max_val=NB)

        def blocks_of(eng, e, body):
            lo = first_block(eng, e)
            hi = first_block(eng, e + 1)
            with eng.Fori(lo, hi) as g:
                body(g)

        with nc.Block() as block:
            @block.sync
            def _(sp):
                with sp.Fori(1, E // 2) as ep:
                    for b in range(2):
                        sp.wait_ge(down_done, first_block(sp, 2 * ep + b - 1) + HEAD)
                        mo.load(sp, 2 * ep + b, b)

            @block.gpsimd
            def _(pool):
                def gather(g):
                    pool.tensor_copy(ig_now[:, :], idx_g[:, bass.ds(g, 1)]).then_inc(ig_set, 1)
                    pool.wait_ge(ig_set, g + 1)
                    pool.sem_inc(ig_seen, 1)
                    pool.indirect_dma_start(xg[:, :], None, mo.rows, bass.IndirectOffsetOnAxis(ap=ig_now[:, 0:1], axis=0)).then_inc(gathered, 16)

                def follow(g):
                    pool.wait_ge(turned, g + 1)
                    pool.wait_ge(gathered, 16 * (g + 1))
                    gather(g + 1)

                def one(g):
                    follow(g + 1)
                    pool.wait_ge(added, 16 * (g + 1))
                    pool.tensor_copy(is_now[:, :], idx_s[:, bass.ds(g, 1)]).then_inc(is_set, 1)
                    pool.wait_ge(is_set, 1)
                    pool.wait_ge(is_set, g + 1)
                    pool.wait_ge(y_ready_v, g + 1 + HEAD)
                    pool.wait_ge(y_ready_a, g + 1 + HEAD)
                    pool.indirect_dma_start(mo.acc, bass.IndirectOffsetOnAxis(ap=is_now[:, 0:1], axis=0), y_blk[:, :], None,
                                            compute_op=ALU.add).then_inc(added, 16)

                pool.memset(y_blk[:, :], 0.0).then_inc(y_zero, 1)
                pool.wait_ge(y_zero, 1)
                pool.dma_start(mo.acc[T:T + P, :], y_blk[:, :]).then_inc(added, 16)
                gather(0)
                follow(0)
                with pool.Fori(0, E) as e:
                    blocks_of(pool, e, one)
                end = first_block(pool, E)
                pool.wait_ge(gathered, 16 * (end + 2))
                pool.wait_ge(added, 16 * (end + 1))

            @block.tensor
            def _(pe):
                for counter in (gu_done, down_done):
                    pe.sem_inc(counter, HEAD)

                def turn(g):
                    pe.wait_ge(gathered, 16 * (g + 1))
                    pe.wait_ge(xt_ready_v, 4 * g + HEAD)
                    pe.wait_ge(xt_ready_a, 4 * g + HEAD)
                    for k in range(KD):
                        last = pe.transpose(bx[k % 2][:, (k // 2) * P:(k // 2 + 1) * P], xg[:, k * P:(k + 1) * P], s.ident[:, :])
                    last.then_inc(turned, 1)

                def one(g, b, ep):
                    pe.wait_ge(w_ready[b], 16 * mo.N_LOAD * (ep + 1))
                    pe.wait_ge(xt_ready_v, 4 * (g + 1) + HEAD)
                    pe.wait_ge(xt_ready_a, 4 * (g + 1) + HEAD)
                    for f in range(KF):
                        pe.wait_ge(hid_ready, KF * g + HEAD)
                        for w, to in ((wg_sb, bg[f]), (wu_sb, bu[f])):
                            for k in range(KD):
                                last = pe.matmul(to[:, 0:P], w[:, b, k, f * P:(f + 1) * P], xgT[:, k, :],
                                                 start=(k == 0), stop=(k == KD - 1))
                            last.then_inc(gu_done, 1)
                    turn(g + 1)
                    pe.wait_ge(hid_ready, KF * (g + 1) + HEAD)
                    pe.wait_ge(y_ready_v, g + HEAD)
                    pe.wait_ge(y_ready_a, g + HEAD)
                    for n in range(2):
                        for f in range(KF):
                            last = pe.matmul(by[n][:, :], hidT[:, f, :], wd_sb[:, b, f, n * 512:(n + 1) * 512],
                                             start=(f == 0), stop=(f == KF - 1))
                    last.then_inc(down_done, 1)

                turn(0)
                with pe.Fori(0, E // 2) as ep:
                    for b in range(2):
                        blocks_of(pe, 2 * ep + b, lambda g, b=b: one(g, b, ep))

            @block.scalar
            def _(act):
                for counter in (xt_ready_a, y_ready_a):
                    act.sem_inc(counter, HEAD)

                def take(g):
                    act.wait_ge(turned, g + 1)
                    act.wait_ge(gu_done, 2 * KF * g + HEAD)
                    for k in range(1, KD, 2):
                        act.activation(xgT[:, k, :], bx[1][:, (k // 2) * P:(k // 2 + 1) * P], ACT.Identity, scale=gain(k),
                                       bias=shift(k) if shift else 0.0).then_inc(xt_ready_a, 1)

                def one(g):
                    for f in range(KF):
                        act.wait_ge(gu_done, 2 * KF * g + 2 * f + 1 + HEAD)
                        act.wait_ge(hid_ready, KF * g + HEAD)
                        act.activation(silu[:, f, :], bg[f][:, 0:P], ACT.Silu).then_inc(silu_ready, 1)
                    take(g + 1)
                    act.wait_ge(down_done, g + 1 + HEAD)
                    act.wait_ge(added, 16 * (g + 1))
                    act.activation(y_blk[:, 512:D], by[1][:, :], ACT.Copy, scale=row_w[:, bass.ds(g, 1)]).then_inc(y_ready_a, 1)

                take(0)
                with act.Fori(0, E) as e:
                    blocks_of(act, e, one)

            @block.vector
            def _(dve):
                for counter in (xt_ready_v, y_ready_v, hid_ready):
                    dve.sem_inc(counter, HEAD)

                def take(g):
                    dve.wait_ge(turned, g + 1)
                    dve.wait_ge(gu_done, 2 * KF * g + HEAD)
                    for k in range(0, KD, 2):
                        of = bx[0][:, (k // 2) * P:(k // 2 + 1) * P]
                        if shift:
                            dve.tensor_scalar(xgT[:, k, :], of, gain(k), shift(k), ALU.mult, ALU.add).then_inc(xt_ready_v, 1)
                        else:
                            dve.tensor_scalar(xgT[:, k, :], of, gain(k), None, ALU.mult).then_inc(xt_ready_v, 1)

                def one(g):
                    for f in range(KF):
                        dve.wait_ge(gu_done, 2 * KF * g + 2 * f + 2 + HEAD)
                        dve.wait_ge(silu_ready, KF * g + f + 1)
                        dve.wait_ge(down_done, g + HEAD)
                        dve.tensor_tensor(hidT[:, f, :], bu[f][:, 0:P], silu[:, f, :], ALU.mult).then_inc(hid_ready, 1)
                    take(g + 1)
                    dve.wait_ge(down_done, g + 1 + HEAD)
                    dve.wait_ge(added, 16 * (g + 1))
                    dve.tensor_scalar(y_blk[:, 0:512], by[0][:, :], row_w[:, bass.ds(g, 1)], None, ALU.mult).then_inc(y_ready_v, 1)

                take(0)
                with dve.Fori(0, E) as e:
                    blocks_of(dve, e, one)


class Shared:

    KF, Y = F1 // P, 4

    def __init__(self, s, mo, buffers):
        tensor = lambda n, shape: buffers.enter_context(s.nc.sbuf_tensor(n, shape, F32))
        self.s, self.mo = s, mo
        self.ws, self.wsd = tensor("ws", [P, 2, KD, F1]), tensor("wsd", [P, self.KF, D])
        self.silu, self.hid, self.y = tensor("sh_silu", [P, 2, 512]), tensor("sh_hid", [P, self.KF, T]), tensor("sh_y", [P, self.Y, D])
        self.w_in, self.gu_done, self.silu_ready, self.hid_ready, self.down_done, self.moved = (
            sem(s, f"sh_{x}") for x in ("w_in", "gu_done", "silu_ready", "hid_ready", "down_done", "moved"))
        self.stored = [sem(s, f"sh_stored{i}") for i in range(self.Y)]

    def load(self, sp):
        A = self.s.A
        for i, n in enumerate(("ws_gate", "ws_up")):
            src = A[n][0].rearrange("(k p) f -> p k f", p=P)
            for k in range(0, KD, 4):
                sp.dma_start(self.ws[:, i, k:k + 4, :], src[:, k:k + 4, :]).then_inc(self.w_in, 16)
        sp.dma_start(self.wsd[:, :, :], A["ws_down"][0].rearrange("(k p) d -> p k d", p=P)).then_inc(self.w_in, 16)

    def store(self, sp):
        for t in range(NT):
            sp.wait_ge(self.moved, 2 * (t + 1))
            sp.dma_start(self.mo.acc[t * P:(t + 1) * P, :], self.y[:, t % self.Y, :]).then_inc(self.stored[t % self.Y], 16)
        for slot in range(self.Y):
            sp.wait_ge(self.stored[slot], 16 * NT // self.Y)

    def tensor(self, pe):
        s, KF = self.s, self.KF
        pe.wait_ge(self.w_in, 80)
        for i in range(2 * KF):
            n, f = divmod(i, KF)
            if i >= 2:
                pe.wait_ge(self.hid_ready, i - 1)
            for g in range(2):
                for k in range(KD):
                    last = pe.matmul(s.bank[2 + 2 * (i % 2) + g], self.ws[:, g, k, f * P:(f + 1) * P], s.hT[:, k, n * 512:(n + 1) * 512],
                                     start=(k == 0), stop=(k == KD - 1))
                last.then_inc(self.gu_done, 1)
        for i in range(2 * NT):
            t, n = divmod(i, 2)
            if t % 4 == 0:
                pe.wait_ge(self.hid_ready, KF * (t // 4 + 1))
            if i >= 2:
                pe.wait_ge(self.moved, i - 1)
            for f in range(KF):
                last = pe.matmul(s.bank[6 + i % 2], self.hid[:, f, t * P:(t + 1) * P], self.wsd[:, f, n * 512:(n + 1) * 512],
                                 start=(f == 0), stop=(f == KF - 1))
            last.then_inc(self.down_done, 1)

    def scalar(self, act):
        for i in range(2 * self.KF):
            act.wait_ge(self.gu_done, 2 * i + 1)
            if i >= 2:
                act.wait_ge(self.hid_ready, i - 1)
            act.activation(self.silu[:, i % 2, :], self.s.bank[2 + 2 * (i % 2)], ACT.Silu).then_inc(self.silu_ready, 1)

    def vector(self, dve):
        for i in range(2 * self.KF):
            n, f = divmod(i, self.KF)
            dve.wait_ge(self.gu_done, 2 * i + 2)
            dve.wait_ge(self.silu_ready, i + 1)
            dve.tensor_tensor(self.hid[:, f, n * 512:(n + 1) * 512], self.s.bank[3 + 2 * (i % 2)], self.silu[:, i % 2, :],
                              ALU.mult).then_inc(self.hid_ready, 1)
        for i in range(2 * NT):
            t, n = divmod(i, 2)
            dve.wait_ge(self.down_done, i + 1)
            if t >= self.Y:
                dve.wait_ge(self.stored[t % self.Y], 16 * (t // self.Y))
            dve.tensor_copy(self.y[:, t % self.Y, n * 512:(n + 1) * 512], self.s.bank[6 + i % 2]).then_inc(self.moved, 1)


def ffn1(s):
    nc, A = s.nc, s.A
    mo = Moe(s, "moe1", E1, TOP1, F1)
    gain, shift = (lambda k: s.mod[:, 3, k, 0:1]), (lambda k: s.mod[:, 2, k, 0:1])
    stage_norm(s, "norm_f", s.x, NT, s.hT, gain, shift, rows_to=mo.rows, sums=s.x_sums)
    with ExitStack() as tables:
        tab = lambda name, shape, dt: tables.enter_context(nc.sbuf_tensor(name, shape, dt))
        start = tab("start1", [P, mo.E + 1], I32)
        idx_g, idx_s = tab("idx_g1", [P, mo.NB + 2], I32), tab("idx_s1", [P, mo.NB], I32)
        row_w = tab("row_w1", [P, mo.NB], F32)
        mo.hold_weights(s, tables, A["we_gate"][0], A["we_up"][0], A["we_down"][0])
        with ExitStack() as routing:
            gate, mask = (routing.enter_context(nc.sbuf_tensor(n, [P, NT, mo.E], F32)) for n in ("gate1", "mask1"))
            shared = Shared(s, mo, routing)
            stage_route1(s, mo, gate, mask, shared)
            stage_dispatch(s, mo, gate, mask, start, idx_g, idx_s, row_w, shared)
        stage_experts(s, mo, start, idx_g, idx_s, row_w, gain, shift)
    with ExitStack() as stack:
        acc = stack.enter_context(nc.sbuf_tensor("acc_tok", [P, NT, D], F32))
        acc_in = [sem(s, f"acc1_in{t}") for t in range(NT)]
        post = Post(s, "post_f", acc, 1, stack)
        with nc.Block() as block:
            @block.sync
            def _(sp):
                for t in range(NT):
                    sp.dma_start(acc[:, t, :], mo.acc[t * P:(t + 1) * P, :]).then_inc(acc_in[t], 16)

            @block.scalar
            def _(act):
                for t in range(NT):
                    act.wait_ge(acc_in[t], 16)
                    post.scalar(act, t)
                    if t >= 1:
                        post.sum_x(act, t - 1)
                post.sum_x(act, NT - 1)

            @block.gpsimd
            def _(pool):
                post.gpsimd(pool)

            @block.vector
            def _(dve):
                for t in range(NT):
                    post.vector(dve, t)


H2, HD = 8, 64
D_A = H2 * HD
C2_U, C2_GATE = 3 * D_A, 3 * D_A + 512
CHUNK2 = 64
BACK = 8 * CHUNK2
KEYS = BACK + P
FUTURE, MAX_REL = CHUNK2 - 1, 256
N_REL = FUTURE + MAX_REL + 1
REXT = P - 1 + KEYS
GRP, SG, SP_ = 32, 16, 64
GG = GRP // 2
L2 = 8
NCH = T // L2
NG2, EPG, E2, TOP2, F2 = 4, 4, 16, 2, 256
BIG = 3.0e38
TWO_PI = (6.28125, 0.0019350051879882812, 3.019916050561733e-07)
ROUND = 12582912.0


class RelativeBias:

    LO = P - 1 - FUTURE

    def __init__(self, s, stack):
        self.s = s
        self.ext = s.nc.dram_tensor("rel_ext", (H2, REXT + 1), F32, kind="Internal")
        self.tile = stack.enter_context(s.nc.sbuf_tensor("bias2", [P, H2, KEYS], F32))
        self.row = stack.enter_context(s.nc.sbuf_tensor("rext", [H2, REXT + 1], F32))
        self.rel_in, self.ext_ready, self.stored, self.loaded = (sem(s, f"b_{x}") for x in ("rel_in", "ext_ready", "stored", "loaded"))

    def load(self, sp):
        sp.dma_start(self.row[:, self.LO:self.LO + N_REL], self.s.A["rel_bias_2"][0]).then_inc(self.rel_in, 16)

    def spread(self, sp):
        sp.wait_ge(self.ext_ready, 2)
        sp.dma_start(self.ext.ap(), self.row[:, :]).then_inc(self.stored, 16)
        sp.wait_ge(self.stored, 16)
        src = self.ext.ap()
        for h in range(H2):
            view = bass.AP(src.tensor, h * (REXT + 1), [[1, P], [1, KEYS]])
            sp.dma_start(self.tile[:, h, :], view).then_inc(self.loaded, 16)

    def extend(self, dve):
        row, lo, hi = self.row, self.LO, self.LO + N_REL
        dve.wait_ge(self.rel_in, 16)
        dve.tensor_copy(row[:, 0:lo], row[:, lo:lo + 1].to_broadcast([H2, lo])).then_inc(self.ext_ready, 1)
        dve.tensor_copy(row[:, hi:REXT + 1], row[:, hi - 1:hi].to_broadcast([H2, REXT + 1 - hi])).then_inc(self.ext_ready, 1)

    def mask(self, dve):
        dve.wait_ge(self.loaded, 16 * H2)
        self.s.dve_c.then(dve.memset(self.tile[0:CHUNK2, :, 0:CHUNK2], NEG))
        self.s.dve_c.then(dve.memset(self.tile[CHUNK2:P, :, KEYS - CHUNK2:KEYS], NEG))


def stage_qkv(s, qT, kT, v_tok, q_tok, k_tok, bias):
    nc, A = s.nc, s.A
    w_src = A["w_in_2"][0].rearrange("(k p) n -> p k n", p=P)
    toks = (q_tok, k_tok, v_tok)
    with nc.sbuf_tensor("w2_ring", [P, 2, KD, 512], F32) as ring, nc.sbuf_tensor("qk_ss", [P, 2, NT * H2], F32) as ss:
        w_ready = [sem(s, f"a_w{i}") for i in range(3)]
        done, copied_v, copied_a, squared, inverted, rooted = (sem(s, f"a_{x}") for x in ("done", "copied_v", "copied_a", "squared", "inverted", "rooted"))
        normed, turned, moved_v, moved_a = (sem(s, f"a_{x}") for x in ("normed", "turned", "moved_v", "moved_a"))
        sq = (qT, kT)
        flat = lambda x: x[:, :, :].rearrange("p a b -> p (a b)")
        with nc.Block() as block:
            @block.sync
            def _(sp):
                bias.load(sp)
                for i in range(3):
                    if i == 2:
                        bias.spread(sp)
                        sp.wait_ge(done, NT)
                    for k in range(0, KD, 4):
                        sp.dma_start(ring[:, i % 2, k:k + 4, :], w_src[:, k:k + 4, i * 512:(i + 1) * 512]).then_inc(w_ready[i], 16)

            @block.tensor
            def _(pe):
                for i in range(3 * NT):
                    g, t = divmod(i, NT)
                    if t == 0:
                        pe.wait_ge(w_ready[g], 32)
                    if i >= 4:
                        pe.wait_ge((copied_v, copied_a)[i % 2], (i - 4) // 2 + 1)
                    for k in range(KD):
                        last = pe.matmul(s.bank[i % 4], s.hT[:, k, t * P:(t + 1) * P], ring[:, g % 2, k, :],
                                         start=(k == 0), stop=(k == KD - 1))
                    last.then_inc(done, 1)
                for i in range(16):
                    g, m, n = i // 8, (i % 8) // 2, i % 2
                    if i % 8 == 0:
                        pe.wait_ge(normed, g + 1)
                    if i >= 4:
                        pe.wait_ge((moved_v, moved_a)[i % 2], (i - 4) // 2 + 1)
                    for t in range(4):
                        last = pe.transpose(s.bank[4 + i % 4][:, t * P:(t + 1) * P], toks[g][:, n * 4 + t, m * P:(m + 1) * P], s.ident[:, :])
                    last.then_inc(turned, 1)

            @block.gpsimd
            def _(pool):
                for g in range(2):
                    pool.wait_ge(copied_v, NT // 2 * (g + 1))
                    pool.wait_ge(copied_a, NT // 2 * (g + 1))
                    pool.tensor_tensor(flat(sq[g]), flat(toks[g]), flat(toks[g]), ALU.mult).then_inc(squared, 1)

            @block.vector
            def _(dve):
                c = s.dve_c

                def copies(g):
                    for t in range(0, NT, 2):
                        dve.wait_ge(done, g * NT + t + 1)
                        dve.tensor_copy(toks[g][:, t, :], s.bank[(g * NT + t) % 4]).then_inc(copied_v, 1)

                def norms(g):
                    dve.wait_ge(squared, g + 1)
                    c.link(dve, dve.tensor_reduce(ss[:, g, :], flat(sq[g]).rearrange("p (a e) -> p a e", e=HD), AX_X, ALU.add))
                    c.link(dve, dve.tensor_scalar(ss[:, g, :], ss[:, g, :], 1.0 / HD, EPS, ALU.mult, ALU.add))
                    dve.reciprocal(ss[:, g, :], ss[:, g, :]).then_inc(inverted, 1)
                    dve.wait_ge(rooted, g + 1)
                    x = flat(toks[g]).rearrange("p (a e) -> p a e", e=HD)
                    r = ss[:, g, :].rearrange("p (a o) -> p a o", o=1).to_broadcast([P, NT * H2, HD])
                    dve.tensor_tensor(x, x, r, ALU.mult).then_inc(normed, 1)

                bias.extend(dve)
                copies(0)
                bias.mask(dve)
                copies(1)
                norms(0)
                copies(2)
                norms(1)
                for i in range(0, 16, 2):
                    g, m, n = i // 8, (i % 8) // 2, i % 2
                    dve.wait_ge(turned, i + 1)
                    dve.tensor_scalar((qT, kT)[g][:, m, n * 512:(n + 1) * 512], s.bank[4 + i % 4], s.vec2[:, 16 + g:17 + g],
                                      HD ** -0.5 if g == 0 else 1.0, ALU.mult, ALU.mult).then_inc(moved_v, 1)

            @block.scalar
            def _(act):
                def copies(g):
                    for t in range(1, NT, 2):
                        act.wait_ge(done, g * NT + t + 1)
                        act.activation(toks[g][:, t, :], s.bank[(g * NT + t) % 4], ACT.Copy).then_inc(copied_a, 1)

                copies(0)
                copies(1)
                act.wait_ge(inverted, 1)
                act.activation(ss[:, 0, :], ss[:, 0, :], ACT.Sqrt).then_inc(rooted, 1)
                copies(2)
                act.wait_ge(inverted, 2)
                act.activation(ss[:, 1, :], ss[:, 1, :], ACT.Sqrt).then_inc(rooted, 1)
                act.activation(s.gain_q[:, :], s.vec2[:, 16:17], ACT.Copy, scale=HD ** -0.5).then_inc(s.gain_q_set, 1)
                act.wait_ge(s.gain_q_set, 1)
                for i in range(1, 16, 2):
                    g, m, n = i // 8, (i % 8) // 2, i % 2
                    act.wait_ge(turned, i + 1)
                    act.activation((qT, kT)[g][:, m, n * 512:(n + 1) * 512], s.bank[4 + i % 4], ACT.Copy,
                                   scale=s.gain_q[:, :] if g == 0 else s.vec2[:, 17:18]).then_inc(moved_a, 1)


def stage_attention(s, qT, kT, v_tok, bias, y_tok, yT):
    nc = s.nc
    units = [(i, h) for i in range(NT) for h in range(H2)]
    NU = len(units)
    with nc.sbuf_tensor("lg", [P, 2, KEYS], F32) as lg, nc.sbuf_tensor("pr", [P, 2, KEYS], F32) as pr, \
            nc.sbuf_tensor("prT", [P, 2, KEYS], F32) as prT, nc.sbuf_tensor("mx", [P, 2, 4], F32) as mx:
        scored, biased, maxed, exped, turned, moved, attended, taken = (sem(s, f"t_{x}") for x in ("scored", "biased", "maxed", "exped", "turned", "moved", "attended", "taken"))
        y_turned, y_moved = sem(s, "t_y_turned"), sem(s, "t_y_moved")

        def span(i):
            n = min(i + 1, KEYS // P) * P
            return n, (i + 1) * P - n

        with nc.Block() as block:
            @block.tensor
            def _(pe):
                def score(u):
                    i, h = units[u]
                    n, k0 = span(i)
                    lanes = slice((h % 2) * HD, (h % 2) * HD + HD)
                    if u >= 2:
                        pe.wait_ge(biased, u - 1)
                    for a in range(0, n, 512):
                        w = min(512, n - a)
                        last = pe.matmul(s.bank[2 * (u % 2) + a // 512][:, 0:w], qT[lanes, h // 2, i * P:(i + 1) * P],
                                         kT[lanes, h // 2, k0 + a:k0 + a + w], start=True, stop=True)
                    last.then_inc(scored, 1)

                score(0)
                score(1)
                for u, (i, h) in enumerate(units):
                    n, k0 = span(i)
                    pe.wait_ge(exped, u + 1)
                    if u >= 1:
                        pe.wait_ge(moved, u)
                    for a in range(n // P):
                        last = pe.transpose(s.psum[:, 4 * 512 + a * P:4 * 512 + (a + 1) * P], pr[:, u % 2, a * P:(a + 1) * P], s.ident[:, :])
                    last.then_inc(turned, 1)
                    if u + 2 < NU:
                        score(u + 2)
                    pe.wait_ge(moved, u + 1)
                    if u >= 2:
                        pe.wait_ge(taken, u - 1)
                    for a in range(n // P):
                        last = pe.matmul(s.bank[6 + u % 2][:, 0:HD], prT[:, u % 2, a * P:(a + 1) * P], v_tok[:, k0 // P + a, h * HD:(h + 1) * HD],
                                         start=(a == 0), stop=(a == n // P - 1))
                    last.then_inc(attended, 1)
                pe.wait_ge(taken, NU)
                for i in range(8):
                    m, n = divmod(i, 2)
                    if i >= 4:
                        pe.wait_ge(y_moved, i - 3)
                    for t in range(4):
                        last = pe.transpose(s.bank[i % 4][:, t * P:(t + 1) * P], y_tok[:, n * 4 + t, m * P:(m + 1) * P], s.ident[:, :])
                    last.then_inc(y_turned, 1)

            @block.vector
            def _(dve):
                c = s.dve_c

                def logits(u):
                    i, h = units[u]
                    n, _ = span(i)
                    dve.wait_ge(scored, u + 1)
                    if u >= 2:
                        dve.wait_ge(exped, u - 1)
                    b = bias[:, h, 0:n][:, ::-1]
                    o = 1024 * (u % 2)
                    dve.tensor_tensor(lg[:, u % 2, 0:n], s.psum[:, o:o + n], b, ALU.add).then_inc(biased, 1)
                    dve.wait_ge(biased, u + 1)
                    dve.tensor_reduce(mx[:, u % 2, 0:1], lg[:, u % 2, 0:n], AX_X, ALU.max, negate=True).then_inc(maxed, 1)

                logits(0)
                for u, (i, h) in enumerate(units):
                    if u + 1 < NU:
                        logits(u + 1)
                    dve.wait_ge(exped, u + 1)
                    c.link(dve, dve.reciprocal(mx[:, u % 2, 2:3], mx[:, u % 2, 1:2]))
                    dve.wait_ge(attended, u + 1)
                    dve.tensor_scalar(y_tok[:, i, h * HD:(h + 1) * HD], s.bank[6 + u % 2][:, 0:HD], mx[:, u % 2, 2:3], None,
                                      ALU.mult).then_inc(taken, 1)
                for i in range(8):
                    m, n = divmod(i, 2)
                    dve.wait_ge(y_turned, i + 1)
                    dve.tensor_copy(yT[:, m, n * 512:(n + 1) * 512], s.bank[i % 4]).then_inc(y_moved, 1)

            @block.scalar
            def _(act):
                def exp(u):
                    n, _ = span(units[u][0])
                    act.wait_ge(maxed, u + 1)
                    if u >= 2:
                        act.wait_ge(turned, u - 1)
                        act.wait_ge(taken, u - 1)
                    act.activation(pr[:, u % 2, 0:n], lg[:, u % 2, 0:n], ACT.Exp, bias=mx[:, u % 2, 0:1],
                                   accum_out=mx[:, u % 2, 1:2]).then_inc(exped, 1)

                exp(0)
                for u, (i, h) in enumerate(units):
                    n, _ = span(i)
                    act.wait_ge(turned, u + 1)
                    if u >= 2:
                        act.wait_ge(attended, u - 1)
                    act.activation(prT[:, u % 2, 0:n], s.psum[:, 2048:2048 + n], ACT.Copy).then_inc(moved, 1)
                    if u + 1 < NU:
                        exp(u + 1)


def attention2(s, yT):
    nc = s.nc
    s.gain_q_set = sem(s, "gain_q_set")
    with ExitStack() as ctx:
        sb = lambda name, shape: ctx.enter_context(nc.sbuf_tensor(name, shape, F32))
        s.gain_q = sb("gain_q", [P, 1])
        qT, kT, v_tok = sb("qT2", [P, 4, T]), sb("kT2", [P, 4, T]), sb("v2_tok", [P, NT, D_A])
        q_tok = s.x[:, 0:NT // 2, :].rearrange("p t (a n) -> p (t a) n", a=2)
        k_tok = s.x[:, NT // 2:NT, :].rearrange("p t (a n) -> p (t a) n", a=2)
        bias = RelativeBias(s, ctx)
        stage_qkv(s, qT, kT, v_tok, q_tok, k_tok, bias)
        stage_attention(s, qT, kT, v_tok, bias.tile, q_tok, yT)


def bank_group(i):
    return 2 * (i % GG) + i // GG


def groups_of(i):
    g = bank_group(4 * i)
    return slice(g, g + 7, 2)


def stage_ssm_tables(s, t):
    nc, A = s.nc, s.A
    V, WT, TM, EC, ES, MG, dskip = t["V"], t["WT"], t["TM"], t["EC"], t["ES"], t["MG"], t["dskip"]
    with ExitStack() as ctx:
        sb = lambda name, shape: ctx.enter_context(nc.sbuf_tensor(name, shape, F32))
        lam = sb("lam", [GG, 3, P])
        step2 = sb("step2", [GG, 2])
        par = sb("par", [P, 16, GG])
        PW = sb("pw", [P, 2, L2 + 1, GG])
        B = sb("ssm_b", [P, 2, GG, SG])
        BB = sb("ssm_bb", [P, 2, GG, SG])
        X = sb("ssm_cx", [P, 4, P])
        CT = sb("ssm_ct", [P, 2, GG, SG])
        K16 = t["R"][0:SG].rearrange("p r g n -> p (r g n)").rearrange("p (g n) -> p g n", n=P)
        tmp = [sb(f"ssm_t{i}", [P, GG * NCH // 2]) for i in range(2)]
        w_tmp = sb("ssm_w_tmp", [P, 2, GG, SG])
        wide = lambda x, n: x.rearrange("p (g o) -> p g o", o=1).to_broadcast([P, GG, n])
        b_ready = sem(s, "s_b_ready")
        ins, b_in, c_in, d_in = (sem(s, f"s_{x}") for x in ("ins", "b_in", "c_in", "d_in"))
        spread, lam_turned, act_in, act_out, c_turned, tm_zero, tm_set = (sem(s, f"s_{x}") for x in ("spread", "lam_turned", "act_in", "act_out", "c_turned", "tm_zero", "tm_set"))
        vk_ready, k_done, k_moved, w_built, w_turned, w_moved = (sem(s, f"s_{x}") for x in ("vk_ready", "k_done", "k_moved", "w_built", "w_turned", "w_moved"))
        WN = t["SP"]
        p = lambda i: par[:, i, :]
        LRE, LIM, STEP, MAG, ANG, SH, CH, AR, AI, FR, FI, T0, T1, T2, M8, NR = range(16)
        with nc.Block() as block:
            @block.sync
            def _(sp):
                sp.dma_start(lam[:, 0, :], A["ssm_lambda_re_2"][0].rearrange("(g two) p -> g (two p)", two=2)).then_inc(ins, 16)
                sp.dma_start(lam[:, 1, :], A["ssm_lambda_im_2"][0].rearrange("(g two) p -> g (two p)", two=2)).then_inc(ins, 16)
                sp.dma_start(step2[:, :], A["ssm_log_step_2"][0].rearrange("(g two) -> g two", two=2)).then_inc(ins, 16)
                for r, n in enumerate(("ssm_b_re_2", "ssm_b_im_2")):
                    sp.dma_start(B[:, r, :, :], A[n][0].rearrange("(g two) p c -> (two p) g c", two=2)).then_inc(b_in, 16)
                for r, n in enumerate(("ssm_c_re_2", "ssm_c_im_2")):
                    src = A[n][0].rearrange("(g two) c p -> g c two p", two=2)
                    for g in range(GG):
                        q = (g % 8) * SG
                        sp.dma_start(X[q:q + SG, 2 * r + g // 8, :].rearrange("c (two p) -> c two p", two=2), src[g]).then_inc(c_in, 16)
                sp.dma_start(dskip[:, :], A["ssm_d_2"].to_broadcast([P, 512])).then_inc(d_in, 16)
                sp.wait_ge(k_moved, 8)
                sp.wait_ge(tm_zero, 1)
                for j in range(L2):
                    sp.dma_start(TM[j * SG:(j + 1) * SG, :, j * SG:P], K16[:, :, 0:P - j * SG]).then_inc(tm_set, 16)
                sp.wait_ge(tm_set, 16 * L2)
                sp.wait_ge(d_in, 16)

            @block.gpsimd
            def _(pool):
                pool.memset(TM[:, :, :], 0.0).then_inc(tm_zero, 1)
                c = s.pool_c
                step = lambda o, a, b, op: c.link(pool, pool.tensor_tensor(o, a, b, op))
                pool.wait_ge(b_ready, 1)
                br, bi, t0, t1 = BB[:, 0], BB[:, 1], w_tmp[:, 0], w_tmp[:, 1]
                for j in range(L2):
                    re, im = (WN[:, r].rearrange("p g (j c) -> p g j c", j=L2)[:, :, j, :] for r in range(2))
                    ar, ai = (wide(PW[:, r, L2 - 1 - j, :], SG) for r in range(2))
                    c.then(pool.tensor_tensor(t0, br, ar, ALU.mult))
                    step(t1, bi, ai, ALU.mult)
                    step(re, t0, t1, ALU.subtract)
                    c.then(pool.tensor_tensor(t0, br, ai, ALU.mult))
                    step(t1, bi, ar, ALU.mult)
                    step(im, t0, t1, ALU.add)
                pool.sem_inc(w_built, 1)

            @block.tensor
            def _(pe):
                pe.wait_ge(spread, 1)
                pe.wait_ge(ins, 48)
                for i in range(3):
                    last = pe.transpose(s.bank[0][:, i * GG:(i + 1) * GG], lam[:, i, :], s.ident[0:GG, 0:GG])
                last.then_inc(lam_turned, 1)
                pe.wait_ge(c_in, 16 * 2 * GG)
                for i in range(4):
                    last = pe.transpose(s.bank[1][:, i * P:(i + 1) * P], X[:, i, :], s.ident[:, :])
                last.then_inc(c_turned, 1)
                pe.wait_ge(vk_ready, 1)
                for i in range(GRP):
                    g = bank_group(i)
                    lanes = slice((g % 2) * SP_, (g % 2) * SP_ + SP_)
                    to = s.bank[i // 4][0:SG, (i % 4) * P:(i % 4 + 1) * P]
                    for r in range(2):
                        last = pe.matmul(to, BB[lanes, r, g // 2, :], V[lanes, r, g // 2, 0:L2, :].rearrange("p d c -> p (d c)"),
                                         start=(r == 0), stop=(r == 1))
                    if i % 4 == 3:
                        last.then_inc(k_done, 1)
                pe.wait_ge(w_built, 1)
                for i in range(8):
                    pe.wait_ge(k_moved, i + 1)
                    for a in range(4):
                        r, g = divmod(i * 4 + a, GG)
                        last = pe.transpose(s.bank[i][:, a * P:(a + 1) * P], WN[:, r, g, :], s.ident[:, :])
                    last.then_inc(w_turned, 1)

            @block.scalar
            def _(act):
                c = s.act_c
                act.wait_ge(act_in, 1)
                c.link(act, act.activation(p(STEP), p(STEP), ACT.Exp))
                act.sem_inc(act_out, 1)
                act.wait_ge(act_in, 2)
                c.link(act, act.activation(p(MAG), p(T0), ACT.Exp))
                c.link(act, act.activation(p(SH), p(T1), ACT.Sin))
                c.link(act, act.activation(p(CH), p(T2), ACT.Sin))
                act.sem_inc(act_out, 1)
                for i in range(8):
                    act.wait_ge(k_done, i + 1)
                    act.activation(K16[:, groups_of(i), :], s.bank[i][0:SG, :].rearrange("p (g n) -> p g n", g=4), ACT.Copy).then_inc(k_moved, 1)
                for i in range(8):
                    act.wait_ge(w_turned, i + 1)
                    act.activation(WT[:, :, :].rearrange("p a n -> p (a n)")[:, i * 512:(i + 1) * 512], s.bank[i], ACT.Copy).then_inc(w_moved, 1)

            @block.vector
            def _(dve):
                c = s.dve_c
                mul = lambda o, a, b: c.link(dve, dve.tensor_tensor(o, a, b, ALU.mult))
                add = lambda o, a, b: c.link(dve, dve.tensor_tensor(o, a, b, ALU.add))
                sub = lambda o, a, b: c.link(dve, dve.tensor_tensor(o, a, b, ALU.subtract))

                def complex_mul(re, im, ar, ai, br, bi, t0, t1, neg_im=False):
                    mul(t0, ar, br)
                    mul(t1, ai, bi)
                    sub(re, t0, t1)
                    mul(t0, ar, bi)
                    mul(t1, ai, br)
                    add(im, t0, t1)
                    if neg_im:
                        c.link(dve, dve.tensor_scalar(im, im, -1.0, None, ALU.mult))

                dve.wait_ge(ins, 48)
                c.link(dve, dve.tensor_copy(lam[:, 2, :].rearrange("g (two p) -> g two p", two=2),
                                            step2[:, :].rearrange("g (two o) -> g two o", o=1).to_broadcast([GG, 2, SP_])))
                dve.sem_inc(spread, 1)
                dve.wait_ge(lam_turned, 1)
                c.link(dve, dve.tensor_copy(par[:, 0:3, :], s.bank[0][:, 0:3 * GG].rearrange("p (i g) -> p i g", i=3)))
                dve.sem_inc(act_in, 1)
                dve.wait_ge(act_out, 1)
                mul(p(T0), p(LRE), p(STEP))
                mul(p(ANG), p(LIM), p(STEP))
                c.link(dve, dve.tensor_scalar(p(NR), p(ANG), 1.0 / (2.0 * math.pi), ROUND, ALU.mult, ALU.add))
                c.link(dve, dve.tensor_scalar(p(NR), p(NR), -ROUND, None, ALU.add))
                for part in TWO_PI:
                    c.link(dve, dve.scalar_tensor_tensor(p(ANG), p(NR), -part, p(ANG), ALU.mult, ALU.add))
                c.link(dve, dve.tensor_scalar(p(T1), p(ANG), 0.5, None, ALU.mult))
                c.link(dve, dve.tensor_scalar(p(T2), p(T1), -1.0, None, ALU.mult))
                c.link(dve, dve.tensor_tensor(p(T2), p(T2), p(T1), ALU.max))
                c.link(dve, dve.tensor_scalar(p(T2), p(T2), -1.0, float(math.pi / 2), ALU.mult, ALU.add))
                dve.sem_inc(act_in, 1)
                dve.wait_ge(act_out, 2)
                mul(p(T0), p(SH), p(SH))
                mul(p(T1), p(SH), p(CH))
                c.link(dve, dve.tensor_scalar(p(CH), p(T0), -2.0, 1.0, ALU.mult, ALU.add))
                c.link(dve, dve.tensor_scalar(p(SH), p(T1), 2.0, None, ALU.mult))
                mul(p(AR), p(MAG), p(CH))
                mul(p(AI), p(MAG), p(SH))
                c.link(dve, dve.tensor_scalar(p(NR), p(AR), -1.0, None, ALU.add))
                mul(p(T0), p(LRE), p(LRE))
                mul(p(T1), p(LIM), p(LIM))
                add(p(T0), p(T0), p(T1))
                c.link(dve, dve.reciprocal(p(T2), p(T0)))
                mul(p(T0), p(NR), p(LRE))
                mul(p(T1), p(AI), p(LIM))
                add(p(T0), p(T0), p(T1))
                mul(p(FR), p(T0), p(T2))
                mul(p(T0), p(AI), p(LRE))
                mul(p(T1), p(NR), p(LIM))
                sub(p(T0), p(T0), p(T1))
                mul(p(FI), p(T0), p(T2))
                c.then(dve.memset(PW[:, 0, 0, :], 1.0))
                c.link(dve, dve.memset(PW[:, 1, 0, :], 0.0))
                for d in range(1, L2 + 1):
                    complex_mul(PW[:, 0, d, :], PW[:, 1, d, :], PW[:, 0, d - 1, :], PW[:, 1, d - 1, :], p(AR), p(AI), p(T0), p(T1))
                mul(p(M8), p(MAG), p(MAG))
                mul(p(M8), p(M8), p(M8))
                mul(p(M8), p(M8), p(M8))
                for _ in range(3):
                    complex_mul(p(T2), p(NR), p(CH), p(SH), p(CH), p(SH), p(T0), p(T1))
                    c.link(dve, dve.tensor_copy(p(CH), p(T2)))
                    c.link(dve, dve.tensor_copy(p(SH), p(NR)))
                dve.wait_ge(b_in, 32)
                small = lambda i, n: tmp[i][:, 0:GG * n].rearrange("p (g c) -> p g c", g=GG)
                complex_mul(BB[:, 0], BB[:, 1], B[:, 0], B[:, 1], wide(p(FR), SG), wide(p(FI), SG), small(0, SG), small(1, SG))
                dve.sem_inc(b_ready, 1)
                dve.wait_ge(c_turned, 1)
                c.link(dve, dve.tensor_copy(CT[:, :, :, :].rearrange("p r g c -> p (r g c)"), s.bank[1]))
                for d in range(L2 + 1):
                    complex_mul(V[:, 0, :, d, :], V[:, 1, :, d, :], CT[:, 0], CT[:, 1], wide(PW[:, 0, d, :], SG), wide(PW[:, 1, d, :], SG),
                                small(0, SG), small(1, SG), neg_im=True)
                dve.sem_inc(vk_ready, 1)
                c.then(dve.memset(EC[:, :, 0:1], 1.0))
                c.link(dve, dve.memset(ES[:, :, 0:1], 0.0))
                n = 1
                while n < NCH:
                    part = lambda i: tmp[i][:, 0:GG * n].rearrange("p (g c) -> p g c", g=GG)
                    complex_mul(EC[:, :, n:2 * n], ES[:, :, n:2 * n], EC[:, :, 0:n], ES[:, :, 0:n], wide(p(CH), n), wide(p(SH), n),
                                part(0), part(1))
                    complex_mul(p(T2), p(NR), p(CH), p(SH), p(CH), p(SH), p(T0), p(T1))
                    c.link(dve, dve.tensor_copy(p(CH), p(T2)))
                    c.link(dve, dve.tensor_copy(p(SH), p(NR)))
                    n *= 2
                c.link(dve, dve.tensor_copy(MG[:, :, :], wide(p(M8), NCH)))
                c.link(dve, dve.memset(MG[:, :, 0:1], 0.0))
                dve.wait_ge(w_moved, 8)


def stage_ssm(s, t, yT):
    nc, A = s.nc, s.A
    V, WT, TM, EC, ES, MG, R, SP, dskip = (t[n] for n in ("V", "WT", "TM", "EC", "ES", "MG", "R", "SP", "dskip"))
    U = s.x[:, 0:4, :].rearrange("p a n -> p (a n)").rearrange("p (g j c) -> p g j c", g=GRP, j=L2)
    UT = s.x[:, 4:8, :].rearrange("p a n -> p (a n)").rearrange("p (g n) -> p g n", g=GRP)
    wu = SP[:, :, :, :].rearrange("p r g n -> p (r g n)").rearrange("p (k n) -> p k n", k=KD)
    Y = WT[:, :, :].rearrange("p a n -> p (a n)").rearrange("p (t c) -> p t c", t=L2)
    zT = R[:, :, :, :].rearrange("p r g n -> p (r g n)").rearrange("p (m t) -> p m t", m=4)
    tmp = WT[:, :, :].rearrange("p a n -> p (a n)")
    rot = t["rot"]
    wglu = MG[:, :, :].rearrange("p g n -> p (g n)").rearrange("p (k n) -> p k n", k=4)
    wu_in, u_done, u_moved, u_turned, ut_moved, du_ready = (sem(s, f"u_{x}") for x in ("wu_in", "u_done", "u_moved", "u_turned", "ut_moved", "du_ready"))
    loc_done, rotated, sp_ready, y_done, y_ready, gelu_ready = (sem(s, f"u_{x}") for x in ("loc_done", "rotated", "sp_ready", "y_done", "y_ready", "gelu_ready"))
    z_turned, z_moved, glu_in, glu_done, glu_sig, scanned, wu_free = (sem(s, f"u_{x}") for x in ("z_turned", "z_moved", "glu_in", "glu_done", "glu_sig", "scanned", "wu_free"))
    with nc.Block() as block:
        @block.sync
        def _(sp):
            src = A["w_in_2"][0].rearrange("(k p) n -> p k n", p=P)
            for k in range(0, KD, 4):
                sp.dma_start(wu[:, k:k + 4, :], src[:, k:k + 4, C2_U:C2_U + 512]).then_inc(wu_in, 16)
            sp.wait_ge(scanned, 2)
            sp.dma_start(wglu, A["w_glu_2"][0].rearrange("(k p) n -> p k n", p=P)).then_inc(glu_in, 16)

        @block.gpsimd
        def _(pool):
            pool.wait_ge(u_turned, 8)
            d = dskip[:, :].rearrange("p (g c) -> p g c", g=GRP)
            for j in range(L2):
                pool.tensor_tensor(U[:, :, j, :], U[:, :, j, :], d, ALU.mult).then_inc(du_ready, 1)

        @block.tensor
        def _(pe):
            pe.wait_ge(wu_in, 32)
            for j in range(L2):
                for k in range(KD):
                    last = pe.matmul(s.bank[j], s.hT[:, k, j:T:L2], wu[:, k, :], start=(k == 0), stop=(k == KD - 1))
                last.then_inc(u_done, 1)
            pe.wait_ge(u_moved, L2)
            for i in range(8):
                for a in range(4):
                    g = 4 * i + a
                    last = pe.transpose(s.bank[i][:, a * P:(a + 1) * P], U[:, g].rearrange("p j c -> p (j c)"), s.ident[:, :])
                last.then_inc(u_turned, 1)
            for i in range(8):
                pe.wait_ge(ut_moved, 8)
                for a in range(2):
                    gg = 2 * i + a
                    for r in range(2):
                        for two in range(2):
                            to = s.bank[i][two * SP_:(two + 1) * SP_, (2 * a + r) * P:(2 * a + r + 1) * P]
                            last = pe.matmul(to, WT[:, r * GG + gg, two * SP_:(two + 1) * SP_], UT[:, 2 * gg + two, :], start=True, stop=True)
                last.then_inc(loc_done, 1)
            pe.wait_ge(sp_ready, 2)
            for i in range(8):
                pe.wait_ge(rotated, 8)
                for a in range(4):
                    g = bank_group(4 * i + a)
                    lanes = slice((g % 2) * SP_, (g % 2) * SP_ + SP_)
                    to = s.bank[i][:, a * P:(a + 1) * P]
                    pe.matmul(to, UT[:, g, :], TM[:, g, :], start=True, stop=False)
                    for r in range(2):
                        last = pe.matmul(to, SP[lanes, r, g // 2, :], V[lanes, r, g // 2, 1:L2 + 1, :].rearrange("p d c -> p (d c)"),
                                         start=False, stop=(r == 1))
                last.then_inc(y_done, 1)
            for j in range(L2):
                pe.wait_ge(gelu_ready, j + 1)
                pe.wait_ge(y_ready, 8)
                for m in range(4):
                    last = pe.transpose(s.bank[j][:, m * P:(m + 1) * P], Y[:, j, m * P:(m + 1) * P], s.ident[:, :])
                last.then_inc(z_turned, 1)
            pe.wait_ge(z_moved, L2)
            pe.wait_ge(glu_in, 16)
            for i in range(8):
                m, n = divmod(i, 2)
                for k in range(4):
                    last = pe.matmul(s.bank[i], wglu[:, k, m * P:(m + 1) * P], zT[:, k, n * 512:(n + 1) * 512], start=(k == 0), stop=(k == 3))
                last.then_inc(glu_done, 1)

        @block.vector
        def _(dve):
            c = s.dve_c
            for j in range(L2):
                dve.wait_ge(u_done, j + 1)
                dve.tensor_copy(U[:, :, j, :], s.bank[j].rearrange("p (g c) -> p g c", g=GRP)).then_inc(u_moved, 1)
            for i in range(8):
                dve.wait_ge(u_turned, i + 1)
                dve.tensor_copy(UT[:, 4 * i:4 * i + 4, :].rearrange("p g n -> p (g n)"), s.bank[i]).then_inc(ut_moved, 1)
            t0, t1 = (rot[:, i * 256:(i + 1) * 256].rearrange("p (a n) -> p a n", a=2) for i in range(2))
            for i in range(8):
                dve.wait_ge(loc_done, i + 1)
                got = s.bank[i].rearrange("p (a r n) -> p a r n", a=2, r=2)
                gs = slice(2 * i, 2 * i + 2)
                c.then(dve.tensor_tensor(t0, got[:, :, 0, :], EC[:, gs, :], ALU.mult))
                c.link(dve, dve.tensor_tensor(t1, got[:, :, 1, :], ES[:, gs, :], ALU.mult))
                c.link(dve, dve.tensor_tensor(R[:, 0, gs, :], t0, t1, ALU.add))
                c.then(dve.tensor_tensor(t0, got[:, :, 1, :], EC[:, gs, :], ALU.mult))
                c.link(dve, dve.tensor_tensor(t1, got[:, :, 0, :], ES[:, gs, :], ALU.mult))
                dve.tensor_tensor(R[:, 1, gs, :], t0, t1, ALU.subtract).then_inc(rotated, 1)
                dve.wait_ge(rotated, i + 1)
            f = lambda x: x.rearrange("p g n -> p (g n)")
            for r in range(2):
                dve.tensor_tensor_scan(f(SP[:, r]), f(MG[:, :, :]), f(R[:, r]), 0.0, ALU.mult, ALU.add).then_inc(scanned, 1)
            dve.wait_ge(scanned, 2)
            n = NCH - 1
            a, b = (tmp[:, i * 2048:(i + 1) * 2048].rearrange("p (g n) -> p g n", g=GG)[:, :, 0:n] for i in range(2))
            c.then(dve.tensor_tensor(a, SP[:, 0, :, 0:n], EC[:, :, 0:n], ALU.mult))
            c.link(dve, dve.tensor_tensor(b, SP[:, 1, :, 0:n], ES[:, :, 0:n], ALU.mult))
            c.link(dve, dve.tensor_tensor(a, a, b, ALU.subtract))
            c.link(dve, dve.tensor_tensor(b, SP[:, 0, :, 0:n], ES[:, :, 0:n], ALU.mult))
            c.link(dve, dve.tensor_tensor(R[:, 0, :, 0:n], SP[:, 1, :, 0:n], EC[:, :, 0:n], ALU.mult))
            c.link(dve, dve.tensor_tensor(SP[:, 1, :, 1:NCH], R[:, 0, :, 0:n], b, ALU.add))
            c.then(dve.memset(SP[:, :, :, 0:1], 0.0))
            c.link(dve, dve.tensor_copy(SP[:, 0, :, 1:NCH], a))
            dve.sem_inc(sp_ready, 2)
            dve.wait_ge(du_ready, L2)
            for i in range(8):
                dve.wait_ge(y_done, i + 1)
                to = Y.rearrange("p t (g c) -> p g t c", g=GRP)[:, groups_of(i)]
                dve.tensor_tensor(to, s.bank[i].rearrange("p (g t c) -> p g t c", g=4, t=L2), U[:, groups_of(i)], ALU.add).then_inc(y_ready, 1)
            for j in range(L2):
                dve.wait_ge(z_turned, j + 1)
                dve.tensor_copy(zT[:, :, j:T:L2], s.bank[j].rearrange("p (m n) -> p m n", m=4)).then_inc(z_moved, 1)
            for i in range(8):
                m, n = divmod(i, 2)
                dve.wait_ge(glu_sig, i + 1)
                cols = slice(n * 512, (n + 1) * 512)
                c.then(dve.tensor_tensor(yT[:, m, cols], yT[:, m, cols], zT[:, m, cols], ALU.mult))

        @block.scalar
        def _(act):
            act.wait_ge(y_ready, 8)
            for j in range(L2):
                act.activation(Y[:, j, :], Y[:, j, :], ACT.Gelu_apprx_tanh).then_inc(gelu_ready, 1)
            for i in range(8):
                m, n = divmod(i, 2)
                act.wait_ge(glu_done, i + 1)
                b = VEC["b_glu_2"] + m
                act.activation(yT[:, m, n * 512:(n + 1) * 512], s.bank[i], ACT.Sigmoid, bias=s.vec[:, b:b + 1]).then_inc(glu_sig, 1)


def ssm2(s):
    nc = s.nc
    yT = s.x[:, 4:8, :]
    with ExitStack() as ctx:
        sb = lambda name, shape: ctx.enter_context(nc.sbuf_tensor(name, shape, F32))
        t = {"V": sb("ssm_V", [P, 2, GG, L2 + 1, SG]), "WT": sb("ssm_WT", [P, 2 * GG, P]), "TM": sb("ssm_TM", [P, GRP, P]),
             "EC": sb("ssm_EC", [P, GG, NCH]), "ES": sb("ssm_ES", [P, GG, NCH]), "MG": sb("ssm_MG", [P, GG, NCH]),
             "dskip": sb("ssm_d", [P, 512])}
        t["SP"] = sb("ssm_SP", [P, 2, GG, NCH])
        t["R"] = s.x[:, 0:4, :].rearrange("p a n -> p (a n)").rearrange("p (r g n) -> p r g n", r=2, g=GG)
        stage_ssm_tables(s, t)
        t["R"] = sb("ssm_R", [P, 2, GG, NCH])
        t["rot"] = sb("ssm_rot", [P, 512])
        stage_ssm(s, t, yT)


def stage_branches(s, yaT, ysT, mT):
    nc, A = s.nc, s.A
    with nc.sbuf_tensor("h_high", [P, KD, T], F32) as h_high, nc.sbuf_tensor("gw_high", [P, 2, KD, 2, P], F32) as w_high, \
            nc.sbuf_tensor("wb_ring", [P, 2, KD, P], F32) as wb, \
            nc.sbuf_tensor("branch_sig", [P, 2, 2, 512], F32) as sig, nc.sbuf_tensor("branch_tmp", [P, 2, 512], F32) as tmp:
        w, w_low = (x[:, 0:4, :].rearrange("p a n -> p (a n)").rearrange("p (q k b c) -> p q k b c", q=2, k=KD, b=2)
                    for x in (s.x, s.x_cut))
        w_ready = [sem(s, f"n_w{i}") for i in range(2)]
        done, sigged, merged = sem(s, "n_done"), sem(s, "n_sigged"), sem(s, "n_merged")
        h_cut, h_low_ready, w_cut, w_low_ready = (sem(s, f"n_{x}") for x in ("h_cut", "h_low_ready", "w_cut", "w_low_ready"))
        w_src = A["w_in_2"][0].rearrange("(k p) n -> p k n", p=P)
        wb_src = A["w_branch_2"][0].rearrange("(k p) n -> p k n", p=P)
        R = lambda ap: ap.bitcast(F32R)
        with nc.Block() as block:
            @block.sync
            def _(sp):
                for m in range(KD):
                    if m >= 2:
                        sp.wait_ge(merged, 2 * (m - 1))
                    c0 = m * P
                    sp.dma_start(wb[:, m % 2], wb_src[:, :, c0:c0 + P]).then_inc(w_ready[m % 2], 16)
                    for b in range(2):
                        sp.dma_start(w[:, m % 2, :, b, :], w_src[:, :, C2_GATE + b * D + c0:C2_GATE + b * D + c0 + P]).then_inc(w_ready[m % 2], 16)

            @block.tensor
            def _(pe):
                for i in range(2 * KD):
                    m, n = divmod(i, 2)
                    if n == 0:
                        pe.wait_ge(w_ready[m % 2], 48 * (m // 2 + 1))
                    if i >= 2:
                        pe.wait_ge(merged, i - 1)
                    cols = slice(n * 512, (n + 1) * 512)
                    for b, y in enumerate((yaT, ysT)):
                        for k in range(4):
                            last = pe.matmul(s.bank[4 * (i % 2) + 2 + b], wb[:, m % 2, 4 * b + k, :], y[:, k, cols],
                                             start=(k == 0), stop=(k == 3))
                        last.then_inc(done, 1)
                    if n == 0:
                        pe.wait_ge(w_low_ready, m + 1)
                    for b in range(2):
                        for k in range(KD):
                            if i == 0 and b == 0:
                                pe.wait_ge(h_low_ready, k + 1)
                            high, low = R(w_high[:, m % 2, k, b, :]), R(w_low[:, m % 2, k, b, :])
                            to = s.bank[4 * (i % 2) + b]
                            pe.matmul(to, high, R(h_high[:, k, cols]), start=(k == 0), stop=False)
                            pe.matmul(to, high, R(s.hT_cut[:, k, cols]), start=False, stop=False)
                            last = pe.matmul(to, low, R(h_high[:, k, cols]), start=False, stop=(k == KD - 1))
                        last.then_inc(done, 1)

            @block.scalar
            def _(act):
                def cut(m):
                    act.wait_ge(w_ready[m % 2], 48 * (m // 2 + 1))
                    if m >= 2:
                        act.wait_ge(merged, 2 * (m - 1))
                    act.activation(R(w_high[:, m % 2]), w[:, m % 2], ACT.Copy).then_inc(w_cut, 1)

                cut(0)
                for k in range(KD):
                    act.activation(R(h_high[:, k, :]), s.hT[:, k, :], ACT.Copy).then_inc(h_cut, 1)
                cut(1)
                for i in range(2 * KD):
                    m, n = divmod(i, 2)
                    if n == 0 and 2 <= m + 1 < KD:
                        cut(m + 1)
                    for b in range(2):
                        act.wait_ge(done, 4 * i + b + 3)
                        if i >= 2:
                            act.wait_ge(merged, i - 1)
                        v = VEC["b_gate_2"] + b * KD + m
                        act.activation(sig[:, i % 2, b, :], s.bank[4 * (i % 2) + b], ACT.Sigmoid, bias=s.vec[:, v:v + 1]).then_inc(sigged, 1)

            @block.vector
            def _(dve):
                c = s.dve_c

                def take_low(m):
                    dve.wait_ge(w_cut, m + 1)
                    dve.tensor_tensor(R(w_low[:, m % 2]), w[:, m % 2], w_high[:, m % 2], ALU.subtract).then_inc(w_low_ready, 1)

                take_low(0)
                for k in range(KD):
                    dve.wait_ge(h_cut, k + 1)
                    dve.tensor_tensor(R(s.hT_cut[:, k, :]), s.hT[:, k, :], h_high[:, k, :], ALU.subtract).then_inc(h_low_ready, 1)
                take_low(1)
                for i in range(2 * KD):
                    m, n = divmod(i, 2)
                    if n == 0 and 2 <= m + 1 < KD:
                        take_low(m + 1)
                    dve.wait_ge(done, 4 * i + 4)
                    dve.wait_ge(sigged, 2 * i + 2)
                    to = mT[:, m, n * 512:(n + 1) * 512]
                    c.then(dve.tensor_tensor(tmp[:, i % 2, :], s.bank[4 * (i % 2) + 2], sig[:, i % 2, 0, :], ALU.mult))
                    c.link(dve, dve.tensor_tensor(to, s.bank[4 * (i % 2) + 3], sig[:, i % 2, 1, :], ALU.mult))
                    dve.tensor_tensor(to, to, tmp[:, i % 2, :], ALU.add).then_inc(merged, 1)


def stage_route2(s, mo, gate, mask):
    nc, A = s.nc, s.A
    NL = NG2 + E2
    with nc.sbuf_tensor("w_r2", [P, KD, NL], F32) as w, nc.sbuf_tensor("b_r2", [P, NL], F32) as b, \
            nc.sbuf_tensor("l2", [P, NT, NL], F32) as lg, nc.sbuf_tensor("pg", [P, NT, 16], F32) as pg, \
            nc.sbuf_tensor("rest2", [P, NT, 16], F32) as rest, nc.sbuf_tensor("top2", [P, NT, 8], F32) as top, \
            nc.sbuf_tensor("find", [P, NT, 8], F32) as find, nc.sbuf_tensor("gm", [P, NT, NG2], F32) as gm, \
            nc.sbuf_tensor("eg", [P, NT, NG2], F32) as eg, nc.sbuf_tensor("el", [P, NT, E2], F32) as el, \
            nc.sbuf_tensor("sums2", [P, 3, NT], F32) as sums, nc.sbuf_tensor("off", [P, NT, NG2], F32) as off:
        w_in, logits_done, to_exp, exped = (sem(s, f"q_{x}") for x in ("w_in", "logits_done", "to_exp", "exped"))
        one = lambda x, n: x.rearrange("p (t o) -> p t o", o=1).to_broadcast([P, NT, n])
        with nc.Block() as block:
            @block.sync
            def _(sp):
                sp.dma_start(w[:, :, 0:NG2], A["w_group_router_2"][0].rearrange("(k p) e -> p k e", p=P)).then_inc(w_in, 16)
                sp.dma_start(w[:, :, NG2:NL], A["w_expert_router_2"][0].rearrange("(k p) e -> p k e", p=P)).then_inc(w_in, 16)
                sp.dma_start(b[:, 0:NG2], A["group_bias_2"].to_broadcast([P, NG2])).then_inc(w_in, 16)
                sp.dma_start(b[:, NG2:NL], A["expert_bias_2"].to_broadcast([P, E2])).then_inc(w_in, 16)

            @block.tensor
            def _(pe):
                pe.wait_ge(w_in, 64)
                for t in range(NT):
                    for k in range(KD):
                        last = pe.matmul(s.bank[0][:, t * NL:(t + 1) * NL], s.hT[:, k, t * P:(t + 1) * P], w[:, k, :],
                                         start=(k == 0), stop=(k == KD - 1))
                last.then_inc(logits_done, 1)

            @block.scalar
            def _(act):
                act.wait_ge(to_exp, 1)
                act.activation(eg[:, :, :], eg[:, :, :], ACT.Exp).then_inc(exped, 1)
                act.wait_ge(to_exp, 2)
                act.activation(gate[:, :, :], gate[:, :, :], ACT.Exp).then_inc(exped, 1)

            @block.vector
            def _(dve):
                c = s.dve_c
                L = lambda ins: c.link(dve, ins)
                dve.wait_ge(w_in, 64)
                dve.wait_ge(logits_done, 1)
                L(dve.tensor_tensor(lg[:, :, :], s.bank[0][:, 0:NT * NL].rearrange("p (t e) -> p t e", t=NT),
                                    b[:, :].rearrange("p (o e) -> p o e", o=1).to_broadcast([P, NT, NL]), ALU.add))
                L(dve.memset(pg[:, :, :], -BIG))
                L(dve.memset(find[:, :, :], -BIG))
                L(dve.tensor_copy(pg[:, :, 0:NG2], lg[:, :, 0:NG2]))
                for t in range(NT):
                    L(dve.max(top[:, t, :], pg[:, t, :]))
                L(dve.tensor_copy(find[:, :, 0:1], top[:, :, 0:1]))
                for t in range(NT):
                    L(dve.match_replace(out=rest[:, t, :], in_to_replace=find[:, t, :], in_values=pg[:, t, :], imm_value=BIG))
                L(dve.tensor_tensor(gm[:, :, :], rest[:, :, 0:NG2], pg[:, :, 0:NG2], ALU.not_equal))
                L(dve.tensor_tensor(eg[:, :, :], lg[:, :, 0:NG2], top[:, :, 0:1].to_broadcast([P, NT, NG2]), ALU.subtract))
                dve.sem_inc(to_exp, 1)
                L(dve.tensor_scalar(off[:, :, :], gm[:, :, :], -1.0, BIG, ALU.add, ALU.mult))
                spread = lambda x: x[:, :, :].rearrange("p t (g o) -> p t g o", o=1).to_broadcast([P, NT, NG2, EPG])
                grouped = el[:, :, :].rearrange("p t (g e) -> p t g e", g=NG2)
                L(dve.tensor_tensor(grouped, lg[:, :, NG2:NL].rearrange("p t (g e) -> p t g e", g=NG2), spread(gm), ALU.mult))
                L(dve.tensor_tensor(grouped, grouped, spread(off), ALU.add))
                for t in range(NT):
                    L(dve.max(top[:, t, :], el[:, t, :]))
                L(dve.tensor_copy(find[:, :, 0:TOP2], top[:, :, 0:TOP2]))
                for t in range(NT):
                    L(dve.match_replace(out=rest[:, t, :], in_to_replace=find[:, t, :], in_values=el[:, t, :], imm_value=BIG))
                L(dve.tensor_tensor(mask[:, :, :], rest[:, :, :], el[:, :, :], ALU.not_equal))
                L(dve.tensor_tensor(mask[:, :, :].rearrange("p t (g e) -> p (t g) e", g=NG2), mask[:, :, :].rearrange("p t (g e) -> p (t g) e", g=NG2),
                                    gm[:, :, :].rearrange("p t (g o) -> p (t g) o", o=1).to_broadcast([P, NT * NG2, EPG]), ALU.mult))
                L(dve.tensor_tensor(gate[:, :, :], el[:, :, :], top[:, :, 0:1].to_broadcast([P, NT, E2]), ALU.subtract))
                dve.sem_inc(to_exp, 1)
                dve.wait_ge(exped, 2)
                L(dve.tensor_tensor(gate[:, :, :], gate[:, :, :], mask[:, :, :], ALU.mult))
                L(dve.tensor_reduce(sums[:, 0, :], gate[:, :, :], AX_X, ALU.add))
                L(dve.tensor_reduce(sums[:, 1, :], eg[:, :, :], AX_X, ALU.add))
                L(dve.tensor_tensor(sums[:, 2, :], sums[:, 0, :], sums[:, 1, :], ALU.mult))
                L(dve.reciprocal(sums[:, 0, :], sums[:, 2, :]))
                L(dve.tensor_tensor(gate[:, :, :], gate[:, :, :], one(sums[:, 0, :], E2), ALU.mult))


def ffn2(s):
    nc, A = s.nc, s.A
    mo = Moe(s, "moe2", E2, TOP2, F2)
    v = VEC["ffn_norm_gain_2"]
    gain = lambda k: s.vec[:, v + k:v + k + 1]
    stage_norm(s, "norm_g", s.x, NT, s.hT, gain, None, rows_to=mo.rows, sums=s.x_sums, keep=mo.acc)
    out_stored = sem(s, "out_stored")
    with ExitStack() as tables:
        tab = lambda name, shape, dt: tables.enter_context(nc.sbuf_tensor(name, shape, dt))
        start = tab("start2", [P, mo.E + 1], I32)
        idx_g, idx_s = tab("idx_g2", [P, mo.NB + 2], I32), tab("idx_s2", [P, mo.NB], I32)
        row_w = tab("row_w2", [P, mo.NB], F32)
        mo.hold_weights(s, tables, A["w_e_gate_2"][0], A["w_e_up_2"][0], A["w_e_down_2"][0])
        with nc.sbuf_tensor("gate2", [P, NT, mo.E], F32) as gate, nc.sbuf_tensor("mask2", [P, NT, mo.E], F32) as mask:
            stage_route2(s, mo, gate, mask)
            stage_dispatch(s, mo, gate, mask, start, idx_g, idx_s, row_w)
        stage_experts(s, mo, start, idx_g, idx_s, row_w, gain, None)
    with nc.Block() as block:
        @block.sync
        def _(sp):
            sp.dma_start(s.out[0], mo.acc[0:T, :]).then_inc(out_stored, 16)
            sp.wait_ge(out_stored, 16)


def block2(s):
    nc, A = s.nc, s.A
    x_kept = nc.dram_tensor("x2_kept", (T, D), F32, kind="Internal").ap()
    v = VEC["mix_norm_gain_2"]
    stage_norm(s, "norm_2", s.x, NT, s.hT, lambda k: s.vec[:, v + k:v + k + 1], None, sums=s.x_sums, keep=x_kept)
    with nc.sbuf_tensor("yaT", [P, 4, T], F32) as yaT:
        attention2(s, yaT)
        ssm2(s)
        ysT = s.x[:, 4:8, :]
        with nc.sbuf_tensor("mT_cut", [P, KD, T], F32) as mT_cut:
            pass
        with nc.sbuf_tensor("mT", [P, KD, T], F32) as mT:
            stage_branches(s, yaT, ysT, mT)
            stage_out(s, "out_2", mT, mT_cut, A["w_out_2"][0], None, x_src=x_kept, src_high=s.hT_cut)
    return_sems(s)
    ffn2(s)


def program(nc, A, out):
    s = setup(nc, A, out)
    stage_condition(s)
    mixer_inputs(s)
    stage_gates(s)
    stage_mlstm(s)
    stage_mix(s)
    s.mixer.close()
    stage_out(s, "out_1", s.hT, s.hT_cut, A["w_out"][0], 0, A["x"][0], A["b_out"][0:1, :])
    return_sems(s)
    ffn1(s)
    return_sems(s)
    block2(s)


def kernel(**inputs):
    import numpy as _np
    import concourse.bacc as _bacc
    from concourse import mybir as _mybir
    from concourse.bass_utils import run_bass_kernel_spmd as _run

    nc = _bacc.Bacc("TRN2", target_bir_lowering=False, num_devices=1)
    arrays, args = {}, {}
    for name, value in inputs.items():
        a = _np.ascontiguousarray(value)
        arrays[f"in_{name}"] = a
        args[name] = nc.dram_tensor(f"in_{name}", a.shape, _mybir.dt.from_np(a.dtype), kind="ExternalInput").ap()
    out = nc.dram_tensor("out_0_dram", (1, T, D), F32, kind="ExternalOutput").ap()
    program(nc, args, out)
    r = _run(nc, [arrays], core_ids=[0])
    return r.results[0]["out_0_dram"]
```
